# Optimizing a Trainium2 kernel written in Bass

```python
import jax, jax.numpy as jnp
from jax import lax
import numpy as np

D_MODEL = 1024
BATCH = 1
SEQ = 2048
DEPTH = 1
DEC_BATCH = 8
DEC_SEQ = 4
PAST_LEN = 4096
PAGE_SIZE = 128

A_GROUPS = ((128, 1), (512, 4), (2048, 16))
A_N_GROUPS = 3
A_HEADS = 8
A_HEAD_DIM = 64
A_QKV = A_N_GROUPS * A_HEADS * A_HEAD_DIM
A_WIDTH = A_HEADS * A_HEAD_DIM
A_BLOCK = 128
A_SCALE = A_HEAD_DIM ** -0.5
ALIBI_MAX = 8.0
B_HEADS = 8
B_NOPE = 64
B_ROPE = 32
B_VDIM = 64
Q_LORA = 256
KV_LORA = 128
B_WIDTH = B_HEADS * B_VDIM
MLA_SCALE = (B_NOPE + B_ROPE) ** -0.5
ROPE_THETA = 10000.0
Q_BLOCK = 128
NORM_EPS = 1e-6
IN_SIZES = (A_QKV, A_QKV, A_QKV, A_WIDTH, Q_LORA, KV_LORA, B_ROPE, B_WIDTH, D_MODEL, D_MODEL)
IN_DIM = 3 * A_QKV + A_WIDTH + Q_LORA + KV_LORA + B_ROPE + B_WIDTH + 2 * D_MODEL

kernel_name = 'dilated_mla_gated_hybrid_step'

def rms_norm(x, g):
    xf = x.astype(jnp.float32)
    y = xf * lax.rsqrt(jnp.mean(xf * xf, axis=-1, keepdims=True) + NORM_EPS)
    return (y * g.astype(jnp.float32)).astype(x.dtype)

def _split_in(h):
    offs = np.cumsum(IN_SIZES)[:-1].tolist()
    return jnp.split(h, offs, axis=-1)

def _alibi_slopes():
    n = A_N_GROUPS * A_HEADS
    m = jnp.exp2(-ALIBI_MAX * jnp.arange(1, n + 1, dtype=jnp.float32) / n)
    return m.reshape(A_N_GROUPS, A_HEADS)

def _rope_cos_sin(pos):
    inv = ROPE_THETA ** (-jnp.arange(0, B_ROPE, 2, dtype=jnp.float32) / B_ROPE)
    ang = pos.astype(jnp.float32)[:, None] * inv[None, :]
    ang = jnp.concatenate([ang, ang], axis=-1)
    return jnp.cos(ang), jnp.sin(ang)

def _apply_rope(x, cos, sin):
    xf = x.astype(jnp.float32)
    x1, x2 = xf[..., :B_ROPE // 2], xf[..., B_ROPE // 2:]
    rot = jnp.concatenate([-x2, x1], axis=-1)
    return (xf * cos + rot * sin).astype(x.dtype)

def _dilated_prompt(q, k, v, window, dil, slopes):
    B, S, H, D = q.shape
    L = S // dil
    nk = window // dil
    nb = -(-L // A_BLOCK)
    Lp = nb * A_BLOCK

    def to_blocks(t):
        t = t.reshape(B, L, dil, H, D).transpose(0, 2, 1, 3, 4).reshape(B * dil, L, H, D)
        t = jnp.pad(t, ((0, 0), (0, Lp - L), (0, 0), (0, 0)))
        return t.reshape(B * dil, nb, A_BLOCK, H, D)

    def with_prev(t):
        prev = jnp.pad(t[:, :-1], ((0, 0), (1, 0), (0, 0), (0, 0), (0, 0)))
        return jnp.concatenate([prev, t], axis=2)

    qb = to_blocks(q)
    kk, vv = with_prev(to_blocks(k)), with_prev(to_blocks(v))
    a = jnp.arange(A_BLOCK)[:, None]
    c = jnp.arange(2 * A_BLOCK)[None, :]
    delta = a + A_BLOCK - c
    first = jnp.arange(nb)[:, None, None] == 0
    valid = (delta >= 0) & (delta <= nk) & ~(first & (c < A_BLOCK))
    bias = -slopes[:, None, None] * (dil * delta).astype(jnp.float32)
    s = jnp.einsum('nbqhd,nbkhd->nbhqk', qb, kk).astype(jnp.float32) * A_SCALE + bias
    s = jnp.where(valid[None, :, None], s, -jnp.inf)
    lse = jax.nn.logsumexp(s, axis=-1)
    p = jnp.exp(s - lse[..., None]).astype(v.dtype)
    o = jnp.einsum('nbhqk,nbkhd->nbqhd', p, vv)
    o = o.reshape(B, dil, Lp, H, D)[:, :, :L].transpose(0, 2, 1, 3, 4).reshape(B, S, H, D)
    lse = lse.transpose(0, 1, 3, 2).reshape(B, dil, Lp, H)[:, :, :L].transpose(0, 2, 1, 3).reshape(B, S, H)
    return o, lse

def _dilated_sample(q, k_all, v_all, n_buf, window, dil, slopes):
    T = q.shape[1]
    steps = jnp.arange(window // dil + 1)
    idx = n_buf + jnp.arange(T)[:, None] - dil * steps[None, :]
    valid = idx >= 0
    idx_c = jnp.maximum(idx, 0)
    kg, vg = k_all[:, idx_c], v_all[:, idx_c]
    bias = -slopes[:, None] * (dil * steps).astype(jnp.float32)[None, :]
    s = jnp.einsum('bthd,btjhd->bhtj', q, kg).astype(jnp.float32) * A_SCALE + bias[:, None, :]
    s = jnp.where(valid, s, -jnp.inf)
    lse = jax.nn.logsumexp(s, axis=-1)
    p = jnp.exp(s - lse[..., None]).astype(vg.dtype)
    o = jnp.einsum('bhtj,btjhd->bthd', p, vg)
    return o, jnp.moveaxis(lse, 1, 2)

def _combine_groups(outs, lses):
    o = jnp.stack(outs)
    w = jax.nn.softmax(jnp.stack(lses), axis=0).astype(o.dtype)
    y = jnp.einsum('gbsh,gbshd->bshd', w, o)
    return y.reshape(y.shape[0], y.shape[1], A_WIDTH)

def _mla_project(cq, ckv_raw, kpe_raw, pos, w_uq, g_q, g_kv):
    B, S, _ = cq.shape
    q = (rms_norm(cq, g_q) @ w_uq).reshape(B, S, B_HEADS, B_NOPE + B_ROPE)
    cos, sin = _rope_cos_sin(pos)
    q_nope = q[..., :B_NOPE]
    q_pe = _apply_rope(q[..., B_NOPE:], cos[:, None, :], sin[:, None, :])
    c_kv = rms_norm(ckv_raw, g_kv)
    k_pe = _apply_rope(kpe_raw, cos, sin)
    return q_nope, q_pe, c_kv, k_pe

def _mla_prompt(q_nope, q_pe, c_kv, k_pe, w_uk, w_uv):
    B, S, H, _ = q_nope.shape
    k_nope = jnp.einsum('bsc,chd->bshd', c_kv, w_uk)
    v = jnp.einsum('bsc,chd->bshd', c_kv, w_uv)
    nqb = S // Q_BLOCK
    kpos = jnp.arange(S)

    def blocks(t):
        return jnp.moveaxis(t.reshape(B, nqb, Q_BLOCK, t.shape[2], t.shape[3]), 1, 0)

    def one(args):
        qn, qp, i = args
        s = (jnp.einsum('bqhd,bkhd->bhqk', qn, k_nope)
             + jnp.einsum('bqhr,bkr->bhqk', qp, k_pe)).astype(jnp.float32) * MLA_SCALE
        qpos = i * Q_BLOCK + jnp.arange(Q_BLOCK)
        s = jnp.where(kpos[None, :] <= qpos[:, None], s, -jnp.inf)
        p = jax.nn.softmax(s, axis=-1).astype(v.dtype)
        return jnp.einsum('bhqk,bkhd->bqhd', p, v)

    o = lax.map(one, (blocks(q_nope), blocks(q_pe), jnp.arange(nqb)))
    return jnp.moveaxis(o, 0, 1).reshape(B, S, H * B_VDIM)

def _mla_sample(q_nope, q_pe, c_kv, k_pe, ckv_past, kpe_past, w_uk, w_uv):
    Bd, T, H, _ = q_nope.shape
    P = ckv_past.shape[1]
    q_lat = jnp.einsum('bthd,chd->bthc', q_nope, w_uk)
    s_past = (jnp.einsum('bthc,bkc->bhtk', q_lat, ckv_past)
              + jnp.einsum('bthr,bkr->bhtk', q_pe, kpe_past)).astype(jnp.float32)
    s_new = (jnp.einsum('bthc,bkc->bhtk', q_lat, c_kv)
             + jnp.einsum('bthr,bkr->bhtk', q_pe, k_pe)).astype(jnp.float32)
    s_new = jnp.where(jnp.tril(jnp.ones((T, T), dtype=bool)), s_new, -jnp.inf)
    s = jnp.concatenate([s_past, s_new], axis=-1) * MLA_SCALE
    p = jax.nn.softmax(s, axis=-1).astype(c_kv.dtype)
    o_lat = (jnp.einsum('bhtk,bkc->bthc', p[..., :P], ckv_past)
             + jnp.einsum('bhtk,bkc->bthc', p[..., P:], c_kv))
    o = jnp.einsum('bthc,chd->bthd', o_lat, w_uv)
    return o.reshape(Bd, T, H * B_VDIM)

def _merge(x, oa, za, ob, zb, ma, mb, w_proj_a, w_proj_b, w_out, g_post):
    pa = (oa * jax.nn.silu(za)) @ w_proj_a
    pb = (ob * jax.nn.silu(zb)) @ w_proj_b
    m = jax.nn.sigmoid(ma) * pa + jax.nn.sigmoid(mb) * pb
    return x + rms_norm(m @ w_out, g_post)

def _layer_prompt(x, params, slopes):
    (w_in, w_uq, w_uk, w_uv, w_proj_a, w_proj_b, w_out, g_pre, g_post, g_q, g_kv) = params
    B, S, _ = x.shape
    qa, ka, va, za, cq, ckv_raw, kpe_raw, zb, ma, mb = _split_in(rms_norm(x, g_pre) @ w_in)
    shp = (B, S, A_N_GROUPS, A_HEADS, A_HEAD_DIM)
    qa, ka, va = qa.reshape(shp), ka.reshape(shp), va.reshape(shp)
    outs, lses, win_new = [], [], []
    for g, (window, dil) in enumerate(A_GROUPS):
        o, lse = _dilated_prompt(qa[:, :, g], ka[:, :, g], va[:, :, g], window, dil, slopes[g])
        outs.append(o)
        lses.append(lse)
        kv = jnp.stack([ka[:, :, g], va[:, :, g]], axis=2)
        win_new.append(kv[:, S - min(window, S):])
    oa = _combine_groups(outs, lses)
    q_nope, q_pe, c_kv, k_pe = _mla_project(cq, ckv_raw, kpe_raw, jnp.arange(S), w_uq, g_q, g_kv)
    ob = _mla_prompt(q_nope, q_pe, c_kv, k_pe, w_uk, w_uv)
    y = _merge(x, oa, za, ob, zb, ma, mb, w_proj_a, w_proj_b, w_out, g_post)
    return y, c_kv, k_pe, win_new

def _layer_sample(x, cache_ckv, cache_kpe, win_states, page_table, params, slopes):
    (w_in, w_uq, w_uk, w_uv, w_proj_a, w_proj_b, w_out, g_pre, g_post, g_q, g_kv) = params
    Bd, T, _ = x.shape
    qa, ka, va, za, cq, ckv_raw, kpe_raw, zb, ma, mb = _split_in(rms_norm(x, g_pre) @ w_in)
    shp = (Bd, T, A_N_GROUPS, A_HEADS, A_HEAD_DIM)
    qa, ka, va = qa.reshape(shp), ka.reshape(shp), va.reshape(shp)
    outs, lses, win_new = [], [], []
    for g, (window, dil) in enumerate(A_GROUPS):
        buf = win_states[g]
        n_buf = buf.shape[1]
        kv_all = jnp.concatenate([buf, jnp.stack([ka[:, :, g], va[:, :, g]], axis=2)], axis=1)
        o, lse = _dilated_sample(qa[:, :, g], kv_all[:, :, 0], kv_all[:, :, 1], n_buf, window, dil, slopes[g])
        outs.append(o)
        lses.append(lse)
        win_new.append(kv_all[:, T:])
    oa = _combine_groups(outs, lses)
    pos = PAST_LEN + jnp.arange(T)
    q_nope, q_pe, c_kv, k_pe = _mla_project(cq, ckv_raw, kpe_raw, pos, w_uq, g_q, g_kv)
    ckv_past = cache_ckv[page_table].reshape(Bd, -1, KV_LORA)
    kpe_past = cache_kpe[page_table].reshape(Bd, -1, B_ROPE)
    ob = _mla_sample(q_nope, q_pe, c_kv, k_pe, ckv_past, kpe_past, w_uk, w_uv)
    y = _merge(x, oa, za, ob, zb, ma, mb, w_proj_a, w_proj_b, w_out, g_post)
    return y, c_kv, k_pe, win_new

def setup_inputs(seed: int = 0) -> dict:
    key = jax.random.key(seed)
    ks = jax.random.split(key, 24)
    n_pages = PAST_LEN // PAGE_SIZE
    n_used = DEC_BATCH * n_pages
    n_pool = (n_used * 5 + 3) // 4

    def nrm(k, shape, scale=1.0):
        return scale * jax.random.normal(k, shape, jnp.float32)

    def win(k, w):
        return nrm(k, (DEPTH, DEC_BATCH, min(w, PAST_LEN), 2, A_HEADS, A_HEAD_DIM))

    page_table = jax.random.permutation(ks[0], n_pool)[:n_used].reshape(DEC_BATCH, n_pages).astype(jnp.int32)
    return {
        'x_prompt': nrm(ks[1], (BATCH, SEQ, D_MODEL)),
        'x_sample': nrm(ks[2], (DEC_BATCH, DEC_SEQ, D_MODEL)),
        'cache_ckv': nrm(ks[3], (DEPTH, n_pool, PAGE_SIZE, KV_LORA)),
        'cache_kpe': nrm(ks[4], (DEPTH, n_pool, PAGE_SIZE, B_ROPE)),
        'state_win0': win(ks[5], A_GROUPS[0][0]),
        'state_win1': win(ks[6], A_GROUPS[1][0]),
        'state_win2': win(ks[7], A_GROUPS[2][0]),
        'page_table': page_table,
        'w_in': nrm(ks[8], (DEPTH, D_MODEL, IN_DIM), D_MODEL ** -0.5),
        'w_uq': nrm(ks[9], (DEPTH, Q_LORA, B_HEADS * (B_NOPE + B_ROPE)), Q_LORA ** -0.5),
        'w_uk': nrm(ks[10], (DEPTH, KV_LORA, B_HEADS, B_NOPE), KV_LORA ** -0.5),
        'w_uv': nrm(ks[11], (DEPTH, KV_LORA, B_HEADS, B_VDIM), KV_LORA ** -0.5),
        'w_proj_a': nrm(ks[12], (DEPTH, A_WIDTH, D_MODEL), A_WIDTH ** -0.5),
        'w_proj_b': nrm(ks[13], (DEPTH, B_WIDTH, D_MODEL), B_WIDTH ** -0.5),
        'w_out': nrm(ks[14], (DEPTH, D_MODEL, D_MODEL), D_MODEL ** -0.5),
        'g_pre': 1.0 + nrm(ks[15], (DEPTH, D_MODEL), 0.02),
        'g_post': 1.0 + nrm(ks[16], (DEPTH, D_MODEL), 0.02),
        'g_q': 1.0 + nrm(ks[17], (DEPTH, Q_LORA), 0.02),
        'g_kv': 1.0 + nrm(ks[18], (DEPTH, KV_LORA), 0.02),
    }

def reference(x_prompt, x_sample, cache_ckv, cache_kpe, state_win0, state_win1, state_win2, page_table,
              w_in, w_uq, w_uk, w_uv, w_proj_a, w_proj_b, w_out, g_pre, g_post, g_q, g_kv):
    slopes = _alibi_slopes()
    hp, hs = x_prompt, x_sample
    ckv_p, kpe_p, ckv_s, kpe_s = [], [], [], []
    win_p = [[] for _ in range(A_N_GROUPS)]
    win_s = [[] for _ in range(A_N_GROUPS)]
    for l in range(DEPTH):
        params = (w_in[l], w_uq[l], w_uk[l], w_uv[l], w_proj_a[l], w_proj_b[l], w_out[l],
                  g_pre[l], g_post[l], g_q[l], g_kv[l])
        hp, c1, k1, wp = _layer_prompt(hp, params, slopes)
        hs, c2, k2, ws = _layer_sample(hs, cache_ckv[l], cache_kpe[l],
                                       (state_win0[l], state_win1[l], state_win2[l]),
                                       page_table, params, slopes)
        ckv_p.append(c1)
        kpe_p.append(k1)
        ckv_s.append(c2)
        kpe_s.append(k2)
        for g in range(A_N_GROUPS):
            win_p[g].append(wp[g])
            win_s[g].append(ws[g])
    return (hp, hs,
            jnp.stack(ckv_p), jnp.stack(kpe_p),
            jnp.stack(win_p[0]), jnp.stack(win_p[1]), jnp.stack(win_p[2]),
            jnp.stack(ckv_s), jnp.stack(kpe_s),
            jnp.stack(win_s[0]), jnp.stack(win_s[1]), jnp.stack(win_s[2]))


_drawn_inputs = setup_inputs


def setup_inputs(seed=0):
    import zlib

    import numpy as np

    out = dict(_drawn_inputs(seed))
    spreads = {}
    factors = {'g_post': 4.027, 'g_q': 8.0, 'g_kv': 2.873}
    for name, (base, spread) in spreads.items():
        noise = np.random.default_rng([zlib.crc32(name.encode()), seed]).standard_normal(out[name].shape)
        drawn = base * np.exp(spread * noise) if base else spread * noise
        out[name] = __import__('jax').numpy.asarray(drawn.astype(out[name].dtype))
    for name, factor in factors.items():
        out[name] = (out[name] * factor).astype(out[name].dtype)
    return out
```

```python
from contextlib import ExitStack

import concourse.bass as bass
from concourse import mybir

F32 = mybir.dt.float32
F32R = mybir.dt.float32r
I32 = mybir.dt.int32
ALU = mybir.AluOpType
ACT = mybir.ActivationFunctionType
AX = mybir.AxisListType
ds = bass.ds

P = 128
D = 1024
KC = D // P
SEQ = 2048
NT = SEQ // P
DB, DT = 8, 4
NS = DB * DT
TOK = SEQ + NS
PAST = 4096
NPG = PAST // P
GROUPS = ((128, 1), (512, 4), (2048, 16))
NG = 3
H = 8
HD = 64
AW = H * HD
QKV = NG * AW
QL, KL, ROPE = 256, 128, 32
NOPE = 64
LAT = QL + KL + ROPE
C_ZA = 3 * QKV
C_CQ = C_ZA + AW
C_ZB = C_CQ + LAT
C_MA = C_ZB + AW
IN_DIM = C_MA + 2 * D
A_SCALE = HD ** -0.5
B_SCALE = (NOPE + ROPE) ** -0.5
EPS = 1e-6
NEG = -1.0e30
LOWEST = -3.0e38
REC = 2 * HD + 4
RECB = HD + 2
VW = 2 * HD + 4
VB = HD + 2


class Mem:

    spent = []

    def __init__(self, nc, ctx, stage):
        self.nc, self.ctx, self.stage = nc, ctx, stage

    def sb(self, name, shape, dt=F32):
        return self.ctx.enter_context(self.nc.sbuf_tensor(f"{self.stage}_{name}", shape, dt))

    def ps(self, name, shape):
        return self.ctx.enter_context(self.nc.psum_tensor(f"{self.stage}_{name}", shape, F32))

    def sem(self, name):
        sem = self.ctx.enter_context(self.nc.semaphore(f"{self.stage}_{name}"))
        Mem.spent.append(sem)
        return sem


def clear_semaphores(nc):
    with nc.Block() as block:
        @block.sync
        def _(sp):
            for sem in Mem.spent:
                sp.sem_clear(sem)
    Mem.spent.clear()


def split_matmul(pe, out, w, x, first, last):
    pe.matmul(out, w[0], x[0], start=first, stop=False)
    pe.matmul(out, w[0], x[1], start=False, stop=False)
    return pe.matmul(out, w[1], x[0], start=False, stop=last)


def waits(eng, sem, count):
    if not isinstance(count, int) or count > 0:
        eng.wait_ge(sem, count)


def held(eng, sem, count, ticks):
    waits(eng, sem, count)
    if not isinstance(count, int):
        eng.sem_inc(ticks, 1)


def peeled(eng, count, step, body):
    body(0)
    with eng.Fori(1, count) as i:
        body(i * step)


def stage_norm(nc, t, xT, xs, ident):
    with ExitStack() as ctx:
        m = Mem(nc, ctx, "norm")
        xin = [m.sb(f"xin{b}", [P, D]) for b in range(2)]
        xn = [m.sb(f"xn{b}", [P, D]) for b in range(2)]
        junk = m.sb("junk", [P, D])
        g = m.sb("g_rows", [P, D])
        eps = m.sb("eps", [P, 1])
        stat = [m.sb(f"stat{b}", [P, 4]) for b in range(2)]
        tp = [m.ps(f"tp{b}", [P, KC, P]) for b in range(2)]
        consts = m.sem("consts")
        x_in = [m.sem(f"x_in{b}") for b in range(2)]
        eps_set, squared, rooted, inverted = (m.sem(n) for n in ("eps_set", "squared", "rooted", "inverted"))
        xn_ready, tp_ready, hi_ready, lo_ready = (m.sem(n) for n in ("xn_ready", "tp_ready", "hi_ready", "lo_ready"))

        with nc.Block() as block:
            @block.sync
            def _(sp):
                sp.dma_start(ident[:, :], t["ident"]).then_inc(consts, 16)
                sp.dma_start(g[:, :], t["g_pre"].partition_broadcast(P)).then_inc(consts, 16)

                def load(i):
                    for b in range(2):
                        waits(sp, xn_ready, i + b - 1)
                        sp.dma_start(xin[b][:, :], t["x_prompt"][ds((i + b) * P, P), :]).then_inc(x_in[b], 16)

                peeled(sp, NT // 2, 2, load)
                sp.wait_ge(xn_ready, NT - 1)
                sp.dma_start(xin[0][0:NS, :], t["x_sample"]).then_inc(x_in[0], 16)

            @block.scalar
            def _(act):
                act.wait_ge(eps_set, 1)

                def square(n, b, loads, rows):
                    act.wait_ge(x_in[b], loads)
                    waits(act, inverted, n - 1)
                    act.activation(junk[0:rows, :], xin[b][0:rows, :], ACT.Square,
                                   accum_out=stat[b][0:rows, 0:1]).then_inc(squared, 1)
                    act.wait_ge(squared, n + 1)
                    act.activation(stat[b][0:rows, 1:2], stat[b][0:rows, 0:1], ACT.Sqrt, bias=eps[0:rows, :],
                                   scale=1.0 / D).then_inc(rooted, 1)

                def high(n, b, out, rows):
                    act.wait_ge(tp_ready, n + 1)
                    act.activation(out, tp[b][:, :, 0:rows], ACT.Copy).then_inc(hi_ready, 1)

                def pair(i):
                    for b in range(2):
                        square(i + b, b, i * 8 + 16, P)
                    for b in range(2):
                        high(i + b, b, xT[0][:, :, ds((i + b) * P, P)], P)

                peeled(act, NT // 2, 2, pair)
                square(NT, 0, NT * 8 + 16, NS)
                high(NT, 0, xs[0][:, :, :], NS)

            @block.vector
            def _(dve):
                dve.memset(eps[:, :], EPS).then_inc(eps_set, 1)
                dve.wait_ge(consts, 32)

                def norm(n, b, rows):
                    dve.wait_ge(rooted, n + 1)
                    dve.reciprocal(stat[b][0:rows, 2:3], stat[b][0:rows, 1:2]).then_inc(inverted, 1)
                    dve.wait_ge(inverted, n + 1)
                    waits(dve, tp_ready, n - 1)
                    dve.scalar_tensor_tensor(xn[b][0:rows, :], xin[b][0:rows, :], stat[b][0:rows, 2:3],
                                             g[0:rows, :], ALU.mult, ALU.mult).then_inc(xn_ready, 1)

                def low(n, b, hi, lo, rows):
                    dve.wait_ge(hi_ready, n + 1)
                    dve.tensor_tensor(lo, tp[b][:, :, 0:rows], hi.bitcast(F32), ALU.subtract).then_inc(lo_ready, 1)

                def pair(i):
                    for b in range(2):
                        norm(i + b, b, P)
                    for b in range(2):
                        at = ds((i + b) * P, P)
                        low(i + b, b, xT[0][:, :, at], xT[1][:, :, at], P)

                peeled(dve, NT // 2, 2, pair)
                norm(NT, 0, NS)
                low(NT, 0, xs[0][:, :, :], xs[1][:, :, :], NS)

            @block.tensor
            def _(pe):
                pe.wait_ge(consts, 32)

                def turn(n, b, rows):
                    pe.wait_ge(xn_ready, n + 1)
                    waits(pe, lo_ready, n - 1)
                    for c in range(KC):
                        last = pe.transpose(tp[b][:, c, 0:rows], xn[b][0:rows, c * P:(c + 1) * P],
                                            ident[0:rows, 0:rows])
                    last.then_inc(tp_ready, 1)

                def pair(i):
                    for b in range(2):
                        turn(i + b, b, P)

                peeled(pe, NT // 2, 2, pair)
                turn(NT, 0, NS)


def stage_latents(nc, t, xT, xs, ident):
    with ExitStack() as ctx:
        m = Mem(nc, ctx, "lat")
        raw = [m.sb(f"raw{b}", [P, LAT]) for b in range(2)]
        w = [m.sb(f"w_{h}", [P, KC, LAT], F32R) for h in ("hi", "lo")]
        lat = [m.sb(f"lat{b}", [P, LAT]) for b in range(2)]
        nat = [m.sb(f"nat{b}", [P, LAT]) for b in range(2)]
        rot = [m.sb(f"rot{b}", [P, 2 * ROPE]) for b in range(2)]
        junk_q, junk_kv = m.sb("junk_q", [P, QL]), m.sb("junk_kv", [P, KL])
        stat = [m.sb(f"stat{b}", [P, 6]) for b in range(2)]
        eps = m.sb("eps", [P, 1])
        gkv = m.sb("gkv_rows", [P, KL])
        gq = m.sb("gq_cols", [P, QL // P])
        cs = m.sb("rope_rows", [P, NT + 1, 2, ROPE])
        cqT = m.sb("cqT", [P, QL // P, TOK])
        ckvT = m.sb("ckvT", [P, TOK])
        kpeT = m.sb("kpeT", [ROPE, TOK])
        pj = [m.ps(f"pj{b}", [P, 512]) for b in range(4)]
        tp = [m.ps(f"tp{b}", [P, 4, P]) for b in range(2)]
        consts = m.sem("consts")
        w_in = [m.sem(f"w_in{b}") for b in range(2)]
        w_hi, w_lo, eps_set = m.sem("w_hi"), m.sem("w_lo"), m.sem("eps_set")
        pj_ready, copied, squared, rooted, inverted = (
            m.sem(n) for n in ("pj_ready", "copied", "squared", "rooted", "inverted"))
        rotated, nat_ready, tp_ready, turned = (m.sem(n) for n in ("rotated", "nat_ready", "tp_ready", "turned"))
        nat_stored = [m.sem(f"nat_stored{b}") for b in range(2)]
        stored = m.sem("stored")
        tiles = [(i, P if i < NT else NS) for i in range(NT + 1)]

        with nc.Block() as block:
            @block.sync
            def _(sp):
                for c in range(KC):
                    waits(sp, w_lo, c - 1)
                    sp.dma_start(raw[c % 2][:, :], t["w_in"][c * P:(c + 1) * P, C_CQ:C_CQ + LAT])\
                        .then_inc(w_in[c % 2], 16)
                sp.dma_start(gkv[:, :], t["g_kv"].partition_broadcast(P)).then_inc(consts, 16)
                with nc.allow_non_contiguous_dma(reason="256 gains, one per partition"):
                    sp.dma_start(gq[:, :], t["g_q"].rearrange("(c p) -> p c", p=P)).then_inc(consts, 16)
                sp.dma_start(cs[:, 0:NT, :, :], t["rope_rows"][0:SEQ].rearrange("(i p) s r -> p i s r", p=P))\
                    .then_inc(consts, 16)
                sp.dma_start(cs[0:NS, NT, :, :], t["rope_rows"][SEQ:TOK]).then_inc(consts, 16)
                for i, rows in tiles:
                    b = i % 2
                    sp.wait_ge(nat_ready, i + 1)
                    if i < NT:
                        ckv, kpe = t["ckv_prompt"][i * P:(i + 1) * P, :], t["kpe_prompt"][i * P:(i + 1) * P, :]
                    else:
                        ckv, kpe = t["ckv_sample"], t["kpe_sample"]
                    sp.dma_start(ckv, nat[b][0:rows, QL:QL + KL]).then_inc(nat_stored[b], 16)
                    sp.dma_start(kpe, nat[b][0:rows, QL + KL:LAT]).then_inc(nat_stored[b], 16)
                sp.wait_ge(turned, NT + 1)
                for c in range(QL // P):
                    sp.dma_start(t["cqT"][c], cqT[:, c, :]).then_inc(stored, 16)
                sp.dma_start(t["ckvT"], ckvT[:, :]).then_inc(stored, 16)
                sp.dma_start(t["kpeT"], kpeT[:, :]).then_inc(stored, 16)
                sp.wait_ge(stored, 64)
                sp.wait_ge(nat_stored[0], 32 * 9)
                sp.wait_ge(nat_stored[1], 32 * 8)

            @block.scalar
            def _(act):
                for c in range(KC):
                    act.wait_ge(w_in[c % 2], 16 * (c // 2 + 1))
                    act.activation(w[0][:, c, :], raw[c % 2][:, :], ACT.Copy).then_inc(w_hi, 1)
                act.wait_ge(eps_set, 1)
                act.wait_ge(consts, 64)

                def turned_out(i, rows):
                    b, at = i % 2, slice(i * P, i * P + rows)
                    act.wait_ge(tp_ready, i + 1)
                    for c in range(QL // P):
                        act.activation(cqT[:, c, at], tp[b][:, c, 0:rows], ACT.Copy, scale=gq[:, c:c + 1])
                    act.activation(ckvT[:, at], tp[b][:, 2, 0:rows], ACT.Copy)
                    act.activation(kpeT[:, at], tp[b][0:ROPE, 3, 0:rows], ACT.Copy).then_inc(turned, 1)

                for i, rows in tiles:
                    b = i % 2
                    act.wait_ge(pj_ready, i + 1)
                    waits(act, nat_ready, i - 1)
                    r = slice(0, rows)
                    act.activation(junk_q[r, :], pj[i % 4][r, 0:QL], ACT.Square,
                                   accum_out=stat[b][r, 0:1]).then_inc(squared, 1)
                    act.activation(junk_kv[r, :], pj[i % 4][r, QL:QL + KL], ACT.Square,
                                   accum_out=stat[b][r, 1:2]).then_inc(squared, 1)
                    act.activation(lat[b][r, :], pj[i % 4][r, 0:LAT], ACT.Copy).then_inc(copied, 1)
                    act.wait_ge(squared, 2 * i + 2)
                    act.activation(stat[b][r, 2:3], stat[b][r, 0:1], ACT.Sqrt, bias=eps[r, :],
                                   scale=1.0 / QL).then_inc(rooted, 1)
                    act.activation(stat[b][r, 3:4], stat[b][r, 1:2], ACT.Sqrt, bias=eps[r, :],
                                   scale=1.0 / KL).then_inc(rooted, 1)
                    if i:
                        turned_out(i - 1, P)
                turned_out(NT, NS)

            @block.vector
            def _(dve):
                dve.memset(eps[:, :], EPS).then_inc(eps_set, 1)
                for c in range(KC):
                    dve.wait_ge(w_hi, c + 1)
                    dve.tensor_tensor(w[1][:, c, :], raw[c % 2][:, :], w[0][:, c, :].bitcast(F32),
                                      ALU.subtract).then_inc(w_lo, 1)
                dve.wait_ge(consts, 64)
                half = ROPE // 2
                for i, rows in tiles:
                    b, r = i % 2, slice(0, rows)
                    dve.wait_ge(rooted, 2 * i + 2)
                    dve.wait_ge(copied, i + 1)
                    dve.reciprocal(stat[b][r, 4:6], stat[b][r, 2:4]).then_inc(inverted, 1)
                    pe_at = lat[b][r, QL + KL:LAT]
                    dve.tensor_tensor(rot[b][r, 0:ROPE], pe_at, cs[r, i, 0, :], ALU.mult)
                    dve.tensor_tensor(rot[b][r, ROPE:ROPE + half], lat[b][r, QL + KL + half:LAT],
                                      cs[r, i, 1, 0:half], ALU.mult)
                    dve.tensor_tensor(rot[b][r, ROPE + half:2 * ROPE], lat[b][r, QL + KL:QL + KL + half],
                                      cs[r, i, 1, half:ROPE], ALU.mult).then_inc(rotated, 1)
                    dve.wait_ge(inverted, i + 1)
                    waits(dve, tp_ready, i - 1)
                    waits(dve, nat_stored[b], 32 * (i // 2))
                    dve.tensor_scalar(nat[b][r, 0:QL], lat[b][r, 0:QL], stat[b][r, 4:5], None, ALU.mult)
                    dve.scalar_tensor_tensor(nat[b][r, QL:QL + KL], lat[b][r, QL:QL + KL], stat[b][r, 5:6],
                                             gkv[r, :], ALU.mult, ALU.mult)
                    dve.wait_ge(rotated, i + 1)
                    dve.tensor_tensor(nat[b][r, QL + KL:LAT], rot[b][r, 0:ROPE], rot[b][r, ROPE:2 * ROPE],
                                      ALU.add).then_inc(nat_ready, 1)

            @block.tensor
            def _(pe):
                pe.wait_ge(w_lo, KC)

                def turn(i, rows):
                    b = i % 2
                    pe.wait_ge(nat_ready, i + 1)
                    waits(pe, turned, i - 1)
                    for c in range(3):
                        pe.transpose(tp[b][:, c, 0:rows], nat[b][0:rows, c * P:(c + 1) * P],
                                     ident[0:rows, 0:rows])
                    pe.transpose(tp[b][0:ROPE, 3, 0:rows], nat[b][0:rows, QL + KL:LAT],
                                 ident[0:rows, 0:rows]).then_inc(tp_ready, 1)

                for i, rows in tiles:
                    waits(pe, copied, i - 3)
                    for c in range(KC):
                        x = [xT[h][:, c, i * P:(i + 1) * P] if i < NT else xs[h][:, c, :] for h in range(2)]
                        last = split_matmul(pe, pj[i % 4][0:rows, 0:LAT], x, [w[h][:, c, :] for h in range(2)],
                                            c == 0, c == KC - 1)
                    last.then_inc(pj_ready, 1)
                    if i:
                        turn(i - 1, P)
                turn(NT, NS)


def stage_dilated(nc, t, xT, xs, ident):
    with ExitStack() as ctx:
        m = Mem(nc, ctx, "dil")
        raw = [m.sb(f"raw{b}", [P, KC, P]) for b in range(2)]
        w = [[m.sb(f"w{b}_{h}", [P, KC, P], F32R) for h in ("hi", "lo")] for b in range(2)]
        qT = m.sb("qT", [P, SEQ])
        kT = m.sb("kT", [P, SEQ])
        v = m.sb("v", [P, NT, VW])
        sm = [m.sb(f"sm{b}", [P, 2, 2, 2 * P]) for b in range(2)]
        pT = [m.sb(f"pT{b}", [P, 4, P]) for b in range(2)]
        neg = [m.sb(f"neg{b}", [P, 2, 2]) for b in range(2)]
        rec = [m.sb(f"rec{b}", [P, 2, REC]) for b in range(4)]
        knat = m.sb("knat", [P, 4, P])
        bias = m.sb("bias", [P, 2, 2 * P])
        hs = m.sb("hs", [NS, 3, P])
        S = m.ps("S", [P, 4, 512])
        T = m.ps("T", [P, 2, 4, P])
        O = m.ps("O", [P, 2, 2, 256])

        raw_in = [m.sem(f"raw_in{b}") for b in range(2)]
        bias_in, ones_set = m.sem("bias_in"), m.sem("ones_set")
        w_hi, w_lo = m.sem("w_hi"), m.sem("w_lo")
        q_ready, k_ready, v_ready, hs_ready = (m.sem(n) for n in ("q_ready", "k_ready", "v_ready", "hs_ready"))
        q_out, k_out, v_out, hs_out = (m.sem(n) for n in ("q_out", "k_out", "v_out", "hs_out"))
        kn_ready, kn_out, kn_stored = m.sem("kn_ready"), m.sem("kn_out"), m.sem("kn_stored")
        v_stored, hs_stored = m.sem("v_stored"), m.sem("hs_stored")
        s_ready, masked, negated, exped = (m.sem(n) for n in ("s_ready", "masked", "negated", "exped"))
        t_ready, t_out_a, t_out_b = m.sem("t_ready"), m.sem("t_out_a"), m.sem("t_out_b")
        pv_ready, rec_out = m.sem("pv_ready"), m.sem("rec_out")
        rec_stored = [m.sem(f"rec_stored{b}") for b in range(4)]
        sp_ticks, dve_ticks = m.sem("sp_ticks"), m.sem("dve_ticks")
        NU = NT // 2
        KN_TILES = [min(w_, SEQ) // P for w_, _ in GROUPS]
        KN = [-(-n // 4) for n in KN_TILES]
        KN_BASE = [sum(4 * KN[h] for h in range(g)) for g in range(NG)]

        def each_pair(eng, body):
            body(0, 0, 0)
            for g in range(NG):
                with eng.Fori(0 if g else 1, 4) as hp:
                    body(g, hp, hp + 4 * g)

        def blocks(g, u):
            nb = NT // GROUPS[g][1]
            return [(s, 2 * u + s, 2 * u + s - ((2 * u + s) % nb > 0), 1 + ((2 * u + s) % nb > 0)) for s in range(2)]

        def tokens(g, j, count=1):
            d = GROUPS[g][1]
            nb = NT // d
            start = j // nb + d * P * (j % nb)
            return slice(start, start + d * (count * P - 1) + 1, d)

        with nc.Block() as block:
            @block.sync
            def _(sp):
                def body(g, hp, n):
                    for which in range(3):
                        if which < 2:
                            held(sp, w_lo, n * 3 - (1 if which else 0), sp_ticks)
                        else:
                            held(sp, w_lo, n * 3 + 1, sp_ticks)
                        src = t["w_in"][:, ds(which * QKV + g * AW + hp * P, P)]
                        sp.dma_start(raw[which % 2][:, :, :], src.rearrange("(c p) n -> p c n", p=P))\
                            .then_inc(raw_in[which % 2], 16)
                    held(sp, masked, n * NU, sp_ticks)
                    sp.dma_start(bias[:, :, :], t["alibi"][g, :, ds(hp * 2, 2), :]).then_inc(bias_in, 16)
                    held(sp, hs_out, n + 1, sp_ticks)
                    for which in range(3):
                        sp.dma_start(t["hs"][:, ds(which * QKV + g * AW + hp * P, P)], hs[:, which, :])\
                            .then_inc(hs_stored, 16)
                    held(sp, v_out, (n + 1) * 4, sp_ticks)
                    win = t[f"win{g}_prompt"][0]
                    col = ds(hp * P, P)
                    if g == 0:
                        sp.dma_start(win[:, 1, col], v[:, NT - 1, 2:2 + P]).then_inc(v_stored, 16)
                    elif g == 1:
                        sp.dma_start(win[:, 1, col].rearrange("(i d) c -> i d c", d=4), v[:, 3:NT:4, 2:2 + P])\
                            .then_inc(v_stored, 16)
                    else:
                        sp.dma_start(win[:, 1, col].rearrange("(i d) c -> i d c", d=NT), v[:, :, 2:2 + P])\
                            .then_inc(v_stored, 16)
                    for k in range(KN[g]):
                        tiles = min(4, KN_TILES[g])
                        held(sp, kn_out, KN_BASE[g] + hp * KN[g] + k + 1, sp_ticks)
                        rows = slice(k * 4 * P, (k * 4 + tiles) * P)
                        sp.dma_start(win[rows, 0, col].rearrange("(s p) c -> p s c", p=P), knat[:, 0:tiles, :])\
                            .then_inc(kn_stored, 16)
                    for u in range(NU):
                        held(sp, rec_out, n * NU + u + 1, sp_ticks)
                        for s, j, _, _ in blocks(g, u):
                            sp.dma_start(t["oa"][tokens(g, j), g, ds(hp, 1), :].rearrange("i o e -> i (o e)"),
                                         rec[u % 4][:, s, :]).then_inc(rec_stored[u % 4], 16)

                each_pair(sp, body)
                sp.wait_ge(hs_stored, 12 * 48)
                sp.wait_ge(v_stored, 12 * 16)
                sp.wait_ge(kn_stored, 16 * (KN_BASE[2] + 4 * KN[2]))
                for b in range(4):
                    sp.wait_ge(rec_stored[b], 12 * NU // 4 * 32)

            @block.gpsimd
            def _(pool):
                pool.memset(v[:, :, 0:1], 1.0)
                pool.memset(v[:, :, 1:2], 0.0)
                pool.memset(v[:, :, 2 + P:3 + P], 1.0)
                pool.memset(v[:, :, 3 + P:VW], 0.0).then_inc(ones_set, 1)

            @block.scalar
            def _(act):
                def high(n, which):
                    b = which % 2
                    act.wait_ge(raw_in[b], n * (16 if b else 32) + (32 if which == 2 else 16))
                    if which < 2:
                        waits(act, hs_ready, n * 3 - (1 if which else 0))
                    else:
                        act.wait_ge(hs_ready, n * 3 + 1)
                    act.activation(w[b][0][:, :, :], raw[b][:, :, :], ACT.Copy).then_inc(w_hi, 1)

                def body(g, hp, n):
                    high(n, 0)
                    high(n, 1)
                    for k in range(4):
                        act.wait_ge(q_ready, n * 4 + k + 1)
                        act.activation(qT[:, k * 512:(k + 1) * 512], S[:, k, :], ACT.Copy, scale=A_SCALE)\
                            .then_inc(q_out, 1)
                    high(n, 2)
                    for k in range(4):
                        act.wait_ge(v_ready, n * 4 + k + 1)
                        if k == 0:
                            waits(act, v_stored, n * 16)
                        act.activation(v[:, 4 * k:4 * k + 4, 2:2 + P],
                                       S[:, k, :].rearrange("p (s c) -> p s c", c=P), ACT.Copy).then_inc(v_out, 1)
                    act.wait_ge(hs_ready, n * 3 + 3)
                    waits(act, hs_stored, n * 48)
                    act.activation(hs[:, :, :], O[0:NS, 0, :, :].rearrange("p a b -> p (a b)")[:, 0:3 * P]
                                   .rearrange("p (a b) -> p a b", a=3), ACT.Copy).then_inc(hs_out, 1)

                    def exps(u):
                        b = u % 2
                        act.wait_ge(negated, n * NU + u + 1)
                        for s, _, _, nk in blocks(g, u):
                            for h in range(2):
                                part = sm[b][:, s, h, 0:nk * P]
                                last = act.activation(part, part, ACT.Exp, bias=neg[b][:, s, h:h + 1])
                        last.then_inc(exped, 1)

                    def turned(u):
                        act.wait_ge(t_ready, (n * NU + u) * 2 + 1)
                        waits(act, pv_ready, n * NU + u)
                        q = 2 * blocks(g, u)[0][3]
                        act.activation(pT[0][:, 0:q, :], T[:, 0, 0:q, :], ACT.Copy).then_inc(t_out_a, 1)

                    for u in range(NU + 1):
                        if u < NU:
                            exps(u)
                        if u:
                            turned(u - 1)

                each_pair(act, body)

            @block.vector
            def _(dve):
                def low(n, which):
                    b = which % 2
                    dve.wait_ge(w_hi, n * 3 + which + 1)
                    dve.tensor_tensor(w[b][1][:, :, :], raw[b][:, :, :], w[b][0][:, :, :].bitcast(F32),
                                      ALU.subtract).then_inc(w_lo, 1)

                def body(g, hp, n):
                    low(n, 0)
                    low(n, 1)
                    low(n, 2)
                    for k in range(4):
                        dve.wait_ge(k_ready, n * 4 + k + 1)
                        dve.tensor_copy(kT[:, k * 512:(k + 1) * 512], S[:, k, :]).then_inc(k_out, 1)
                    tiles = min(4, KN_TILES[g])
                    for k in range(KN[g]):
                        c = KN_BASE[g] + hp * KN[g] + k
                        dve.wait_ge(kn_ready, c + 1)
                        waits(dve, kn_stored, c * 16)
                        dve.tensor_copy(knat[:, 0:tiles, :], T[:, k % 2, 0:tiles, :]).then_inc(kn_out, 1)
                    dve.wait_ge(bias_in, n * 16 + 16)

                    def mask(u):
                        b, c = u % 2, n * NU + u
                        dve.wait_ge(s_ready, c + 1)
                        waits(dve, t_ready, (c - 1) * 2)
                        held(dve, rec_stored[u % 4], (n * (NU // 4) + u // 4) * 32, dve_ticks)
                        for s, _, _, nk in blocks(g, u):
                            for h in range(2):
                                last = dve.tensor_tensor_reduce(
                                    sm[b][:, s, h, 0:nk * P], S[:, 2 * b + h, s * 2 * P:(s * 2 + nk) * P],
                                    bias[:, h, (2 - nk) * P:2 * P], 1.0, LOWEST, ALU.add, ALU.max,
                                    rec[u % 4][:, s, 2 * HD + 2 + h:2 * HD + 3 + h])
                        last.then_inc(masked, 1)
                        dve.wait_ge(masked, c + 1)
                        dve.tensor_scalar(neg[b][:, :, :], rec[u % 4][:, :, 2 * HD + 2:REC], -1.0, None, ALU.mult)\
                            .then_inc(negated, 1)

                    def turned(u):
                        c = n * NU + u
                        dve.wait_ge(t_ready, c * 2 + 2)
                        waits(dve, pv_ready, c)
                        q = 2 * blocks(g, u)[1][3]
                        dve.tensor_copy(pT[1][:, 0:q, :], T[:, 1, 0:q, :]).then_inc(t_out_b, 1)

                    def records(u):
                        b = u % 2
                        dve.wait_ge(pv_ready, n * NU + u + 1)
                        dve.tensor_copy(rec[u % 4][:, :, 0:2 * HD], O[:, b, :, 2:2 + 2 * HD])
                        dve.tensor_copy(rec[u % 4][:, :, 2 * HD:2 * HD + 2], O[:, b, :, 0:2 + P + 1:P + 2])\
                            .then_inc(rec_out, 1)

                    for u in range(NU + 2):
                        if u < NU:
                            mask(u)
                        if 0 < u <= NU:
                            turned(u - 1)
                        if u > 1:
                            records(u - 2)

                each_pair(dve, body)

            @block.tensor
            def _(pe):
                def body(g, hp, n):
                    for which, ready in ((0, q_ready), (1, k_ready)):
                        pe.wait_ge(w_lo, n * 3 + which + 1)
                        for k in range(4):
                            if which == 0:
                                waits(pe, masked, n * NU)
                            else:
                                pe.wait_ge(q_out, n * 4 + k + 1)
                            for c in range(KC):
                                last = split_matmul(pe, S[:, k, :], [w[which][h][:, c, :] for h in range(2)],
                                                    [xT[h][:, c, k * 512:(k + 1) * 512] for h in range(2)],
                                                    c == 0, c == KC - 1)
                            last.then_inc(ready, 1)
                        sample(g, n, which)
                    pe.wait_ge(w_lo, n * 3 + 3)
                    for k in range(4):
                        pe.wait_ge(k_out, n * 4 + k + 1)
                        for s in range(4):
                            at = tokens(g, 4 * k + s)
                            for c in range(KC):
                                last = split_matmul(pe, S[:, k, s * P:(s + 1) * P],
                                                    [xT[h][:, c, at] for h in range(2)],
                                                    [w[0][h][:, c, :] for h in range(2)], c == 0, c == KC - 1)
                        last.then_inc(v_ready, 1)
                    sample(g, n, 2)
                    for k in range(KN[g]):
                        c = KN_BASE[g] + hp * KN[g] + k
                        if k < 2:
                            waits(pe, t_out_a, n * NU)
                            waits(pe, t_out_b, n * NU)
                        else:
                            pe.wait_ge(kn_out, c - 1)
                        for s in range(min(4, KN_TILES[g])):
                            at = SEQ - KN_TILES[g] * P + (4 * k + s) * P
                            last = pe.transpose(T[:, k % 2, s, :], kT[:, at:at + P], ident[:, :])
                        last.then_inc(kn_ready, 1)
                    pe.wait_ge(v_out, n * 4 + 4)
                    pe.wait_ge(ones_set, 1)

                    def scores(u):
                        c = n * NU + u
                        if u > 1:
                            pe.wait_ge(masked, c - 1)
                        for s, j, j0, nk in blocks(g, u):
                            for h in range(2):
                                r = slice(h * HD, (h + 1) * HD)
                                last = pe.matmul(S[:, 2 * (u % 2) + h, s * 2 * P:(s * 2 + nk) * P],
                                                 qT[r, tokens(g, j)], kT[r, tokens(g, j0, nk)],
                                                 start=True, stop=True)
                        last.then_inc(s_ready, 1)

                    def turns(u):
                        c = n * NU + u
                        pe.wait_ge(exped, c + 1)
                        if u:
                            pe.wait_ge(t_out_a, c)
                            pe.wait_ge(t_out_b, c)
                        else:
                            pe.wait_ge(kn_out, KN_BASE[g] + hp * KN[g] + KN[g])
                            waits(pe, t_out_a, c)
                            waits(pe, t_out_b, c)
                        for s, _, _, nk in blocks(g, u):
                            for h in range(2):
                                for k in range(nk):
                                    last = pe.transpose(T[:, s, h * nk + k, :],
                                                        sm[u % 2][:, s, h, k * P:(k + 1) * P], ident[:, :])
                            last.then_inc(t_ready, 1)

                    def values(u):
                        c = n * NU + u
                        pe.wait_ge(t_out_a, c + 1)
                        pe.wait_ge(t_out_b, c + 1)
                        if u > 1:
                            pe.wait_ge(rec_out, c - 1)
                        elif u == 0:
                            pe.wait_ge(hs_out, n + 1)
                            waits(pe, rec_out, c - 1)
                        else:
                            waits(pe, rec_out, c - 1)
                        for s, j, j0, nk in blocks(g, u):
                            for h in range(2):
                                for k in range(nk):
                                    last = pe.matmul(O[:, u % 2, s, h * 66:(h + 1) * 66], pT[s][:, h * nk + k, :],
                                                     v[:, j0 + k, h * 66:(h + 1) * 66],
                                                     start=(k == 0), stop=(k == nk - 1))
                        last.then_inc(pv_ready, 1)

                    for u in range(NU + 2):
                        if u < NU:
                            scores(u)
                        if 0 < u <= NU:
                            turns(u - 1)
                        if u > 1:
                            values(u - 2)

                def sample(g, n, which):
                    if which == 0:
                        waits(pe, rec_out, n * NU)
                    out = O[0:NS, 0, :, :].rearrange("p a b -> p (a b)")[:, which * P:(which + 1) * P]
                    for c in range(KC):
                        last = split_matmul(pe, out, [xs[h][:, c, :] for h in range(2)],
                                            [w[which % 2][h][:, c, :] for h in range(2)], c == 0, c == KC - 1)
                    last.then_inc(hs_ready, 1)

                each_pair(pe, body)


def stage_gates(nc, t, xT, xs):
    with ExitStack() as ctx:
        m = Mem(nc, ctx, "gate")
        raw = [m.sb(f"raw{b}", [P, KC, P]) for b in range(2)]
        w = [[m.sb(f"w{b}_{h}", [P, KC, P], F32R) for h in ("hi", "lo")] for b in range(2)]
        out = [m.sb(f"out{b}", [P, TOK]) for b in range(2)]
        BANKS = 5
        ps = m.ps("ps", [P, BANKS, 512])
        raw_in = [m.sem(f"raw_in{b}") for b in range(2)]
        w_hi, w_lo, ready, sig, emptied = (m.sem(n) for n in ("w_hi", "w_lo", "ready", "sig", "emptied"))
        stored = [m.sem(f"stored{b}") for b in range(2)]
        sp_ticks = m.sem("sp_ticks")
        KINDS = ((C_ZA, 0, 2, True), (C_ZB, 4, 2, True), (C_MA, 8, 8, False))
        CHUNKS = [(k * 512, 512) for k in range(4)] + [(SEQ, NS)]

        def each(eng, body):
            n = 0
            for col, blk, pairs, mult in KINDS:
                if n == 0:
                    body(col, blk, 0, mult)
                with eng.Fori(0 if n else 1, pairs) as i:
                    body(i * 2 * P + col, i * 2 + blk, i + n, mult)
                n += pairs

        with nc.Block() as block:
            @block.sync
            def _(sp):
                def body(col, blk, n, mult):
                    for b in range(2):
                        held(sp, w_lo, n * 2 - 1 + b, sp_ticks)
                        sp.dma_start(raw[b][:, :, :],
                                     t["w_in"][:, ds(col + b * P, P)].rearrange("(c p) n -> p c n", p=P))\
                            .then_inc(raw_in[b], 16)

                each(sp, body)

            @block.scalar
            def _(act):
                def body(col, blk, n, mult):
                    for b in range(2):
                        act.wait_ge(raw_in[b], n * 16 + 16)
                        waits(act, ready, (n * 2 + b - 1) * 5)
                        act.activation(w[b][0][:, :, :], raw[b][:, :, :], ACT.Copy).then_inc(w_hi, 1)
                    for b in range(2):
                        waits(act, stored[b], n * 16)
                        for k, (at, width) in enumerate(CHUNKS):
                            act.wait_ge(ready, n * 10 + b * 5 + k + 1)
                            act.activation(out[b][:, at:at + width], ps[:, k, 0:width], ACT.Sigmoid)\
                                .then_inc(sig, 1)

                each(act, body)

            @block.gpsimd
            def _(pool):
                def body(col, blk, n, mult):
                    for b in range(2):
                        pool.wait_ge(emptied, n * 10 + b * 5 + 5)
                        pool.dma_start(t["gates"][ds(blk + b, 1)].rearrange("o p n -> (o p) n"), out[b][:, :])\
                            .then_inc(stored[b], 16)

                each(pool, body)
                for b in range(2):
                    pool.wait_ge(stored[b], 12 * 16)

            @block.vector
            def _(dve):
                def body(col, blk, n, mult):
                    for b in range(2):
                        dve.wait_ge(w_hi, n * 2 + b + 1)
                        dve.tensor_tensor(w[b][1][:, :, :], raw[b][:, :, :], w[b][0][:, :, :].bitcast(F32),
                                          ALU.subtract).then_inc(w_lo, 1)
                    for b in range(2):
                        for k, (at, width) in enumerate(CHUNKS):
                            dve.wait_ge(sig, n * 10 + b * 5 + k + 1)
                            o = out[b][:, at:at + width]
                            if mult:
                                dve.tensor_tensor(o, o, ps[:, k, 0:width], ALU.mult).then_inc(emptied, 1)
                            else:
                                dve.sem_inc(emptied, 1)

                each(dve, body)

            @block.tensor
            def _(pe):
                def body(col, blk, n, mult):
                    for b in range(2):
                        pe.wait_ge(w_lo, n * 2 + b + 1)
                        for k, (at, width) in enumerate(CHUNKS):
                            waits(pe, emptied, (n * 2 + b - 1) * 5 + k + 1)
                            for c in range(KC):
                                x = [xT[h][:, c, at:at + width] if at < SEQ else xs[h][:, c, :] for h in range(2)]
                                last = split_matmul(pe, ps[:, k, 0:width], [w[b][h][:, c, :] for h in range(2)],
                                                    x, c == 0, c == KC - 1)
                            last.then_inc(ready, 1)

                each(pe, body)


def load_latents(sp, t, cqT, ckvT, k96, rope, causal, loaded):
    for c in range(QL // P):
        sp.dma_start(cqT[:, c, :], t["cqT"][c]).then_inc(loaded, 16)
    sp.dma_start(ckvT[:, :], t["ckvT"]).then_inc(loaded, 16)
    sp.dma_start(k96[NOPE:NOPE + ROPE, :], t["kpeT"][:, 0:SEQ]).then_inc(loaded, 16)
    sp.dma_start(rope[NOPE:P, :], t["rope_cols"]).then_inc(loaded, 16)
    sp.dma_start(causal[:, :], t["causal"]).then_inc(loaded, 16)


def load_head_weights(eng, t, h, wq, wk, wv, sem):
    W = NOPE + ROPE
    half = ROPE // 2
    uq = t["w_uq"].rearrange("(c p) n -> p c n", p=P)
    eng.dma_start(wq[:, :, 0:W], uq[:, :, ds(h * W, W)]).then_inc(sem, 16)
    eng.dma_start(wq[:, :, W:W + half], uq[:, :, ds(h * W + NOPE + half, half)]).then_inc(sem, 16)
    eng.dma_start(wq[:, :, W + half:P], uq[:, :, ds(h * W + NOPE, half)]).then_inc(sem, 16)
    eng.dma_start(wk[:, :], t["w_uk"][:, ds(h, 1), :].rearrange("c o d -> c (o d)")).then_inc(sem, 16)
    eng.dma_start(wv[:, :], t["w_uv"][:, ds(h, 1), :].rearrange("c o d -> c (o d)")).then_inc(sem, 16)


def stage_latent_attn(nc, t, ident):
    with ExitStack() as ctx:
        m = Mem(nc, ctx, "mla")
        cqT = m.sb("cqT", [P, QL // P, TOK])
        ckvT = m.sb("ckvT", [P, TOK])
        rope = m.sb("rope", [P, TOK])
        causal = m.sb("causal", [P, P])
        q96 = m.sb("q96", [P, TOK])
        k96 = m.sb("k96", [P, SEQ])
        turned = [m.sb(f"turned{b}", [P, 2, 512]) for b in range(2)]
        wq = [m.sb(f"wq{b}", [P, QL // P, P]) for b in range(2)]
        wk = [m.sb(f"wk{b}", [P, NOPE]) for b in range(2)]
        wv = [m.sb(f"wv{b}", [P, HD]) for b in range(2)]
        v = m.sb("v", [P, NT, VB])
        p = [m.sb(f"p{b}", [P, 8 * P]) for b in range(2)]
        pT = [m.sb(f"pT{b}", [P, 4, P]) for b in range(2)]
        stat = [m.sb(f"stat{b}", [P, 2]) for b in range(2)]
        rec = [m.sb(f"rec{b}", [P, RECB]) for b in range(4)]
        S = m.ps("S", [P, 4, 512])
        T = m.ps("T", [P, 2, 4, P])
        O = m.ps("O", [P, 2, 512])
        loaded, ones_set = m.sem("loaded"), m.sem("ones_set")
        w_in = [m.sem(f"w_in{b}") for b in range(2)]
        q_ready, q_out, q_t, q_rot, k_ready, k_out, v_ready, v_out = (
            m.sem(n) for n in ("q_ready", "q_out", "q_t", "q_rot", "k_ready", "k_out", "v_ready", "v_out"))
        s_ready, capped, maxed, negated, exped, t_ready, t_out_a, t_out_b, pv_ready, rec_out = (
            m.sem(n) for n in ("s_ready", "capped", "maxed", "negated", "exped", "t_ready", "t_out_a", "t_out_b",
                               "pv_ready", "rec_out"))
        q_stored, sp_ticks = m.sem("q_stored"), m.sem("sp_ticks")
        rec_stored = [m.sem(f"rec_stored{b}") for b in range(4)]
        UNITS = [(i, 8 * c, min(i + 1 - 8 * c, 8)) for i in range(NT) for c in range(1 + i // 8)]
        NU = len(UNITS)
        assert NU % 4 == 0
        HALF_B = [sum(k > 4 for _, _, k in UNITS[:u]) for u in range(NU + 1)]
        DIAG = [sum(j + k == i + 1 for i, j, k in UNITS[:u]) for u in range(NU + 1)]
        QCH = [(k * 512, 512) for k in range(4)] + [(SEQ, NS)]

        def each_head(eng, body):
            body(0, 0)
            body(1, 1)
            with eng.Fori(1, H // 2) as i:
                body(i * 2, 0)
                body(i * 2 + 1, 1)

        with nc.Block() as block:
            @block.sync
            def _(sp):
                load_latents(sp, t, cqT, ckvT, k96, rope, causal, loaded)
                load_head_weights(sp, t, 0, wq[0], wk[0], wv[0], w_in[0])
                load_head_weights(sp, t, 1, wq[1], wk[1], wv[1], w_in[1])

                def body(h, b):
                    if isinstance(h, int):
                        pass
                    else:
                        held(sp, v_ready, h * 2 - 2, sp_ticks)
                        load_head_weights(sp, t, h, wq[b], wk[b], wv[b], w_in[b])
                    held(sp, q_rot, h * 5 + 5, sp_ticks)
                    held(sp, q_out, h * 5 + 5, sp_ticks)
                    sp.dma_start(t["qs96"][ds(h, 1)].rearrange("o c n -> (o c) n"),
                                 q96[0:NOPE + ROPE, SEQ:TOK]).then_inc(q_stored, 16)
                    for u, (i, j, _) in enumerate(UNITS):
                        held(sp, rec_out, h * NU + u + 1, sp_ticks)
                        sp.dma_start(t["ob"][i * P:(i + 1) * P, j // 8, ds(h, 1), :].rearrange("i o e -> i (o e)"),
                                     rec[u % 4][:, :]).then_inc(rec_stored[u % 4], 16)

                each_head(sp, body)
                sp.wait_ge(q_stored, 16 * H)
                for b in range(4):
                    sp.wait_ge(rec_stored[b], 16 * H * NU // 4)

            @block.gpsimd
            def _(pool):
                pool.memset(v[:, :, HD:HD + 1], 1.0)
                pool.memset(v[:, :, HD + 1:VB], 0.0).then_inc(ones_set, 1)

            @block.scalar
            def _(act):
                def body(h, b):
                    waits(act, q_stored, h * 16)
                    for k, (at, width) in enumerate(QCH):
                        act.wait_ge(q_ready, h * 5 + k + 1)
                        act.activation(q96[0:NOPE, at:at + width], S[0:NOPE, k % 4, 0:width], ACT.Copy)\
                            .then_inc(q_out, 1)
                    for k in range(4):
                        act.wait_ge(k_ready, h * 4 + k + 1)
                        act.activation(k96[0:NOPE, k * 512:(k + 1) * 512], S[0:NOPE, k, :], ACT.Copy)\
                            .then_inc(k_out, 1)
                    for k in range(2):
                        act.wait_ge(v_ready, h * 2 + k + 1)
                        act.activation(v[:, 8 * k:8 * k + 8, 0:HD],
                                       O[:, k, :].rearrange("p (s c) -> p s c", c=HD), ACT.Copy).then_inc(v_out, 1)

                    def exps(u):
                        c, (i, j, nk) = h * NU + u, UNITS[u]
                        act.wait_ge(negated, c + 1)
                        waits(act, t_ready, (c - 1) * 2)
                        s2 = S[:, 2 * (u % 2):2 * (u % 2) + 2, :].rearrange("p a b -> p (a b)")
                        act.activation(p[u % 2][:, 0:nk * P], s2[:, 0:nk * P], ACT.Exp,
                                       bias=stat[u % 2][:, 1:2], scale=B_SCALE).then_inc(exped, 1)

                    def turn_out(u):
                        c, (_, _, nk) = h * NU + u, UNITS[u]
                        act.wait_ge(t_ready, c * 2 + 1)
                        waits(act, pv_ready, c)
                        q = min(nk, 4)
                        act.activation(pT[0][:, 0:q, :], T[:, 0, 0:q, :], ACT.Copy).then_inc(t_out_a, 1)

                    for u in range(NU + 1):
                        if u < NU:
                            exps(u)
                        if u:
                            turn_out(u - 1)

                each_head(act, body)

            @block.vector
            def _(dve):
                dve.wait_ge(loaded, 96)

                def body(h, b):
                    for k, (at, width) in enumerate(QCH):
                        n = h * 5 + k
                        dve.wait_ge(q_ready, n + 1)
                        waits(dve, q_rot, n - 1)
                        if k == 4:
                            waits(dve, q_stored, h * 16)
                        src = slice(at, at + width)
                        r, sw = slice(NOPE, NOPE + ROPE), slice(NOPE + ROPE, P)
                        tb = turned[k % 2]
                        dve.tensor_tensor(tb[r, 0, 0:width], S[r, k % 4, 0:width], rope[r, src], ALU.mult)
                        dve.tensor_tensor(tb[r, 1, 0:width], S[sw, k % 4, 0:width], rope[sw, src], ALU.mult)\
                            .then_inc(q_t, 1)
                        dve.wait_ge(q_t, n + 1)
                        dve.tensor_tensor(q96[r, src], tb[r, 0, 0:width], tb[r, 1, 0:width], ALU.add)\
                            .then_inc(q_rot, 1)

                    def maxima(u):
                        c, (i, j, nk), b2 = h * NU + u, UNITS[u], u % 2
                        dve.wait_ge(s_ready, c + 1)
                        waits(dve, rec_stored[u % 4], (h * (NU // 4) + u // 4) * 16)
                        waits(dve, exped, c - 1)
                        s2 = S[:, 2 * b2:2 * b2 + 2, :].rearrange("p a b -> p (a b)")
                        if j + nk == i + 1:
                            diag = s2[:, (nk - 1) * P:nk * P]
                            dve.tensor_tensor(diag, diag, causal[:, :], ALU.add).then_inc(capped, 1)
                            dve.wait_ge(capped, h * DIAG[NU] + DIAG[u] + 1)
                        dve.tensor_reduce(stat[b2][:, 0:1], s2[:, 0:nk * P], AX.X, ALU.max).then_inc(maxed, 1)
                        dve.wait_ge(maxed, c + 1)
                        dve.tensor_scalar(stat[b2][:, 1:2], stat[b2][:, 0:1], -B_SCALE, None, ALU.mult)\
                            .then_inc(negated, 1)
                        dve.tensor_scalar(rec[u % 4][:, HD + 1:RECB], stat[b2][:, 0:1], B_SCALE, None, ALU.mult)

                    def turn_out(u):
                        c, (_, _, nk) = h * NU + u, UNITS[u]
                        if nk > 4:
                            dve.wait_ge(t_ready, c * 2 + 2)
                            waits(dve, pv_ready, c)
                            dve.tensor_copy(pT[1][:, 0:nk - 4, :], T[:, 1, 0:nk - 4, :]).then_inc(t_out_b, 1)

                    def record(u):
                        dve.wait_ge(pv_ready, h * NU + u + 1)
                        dve.tensor_copy(rec[u % 4][:, 0:HD + 1], O[:, u % 2, 0:HD + 1]).then_inc(rec_out, 1)

                    for u in range(NU + 2):
                        if u < NU:
                            maxima(u)
                        if 0 < u <= NU:
                            turn_out(u - 1)
                        if u > 1:
                            record(u - 2)

                each_head(dve, body)

            @block.tensor
            def _(pe):
                pe.wait_ge(loaded, 96)
                pe.wait_ge(ones_set, 1)

                def body(h, b):
                    pe.wait_ge(w_in[b], (h - b + 2) * 40)
                    for k, (at, width) in enumerate(QCH):
                        if k < 4:
                            waits(pe, exped, h * NU)
                        else:
                            pe.wait_ge(q_out, h * 5 + 1)
                            pe.wait_ge(q_rot, h * 5 + 1)
                        for c in range(QL // P):
                            last = pe.matmul(S[:, k % 4, 0:width], wq[b][:, c, :], cqT[:, c, at:at + width],
                                             start=c == 0, stop=c == QL // P - 1)
                        last.then_inc(q_ready, 1)
                    for k in range(4):
                        pe.wait_ge(q_out, h * 5 + (5 if k == 0 else k + 1))
                        pe.wait_ge(q_rot, h * 5 + (5 if k == 0 else k + 1))
                        pe.matmul(S[0:NOPE, k, :], wk[b][:, :], ckvT[:, k * 512:(k + 1) * 512],
                                  start=True, stop=True).then_inc(k_ready, 1)
                    waits(pe, rec_out, h * NU)
                    for k in range(2):
                        for s in range(8):
                            at = (8 * k + s) * P
                            last = pe.matmul(O[:, k, s * HD:(s + 1) * HD], ckvT[:, at:at + P], wv[b][:, :],
                                             start=True, stop=True)
                        last.then_inc(v_ready, 1)
                    pe.wait_ge(k_out, h * 4 + 4)
                    pe.wait_ge(v_out, h * 2 + 2)

                    def scores(u):
                        c, (i, j, nk) = h * NU + u, UNITS[u]
                        if u > 1:
                            pe.wait_ge(exped, c - 1)
                        for a in range(0, nk, 4):
                            width = min(nk - a, 4) * P
                            last = pe.matmul(S[:, 2 * (u % 2) + a // 4, 0:width], q96[0:NOPE + ROPE, i * P:(i + 1) * P],
                                             k96[0:NOPE + ROPE, (j + a) * P:(j + a) * P + width],
                                             start=True, stop=True)
                        last.then_inc(s_ready, 1)

                    def turns(u):
                        c, (_, _, nk) = h * NU + u, UNITS[u]
                        pe.wait_ge(exped, c + 1)
                        waits(pe, t_out_a, c)
                        for k in range(min(nk, 4)):
                            last = pe.transpose(T[:, 0, k, :], p[u % 2][:, k * P:(k + 1) * P], ident[:, :])
                        if nk <= 4:
                            last.then_inc(t_ready, 2)
                            return
                        last.then_inc(t_ready, 1)
                        waits(pe, t_out_b, h * HALF_B[NU] + HALF_B[u])
                        for k in range(4, nk):
                            last = pe.transpose(T[:, 1, k - 4, :], p[u % 2][:, k * P:(k + 1) * P], ident[:, :])
                        last.then_inc(t_ready, 1)

                    def values(u):
                        c, (_, j, nk) = h * NU + u, UNITS[u]
                        pe.wait_ge(t_out_a, c + 1)
                        if nk > 4:
                            pe.wait_ge(t_out_b, h * HALF_B[NU] + HALF_B[u] + 1)
                        if u > 1:
                            pe.wait_ge(rec_out, c - 1)
                        for k in range(nk):
                            last = pe.matmul(O[:, u % 2, 0:VB], pT[k // 4][:, k % 4, :], v[:, j + k, :],
                                             start=k == 0, stop=k == nk - 1)
                        last.then_inc(pv_ready, 1)

                    for u in range(NU + 2):
                        if u < NU:
                            scores(u)
                        if 0 < u <= NU:
                            turns(u - 1)
                        if u > 1:
                            values(u - 2)

                each_head(pe, body)


def stage_sample_dilated(nc, t, ident):
    with ExitStack() as ctx:
        m = Mem(nc, ctx, "sdil")
        R = DT * H
        kv = [m.sb(f"kv{b}", [P, DT, NG, 2, AW]) for b in range(2)]
        qb = [m.sb(f"qb{b}", [P, DT, NG, AW]) for b in range(2)]
        row = [m.sb(f"row{b}", [R, 3, NG, HD]) for b in range(2)]
        prod = [m.sb(f"prod{b}", [P, NG, AW]) for b in range(2)]
        st = m.sb("st", [P, NG, R])
        sr = m.sb("sr", [R, NG * P + NG])
        selfp = m.sb("selfp", [R, NG, HD])
        bias = m.sb("bias", [R, NG, P])
        stat = m.sb("stat", [R, 4])
        own = m.sb("own", [R, 2, HD])
        own3 = m.sb("own3", [R, NG, HD])
        pT = m.sb("pT", [P, NG, R])
        ownT = m.sb("ownT", [P, R])
        oT = m.sb("oT", [P, 4, NS])
        tS = m.ps("tS", [P, 512])
        tP = m.ps("tP", [P, 512])
        tO = m.ps("tO", [P, 512])
        pO = m.ps("pO", [P, 512])
        bias_in, kv_in = m.sem("bias_in"), [m.sem(f"kv_in{b}") for b in range(2)]
        prod_ready, dotted, st_turned, biased, own_scored = (
            m.sem(n) for n in ("prod_ready", "dotted", "st_turned", "biased", "own_scored"))
        maxed, negated, exped, inverted, scaled, p_turned, pT_out = (
            m.sem(n) for n in ("maxed", "negated", "exped", "inverted", "scaled", "p_turned", "pT_out"))
        own_mult, own_added, own_copied, own_turned, ownT_out, pv_ready, o_copied, o_added = (
            m.sem(n) for n in ("own_mult", "own_added", "own_copied", "own_turned", "ownT_out", "pv_ready",
                               "o_copied", "o_added"))
        selfm, sp_ticks, pe_ticks, stored = (m.sem(n) for n in ("selfm", "sp_ticks", "pe_ticks", "stored"))
        PER = 9 + DT + DT * NG + 2 * (DT - 1)

        def each_pair(eng, body):
            body(0, 0)
            body(1, 1)
            with eng.Fori(1, DB // 2) as i:
                body(i * 2, 0)
                body(i * 2 + 1, 1)

        with nc.Block() as block:
            @block.sync
            def _(sp):
                sp.dma_start(bias[:, :, :], t["sample_alibi"][0:R]).then_inc(bias_in, 16)

                def body(b, f):
                    held(sp, o_added, (b - 1) * 2, sp_ticks)
                    count = 0
                    for which in range(3):
                        for g in range(NG):
                            src = t["hs"][ds(b * DT, DT), which * QKV + g * AW:which * QKV + (g + 1) * AW]
                            sp.dma_start(row[f][:, which, g, :], src.rearrange("t (h d) -> t h d", h=H))\
                                .then_inc(kv_in[f], 16)
                            count += 1
                    for tk in range(DT):
                        src = t["hs"][ds(b * DT + tk, 1), 0:QKV]
                        sp.dma_start(qb[f][:, tk, :, :].rearrange("p g c -> p (g c)"),
                                     src.rearrange("o n -> (o n)").partition_broadcast(P)).then_inc(kv_in[f], 16)
                        count += 1
                        for g, (win, dil) in enumerate(GROUPS):
                            state = t[f"state_win{g}"]
                            old = P - tk if dil == 1 else P
                            src = state[ds(b, 1), tk:tk + dil * (old - 1) + 1:dil, :, :]
                            sp.dma_start(kv[f][0:old, tk, g, :, :], src.rearrange("o i c n -> (o i) c n"))\
                                .then_inc(kv_in[f], 16)
                            count += 1
                            if old < P:
                                for which in (1, 2):
                                    src = t["hs"][ds(b * DT, tk), which * QKV + g * AW:which * QKV + (g + 1) * AW]
                                    sp.dma_start(kv[f][old:P, tk, g, which - 1, :], src).then_inc(kv_in[f], 16)
                                    count += 1
                    assert count == PER

                each_pair(sp, body)
                sp.wait_ge(o_added, 2 * DB)
                for c in range(4):
                    sp.dma_start(t["oaT_s"][c], oT[:, c, :]).then_inc(stored, 16)
                sp.wait_ge(stored, 64)

            @block.gpsimd
            def _(pool):
                def body(b, f):
                    pool.wait_ge(kv_in[f], (b - f + 2) * (8 * PER))
                    for tk in range(DT):
                        n = b * DT + tk
                        waits(pool, dotted, n - 1)
                        pool.tensor_tensor(prod[tk % 2][:, :, :], qb[f][:, tk, :, :], kv[f][:, tk, :, 0, :],
                                           ALU.mult).then_inc(prod_ready, 1)

                each_pair(pool, body)

            @block.vector
            def _(dve):
                dve.wait_ge(bias_in, 16)

                def dots(b, f):
                    for tk in range(DT):
                        n = b * DT + tk
                        dve.wait_ge(prod_ready, n + 1)
                        if tk == 0:
                            waits(dve, st_turned, b)
                        dve.tensor_reduce(st[:, :, tk * H:(tk + 1) * H],
                                          prod[tk % 2][:, :, :].rearrange("p g (h d) -> p g h d", h=H),
                                          AX.X, ALU.add).then_inc(dotted, 1)

                def softmax(b, f):
                    dve.wait_ge(kv_in[f], (b - f + 2) * (8 * PER))
                    dve.tensor_tensor(selfp[:, :, :], row[f][:, 0, :, :], row[f][:, 1, :, :], ALU.mult)\
                        .then_inc(selfm, 1)
                    dve.wait_ge(selfm, b + 1)
                    waits(dve, own_added, b * 3)
                    dve.tensor_reduce(stat[:, 0:NG], selfp[:, :, :], AX.X, ALU.add).then_inc(own_scored, 1)
                    dve.wait_ge(own_scored, b + 1)
                    waits(dve, p_turned, b)
                    dve.tensor_scalar(sr[:, NG * P:NG * P + NG], stat[:, 0:NG], A_SCALE, None, ALU.mult)
                    dve.wait_ge(st_turned, b + 1)
                    dve.scalar_tensor_tensor(sr[:, 0:NG * P], tS[0:R, 0:NG * P], A_SCALE,
                                             bias[:, :, :].rearrange("p g k -> p (g k)"), ALU.mult, ALU.add)\
                        .then_inc(biased, 1)
                    dve.wait_ge(biased, b + 1)
                    dve.tensor_reduce(stat[:, 0:1], sr[:, :], AX.X, ALU.max).then_inc(maxed, 1)
                    dve.wait_ge(maxed, b + 1)
                    dve.tensor_scalar(stat[:, 1:2], stat[:, 0:1], -1.0, None, ALU.mult).then_inc(negated, 1)
                    dve.wait_ge(exped, b + 1)
                    dve.reciprocal(stat[:, 3:4], stat[:, 2:3]).then_inc(inverted, 1)
                    dve.wait_ge(inverted, b + 1)
                    dve.tensor_scalar(sr[:, :], sr[:, :], stat[:, 3:4], None, ALU.mult).then_inc(scaled, 1)
                    dve.wait_ge(scaled, b + 1)
                    waits(dve, own_turned, b)
                    for g in range(NG):
                        dve.tensor_scalar(own3[:, g, :], row[f][:, 2, g, :], sr[:, NG * P + g:NG * P + g + 1], None,
                                          ALU.mult).then_inc(own_mult, 1)
                    dve.wait_ge(own_mult, (b + 1) * 3)
                    dve.tensor_tensor(own[:, 0, :], own3[:, 0, :], own3[:, 1, :], ALU.add).then_inc(own_added, 1)
                    dve.wait_ge(own_added, b * 3 + 1)
                    dve.tensor_tensor(own[:, 1, :], own[:, 0, :], own3[:, 2, :], ALU.add).then_inc(own_added, 1)
                    dve.wait_ge(own_added, b * 3 + 2)
                    dve.tensor_copy(own[:, 0, :], own[:, 1, :]).then_inc(own_added, 1)

                def outputs(b, f):
                    dve.wait_ge(ownT_out, b + 1)
                    dve.wait_ge(pv_ready, b + 1)
                    for h in range(2):
                        r = slice(h * HD, (h + 1) * HD)
                        dve.tensor_tensor(oT[r, :, ds(b * DT, DT)],
                                          pO[r, 0:DT * 8].rearrange("p (k c s) -> p c k s", k=DT, c=4)[:, :, :, h],
                                          ownT[r, :].rearrange("p (k c s) -> p c k s", k=DT, c=4)[:, :, :, h],
                                          ALU.add).then_inc(o_added, 1)

                def body(b, f):
                    dots(b, f)
                    softmax(b, f)
                    outputs(b, f)

                each_pair(dve, body)

            @block.scalar
            def _(act):
                def body(b, f):
                    act.wait_ge(negated, b + 1)
                    act.activation(sr[:, :], sr[:, :], ACT.Exp, bias=stat[:, 1:2], accum_out=stat[:, 2:3])\
                        .then_inc(exped, 1)
                    act.wait_ge(p_turned, b + 1)
                    waits(act, pv_ready, b)
                    act.activation(pT[:, :, :], tP[:, 0:NG * R].rearrange("p (g r) -> p g r", g=NG), ACT.Copy)\
                        .then_inc(pT_out, 1)
                    act.wait_ge(own_turned, b + 1)
                    waits(act, o_added, b * 2)
                    act.activation(ownT[:, :], tO[:, 0:R], ACT.Copy).then_inc(ownT_out, 1)

                each_pair(act, body)

            @block.tensor
            def _(pe):
                def body(b, f):
                    pe.wait_ge(dotted, (b + 1) * DT)
                    waits(pe, biased, b)
                    for g in range(NG):
                        last = pe.transpose(tS[0:R, g * P:(g + 1) * P], st[:, g, :], ident[:, :])
                    last.then_inc(st_turned, 1)
                    pe.wait_ge(scaled, b + 1)
                    waits(pe, pT_out, b)
                    pe.sem_inc(pe_ticks, 1)
                    for g in range(NG):
                        last = pe.transpose(tP[:, g * R:(g + 1) * R], sr[:, g * P:(g + 1) * P], ident[0:R, 0:R])
                    last.then_inc(p_turned, 1)
                    pe.wait_ge(own_added, b * 3 + 3)
                    waits(pe, ownT_out, b)
                    pe.sem_inc(pe_ticks, 1)
                    pe.transpose(tO[:, 0:R], own[:, :, :].rearrange("p a d -> p (a d)"), ident[0:R, 0:R])\
                        .then_inc(own_turned, 1)
                    pe.wait_ge(pT_out, b + 1)
                    waits(pe, o_added, b * 2)
                    for tk in range(DT):
                        for c in range(4):
                            for g in range(NG):
                                last = pe.matmul(pO[:, tk * H + 2 * c:tk * H + 2 * c + 2],
                                                 kv[f][:, tk, g, 1, c * P:(c + 1) * P],
                                                 pT[:, g, tk * H + 2 * c:tk * H + 2 * c + 2],
                                                 start=g == 0, stop=g == NG - 1)
                    last.then_inc(pv_ready, 1)

                each_pair(pe, body)


def stage_sample_latent(nc, t, ident):
    with ExitStack() as ctx:
        m = Mem(nc, ctx, "slat")
        R = H * DT
        GP = 4
        NGP = NPG // GP
        table = m.sb("table", [1, DB * NPG], I32)
        ckv = [m.sb(f"ckv{b}", [P, NPG, KL]) for b in range(2)]
        kpe = [m.sb(f"kpe{b}", [P, NPG, ROPE]) for b in range(2)]
        new = [m.sb(f"new{b}", [DT, KL]) for b in range(2)]
        q64 = m.sb("q64", [NOPE, H, NS])
        qpe = m.sb("qpe", [P, H, NS])
        wuk = m.sb("wuk", [P, AW])
        wuv = m.sb("wuv", [P, AW])
        wukT = m.sb("wukT", [NOPE, H, P])
        qlat = m.sb("qlat", [P, H, NS])
        newT = m.sb("newT", [P, NS])
        newpT = m.sb("newpT", [ROPE, NS])
        mask = m.sb("mask", [DT, R])
        qc = [m.sb(f"qc{b}", [P, R]) for b in range(2)]
        qz = [m.sb(f"qz{b}", [P, GP, R]) for b in range(2)]
        nc_ = [m.sb(f"nc{b}", [P, DT]) for b in range(2)]
        np_ = [m.sb(f"np{b}", [ROPE, DT]) for b in range(2)]
        cT = [m.sb(f"cT{b}", [P, GP, P]) for b in range(2)]
        pTt = [m.sb(f"pTt{b}", [P, P]) for b in range(2)]
        sx = m.sb("sx", [P, NPG + 1, R])
        pr = m.sb("pr", [P, NPG + 1, R])
        top = m.sb("top", [P, R])
        rmax = m.sb("rmax", [R, 4])
        rmaxb = m.sb("rmaxb", [R, P])
        mb = m.sb("mb", [P, R])
        ones = m.sb("ones", [P, 1])
        psumx = m.sb("psumx", [P, R])
        ol = m.sb("ol", [R, KL])
        olT = m.sb("olT", [P, H, NS])
        obT = m.sb("obT", [P, 4, NS])
        tc_ = [m.ps(f"tc{b}", [P, 512]) for b in range(2)]
        S = m.ps("S", [P, 2, 512])
        X = m.ps("X", [P, 512])
        N = m.ps("N", [P, 512])
        OL = m.ps("OL", [P, 512])
        sems = ("loaded", "ones_set", "uk_turned", "uk_out", "ql_ready", "ql_out", "c_turned", "c_out", "s_ready",
                "sx_out", "new_out", "topped", "top_turned", "rmaxed", "rmax_wide", "mb_turned", "mb_out", "centred",
                "exped", "p_summed", "ol_ready", "inverted", "ol_scaled", "ol_turned", "olT_out", "q_laid",
                "ob_ready", "ob_out", "stored", "x_turned", "x_out", "n_ready", "zeroed", "sp_ticks", "pe_ticks")
        s = {n: m.sem(n) for n in sems}
        page_in = [m.sem(f"page_in{b}") for b in range(2)]
        HALF = NGP // 2

        def each_pair(eng, body):
            body(0, 0)
            body(1, 1)
            with eng.Fori(1, DB // 2) as i:
                body(i * 2, 0)
                body(i * 2 + 1, 1)

        with nc.Block() as block:
            @block.sync
            def _(sp):
                ld = s["loaded"]
                sp.dma_start(table[:, :], t["page_table"].rearrange("b n -> (b n)").unsqueeze(0)).then_inc(ld, 16)
                sp.dma_start(q64[:, :, :], t["qs96"][:, 0:NOPE, :].rearrange("h c n -> c h n")).then_inc(ld, 16)
                for j in range(GP):
                    sp.dma_start(qpe[j * ROPE:(j + 1) * ROPE, :, :],
                                 t["qs96"][:, NOPE:NOPE + ROPE, :].rearrange("h c n -> c h n")).then_inc(ld, 16)
                sp.dma_start(wuk[:, :], t["w_uk"].rearrange("c h d -> c (h d)")).then_inc(ld, 16)
                sp.dma_start(wuv[:, :], t["w_uv"].rearrange("c h d -> c (h d)")).then_inc(ld, 16)
                sp.dma_start(newT[:, :], t["ckvT"][:, SEQ:TOK]).then_inc(ld, 16)
                sp.dma_start(newpT[:, :], t["kpeT"][:, SEQ:TOK]).then_inc(ld, 16)
                sp.dma_start(mask[:, :], t["sample_causal"]).then_inc(ld, 16)
                sp.wait_ge(ld, 16 * 11)

                def body(b, f):
                    held(sp, s["ol_ready"], b - 1, s["sp_ticks"])
                    sp.dma_start(new[f][:, :], t["ckv_sample"][ds(b * DT, DT), :]).then_inc(page_in[f], 16)

                    def page(i):
                        at = sp.value_load(table[0:1, ds(b * NPG + i, 1)], min_val=0,
                                           max_val=t["cache_ckv"].shape[0] - 1)
                        sp.dma_start(ckv[f][:, ds(i, 1), :].rearrange("p o c -> p (o c)"),
                                     t["cache_ckv"][ds(at, 1)].rearrange("o s c -> (o s) c"))\
                            .then_inc(page_in[f], 16)
                        sp.dma_start(kpe[f][:, ds(i, 1), :].rearrange("p o c -> p (o c)"),
                                     t["cache_kpe"][ds(at, 1)].rearrange("o s c -> (o s) c"))\
                            .then_inc(page_in[f], 16)

                    with sp.Fori(0, NPG) as i:
                        page(i)

                each_pair(sp, body)
                sp.wait_ge(s["ob_out"], 2)
                for c in range(4):
                    sp.dma_start(t["obT_s"][c], obT[:, c, :]).then_inc(s["stored"], 16)
                sp.wait_ge(s["stored"], 64)

            PAGES_IN = 16 * (2 * NPG + 1)

            @block.gpsimd
            def _(pool):
                pool.memset(ones[:, :], 1.0).then_inc(s["ones_set"], 1)
                pool.memset(sx[:, NPG:NPG + 1, :], NEG).then_inc(s["ones_set"], 1)
                for f in range(2):
                    pool.memset(qz[f][:, :, :], 0.0).then_inc(s["zeroed"], 1)

            @block.scalar
            def _(act):
                act.wait_ge(s["uk_turned"], 1)
                act.activation(wukT[:, 0:4, :], tc_[0][0:NOPE, :].rearrange("p (h c) -> p h c", h=4), ACT.Copy)
                act.activation(wukT[:, 4:8, :], tc_[1][0:NOPE, :].rearrange("p (h c) -> p h c", h=4), ACT.Copy)\
                    .then_inc(s["uk_out"], 1)
                act.wait_ge(s["ql_ready"], 1)
                act.activation(qlat[:, :, :], S[:, 0, 0:H * NS].rearrange("p (h k) -> p h k", h=H), ACT.Copy)\
                    .then_inc(s["ql_out"], 1)

                def body(b, f):
                    for k in range(NGP):
                        n = b * NGP + k
                        act.wait_ge(s["c_turned"], n + 1)
                        waits(act, s["s_ready"], n - 1)
                        act.activation(cT[k % 2][:, :, :], tc_[k % 2][:, :].rearrange("p (g k) -> p g k", g=GP),
                                       ACT.Copy).then_inc(s["c_out"], 1)
                    act.wait_ge(s["top_turned"], b + 1)
                    act.wait_ge(s["mb_turned"], b + 1)
                    waits(act, s["centred"], b * 2)
                    act.activation(mb[:, :], N[:, P * 2:P * 2 + R], ACT.Copy).then_inc(s["mb_out"], 1)
                    act.wait_ge(s["centred"], b * 2 + 2)
                    waits(act, s["ol_ready"], b)
                    act.activation(pr[:, :, :], sx[:, :, :], ACT.Exp, scale=B_SCALE).then_inc(s["exped"], 1)
                    act.wait_ge(s["ol_turned"], b + 1)
                    act.activation(olT[:, :, ds(b * DT, DT)], N[:, P * 3:P * 3 + R].rearrange("p (h k) -> p h k", h=H),
                                   ACT.Copy).then_inc(s["olT_out"], 1)

                each_pair(act, body)
                act.wait_ge(s["ob_ready"], 1)
                act.activation(obT[:, :, :], X[:, 0:4 * NS].rearrange("p (c k) -> p c k", c=4), ACT.Copy)\
                    .then_inc(s["ob_out"], 2)

            @block.vector
            def _(dve):
                dve.wait_ge(s["loaded"], 16 * 11)
                dve.wait_ge(s["ones_set"], 2)
                dve.wait_ge(s["zeroed"], 2)
                dve.wait_ge(s["ql_out"], 1)

                def lay_queries(b, f):
                    waits(dve, s["n_ready"], b - 1)
                    at = ds(b * DT, DT)
                    dve.tensor_copy(qc[f][:, :].rearrange("p (h k) -> p h k", h=H), qlat[:, :, at])
                    dve.tensor_copy(nc_[f][:, :], newT[:, at])
                    dve.tensor_copy(np_[f][:, :], newpT[:, at])
                    for j in range(GP):
                        r = slice(j * ROPE, (j + 1) * ROPE)
                        last = dve.tensor_copy(qz[f][r, j, :].rearrange("p (h k) -> p h k", h=H), qpe[r, :, at])
                    last.then_inc(s["q_laid"], 1)

                def body(b, f):
                    lay_queries(b, f)
                    for k in range(NGP):
                        n = b * NGP + k
                        dve.wait_ge(s["x_turned"], n + 1)
                        waits(dve, s["s_ready"], n - 1)
                        dve.tensor_copy(pTt[k % 2][:, :], X[:, (k % 2) * P:(k % 2) * P + P]).then_inc(s["x_out"], 1)
                    waits(dve, s["exped"], b)
                    dve.wait_ge(s["s_ready"], (b + 1) * NGP)
                    for k in range(2):
                        dve.tensor_copy(sx[:, k * 16:(k + 1) * 16, :], S[:, k, :].rearrange("p (g r) -> p g r", g=16))\
                            .then_inc(s["sx_out"], 1)
                    dve.wait_ge(s["n_ready"], b + 1)
                    dve.tensor_tensor(sx[0:DT, NPG, :], N[0:DT, 0:R], mask[:, :], ALU.add).then_inc(s["new_out"], 1)
                    dve.wait_ge(s["sx_out"], (b + 1) * 2)
                    dve.wait_ge(s["new_out"], b + 1)
                    dve.tensor_reduce(top[:, :], sx[:, :, :].rearrange("p g r -> p r g"), AX.X, ALU.max)\
                        .then_inc(s["topped"], 1)
                    dve.wait_ge(s["top_turned"], b + 1)
                    dve.tensor_reduce(rmax[:, 0:1], N[0:R, P:2 * P], AX.X, ALU.max).then_inc(s["rmaxed"], 1)
                    dve.wait_ge(s["rmaxed"], b + 1)
                    dve.tensor_copy(rmaxb[:, :], rmax[:, 0:1].to_broadcast([R, P])).then_inc(s["rmax_wide"], 1)
                    dve.wait_ge(s["mb_out"], b + 1)
                    dve.tensor_tensor(sx[:, 0:NPG, :], sx[:, 0:NPG, :],
                                      mb[:, :].unsqueeze(1).to_broadcast([P, NPG, R]), ALU.subtract)\
                        .then_inc(s["centred"], 1)
                    dve.tensor_tensor(sx[0:DT, NPG, :], sx[0:DT, NPG, :], mb[0:DT, :], ALU.subtract)\
                        .then_inc(s["centred"], 1)
                    dve.wait_ge(s["exped"], b + 1)
                    dve.tensor_reduce(psumx[:, :], pr[:, :, :].rearrange("p g r -> p r g"), AX.X, ALU.add)\
                        .then_inc(s["p_summed"], 1)
                    dve.wait_ge(s["ol_ready"], b + 1)
                    dve.reciprocal(rmax[:, 1:2], OL[0:R, KL:KL + 1]).then_inc(s["inverted"], 1)
                    dve.wait_ge(s["inverted"], b + 1)
                    dve.tensor_scalar(ol[:, :], OL[0:R, 0:KL], rmax[:, 1:2], None, ALU.mult)\
                        .then_inc(s["ol_scaled"], 1)

                each_pair(dve, body)

            @block.tensor
            def _(pe):
                pe.wait_ge(s["loaded"], 16 * 11)
                pe.wait_ge(s["ones_set"], 2)
                for h in range(H):
                    last = pe.transpose(tc_[h // 4][0:NOPE, (h % 4) * P:(h % 4 + 1) * P],
                                        wuk[:, h * NOPE:(h + 1) * NOPE], ident[:, :])
                last.then_inc(s["uk_turned"], 1)
                pe.wait_ge(s["uk_out"], 1)
                for h in range(H):
                    last = pe.matmul(S[:, 0, h * NS:(h + 1) * NS], wukT[:, h, :], q64[:, h, :], start=True, stop=True)
                last.then_inc(s["ql_ready"], 1)
                pe.wait_ge(s["ql_out"], 1)

                def body(b, f):
                    pe.wait_ge(page_in[f], (b - f + 2) * (PAGES_IN // 2))
                    pe.wait_ge(s["q_laid"], b + 1)

                    def turns(k):
                        n = b * NGP + k
                        waits(pe, s["c_out"], n - 1)
                        for j in range(GP):
                            last = pe.transpose(tc_[k % 2][:, j * P:(j + 1) * P], ckv[f][:, k * GP + j, :],
                                                ident[:, :])
                        last.then_inc(s["c_turned"], 1)
                        waits(pe, s["x_out"], n)
                        pe.transpose(X[:, (k % 2) * P:(k % 2) * P + P],
                                     kpe[f][:, k * GP:(k + 1) * GP, :].rearrange("p g r -> p (g r)"), ident[:, :])\
                            .then_inc(s["x_turned"], 1)

                    def scores(k):
                        n = b * NGP + k
                        pe.wait_ge(s["c_out"], n + 1)
                        pe.wait_ge(s["x_out"], n + 1)
                        if k == 0:
                            waits(pe, s["sx_out"], b * 2)
                        bank, at = k // HALF, (k % HALF) * GP * R
                        pe.matmul(S[:, bank, at:at + GP * R], pTt[k % 2][:, :],
                                  qz[f][:, :, :].rearrange("p g r -> p (g r)"), start=True, stop=False,
                                  skip_group_check=True)
                        for j in range(GP):
                            last = pe.matmul(S[:, bank, at + j * R:at + (j + 1) * R], cT[k % 2][:, j, :], qc[f][:, :],
                                             start=False, stop=True, skip_group_check=True)
                        last.then_inc(s["s_ready"], 1)

                    for k in range(NGP + 1):
                        if k < NGP:
                            turns(k)
                        if k:
                            scores(k - 1)
                    waits(pe, s["olT_out"], b)
                    pe.matmul(N[0:DT, 0:R], nc_[f][:, :], qc[f][:, :], start=True, stop=False)
                    pe.matmul(N[0:DT, 0:R], np_[f][:, :], qz[f][0:ROPE, 0, :], start=False, stop=True)\
                        .then_inc(s["n_ready"], 1)
                    pe.wait_ge(s["topped"], b + 1)
                    pe.transpose(N[0:R, P:2 * P], top[:, :], ident[:, :]).then_inc(s["top_turned"], 1)
                    pe.wait_ge(s["rmax_wide"], b + 1)
                    pe.sem_inc(s["pe_ticks"], 1)
                    pe.transpose(N[:, 2 * P:2 * P + R], rmaxb[:, :], ident[0:R, 0:R]).then_inc(s["mb_turned"], 1)
                    pe.wait_ge(s["exped"], b + 1)
                    waits(pe, s["ol_scaled"], b)
                    for k in range(NPG):
                        pe.matmul(OL[0:R, 0:KL], pr[:, k, :], ckv[f][:, k, :], start=k == 0, stop=False)
                    pe.matmul(OL[0:R, 0:KL], pr[0:DT, NPG, :], new[f][:, :], start=False, stop=True)
                    pe.wait_ge(s["p_summed"], b + 1)
                    pe.matmul(OL[0:R, KL:KL + 1], psumx[:, :], ones[:, :], start=True, stop=True)\
                        .then_inc(s["ol_ready"], 1)
                    pe.wait_ge(s["ol_scaled"], b + 1)
                    pe.sem_inc(s["pe_ticks"], 1)
                    pe.transpose(N[:, 3 * P:3 * P + R], ol[:, :], ident[0:R, 0:R]).then_inc(s["ol_turned"], 1)

                each_pair(pe, body)
                pe.wait_ge(s["olT_out"], DB)
                for h in range(H):
                    r = slice((h % 2) * HD, (h % 2 + 1) * HD)
                    last = pe.matmul(X[r, (h // 2) * NS:(h // 2 + 1) * NS], wuv[:, h * HD:(h + 1) * HD], olT[:, h, :],
                                     start=True, stop=True)
                last.then_inc(s["ob_ready"], 1)


def start_window_copies(nc, t, copied):
    with nc.Block() as block:
        @block.gpsimd
        def _(pool):
            for g, (win, _) in enumerate(GROUPS):
                for b in range(DB):
                    pool.dma_start(t[f"win{g}_sample"][b, 0:win - DT].rearrange("i c n -> i (c n)"),
                                   t[f"state_win{g}"][b, DT:win].rearrange("i c n -> i (c n)")).then_inc(copied, 16)


def stage_join(nc, t, ident):
    with ExitStack() as ctx:
        m = Mem(nc, ctx, "join")
        oa = [m.sb(f"oa{b}", [P, NG, 4, REC]) for b in range(2)]
        ob = [m.sb(f"ob{b}", [P, 2, H, RECB]) for b in range(2)]
        gz = [m.sb(f"gz{b}", [P, 8, P]) for b in range(2)]
        us = m.sb("us", [P, 3, 8, NS])
        big = m.sb("big", [P, NG * H, HD])
        part = m.sb("part", [P, H, HD])
        mx = m.sb("mx", [P, 2, H])
        wt = m.sb("wt", [P, 2, NG * H])
        sl = m.sb("sl", [P, NG * H])
        sums = m.sb("sums", [P, 2, H])
        nat = [m.sb(f"nat{b}", [P, 2, AW]) for b in range(2)]
        uT = [m.sb(f"uT{b}", [P, 8, P]) for b in range(2)]
        tp = [m.ps(f"tp{b}", [P, 8, P]) for b in range(2)]
        oin = [m.sem(f"in{b}") for b in range(2)]
        us_in, us_out, step, expin, exped, nat_ready, tp_ready, u_ready, sp_ticks = (
            m.sem(n) for n in ("us_in", "us_out", "step", "expin", "exped", "nat_ready", "tp_ready", "u_ready",
                               "sp_ticks"))
        stored = [m.sem(f"stored{b}") for b in range(2)]
        us_stored = m.sem("us_stored")
        HALF = NT // 2
        STEPS = {1: 11, 2: 16}
        EXPS = {1: 1, 2: 2}

        def each_tile(eng, body):
            body(0, 0, 1)
            body(1, 1, 1)
            with eng.Fori(1, HALF // 2) as i:
                body(i * 2, 0, 1)
                body(i * 2 + 1, 1, 1)
            with eng.Fori(HALF // 2, HALF) as i:
                body(i * 2, 0, 2)
                body(i * 2 + 1, 1, 2)

        def before(i, chunks, per):
            return i * per[1] if chunks == 1 else (i - HALF) * per[2] + HALF * per[1]

        with nc.Block() as block:
            @block.sync
            def _(sp):
                for k, name in enumerate(("oaT_s", "obT_s")):
                    sp.dma_start(us[:, 0, 4 * k:4 * k + 4, :], t[name].rearrange("c p n -> p c n")).then_inc(us_in, 16)
                sp.dma_start(us[:, 1, :, :], t["gates"][0:8, :, SEQ:TOK].rearrange("k p n -> p k n")).then_inc(us_in, 16)

                def body(i, b, chunks):
                    held(sp, u_ready, i - 1, sp_ticks)
                    rows = ds(i * P, P)
                    sp.dma_start(oa[b][:, :, :, :], t["oa"][rows]).then_inc(oin[b], 16)
                    sp.dma_start(ob[b][:, 0:chunks, :, :], t["ob"][rows, 0:chunks]).then_inc(oin[b], 16)
                    sp.dma_start(gz[b][:, :, :], t["gates"][0:8, :, rows].rearrange("k p n -> p k n"))\
                        .then_inc(oin[b], 16)

                each_tile(sp, body)
                sp.wait_ge(us_out, 1)
                sp.dma_start(t["uT"][:, :, SEQ:TOK].rearrange("k p n -> p k n"), us[:, 2, :, :]).then_inc(us_stored, 16)
                sp.wait_ge(us_stored, 16)

            @block.gpsimd
            def _(pool):
                def body(i, b, chunks):
                    pool.wait_ge(u_ready, i + 1)
                    pool.dma_start(t["uT"][:, :, ds(i * P, P)].rearrange("k p n -> p k n"), uT[b][:, :, :])\
                        .then_inc(stored[b], 16)

                each_tile(pool, body)
                for b in range(2):
                    pool.wait_ge(stored[b], 16 * HALF)

            @block.scalar
            def _(act):
                def body(i, b, chunks):
                    for k in range(chunks):
                        n = before(i, chunks, EXPS) + k
                        act.wait_ge(expin, n + 1)
                        width = NG * H if k == 0 else 2 * H
                        act.activation(wt[:, k, 0:width], wt[:, k, 0:width], ACT.Exp).then_inc(exped, 1)

                each_tile(act, body)

            @block.vector
            def _(dve):
                dve.wait_ge(us_in, 48)
                dve.tensor_tensor(us[:, 2, :, :], us[:, 0, :, :], us[:, 1, :, :], ALU.mult).then_inc(us_out, 1)

                def body(i, b, chunks):
                    first = before(i, chunks, STEPS)
                    count = [0]

                    def then(ins):
                        count[0] += 1
                        ins.then_inc(step, 1)
                        dve.wait_ge(step, first + count[0])

                    def join(k, groups, o, sums_of, maxima, out):
                        def heads(ap):
                            return ap.rearrange("p (c s) -> p c s", s=2) if groups == NG else ap

                        w3 = [heads(wt[:, k, g * H:(g + 1) * H]) for g in range(groups)]
                        s3 = [heads(sl[:, g * H:(g + 1) * H]) for g in range(groups)]
                        top = heads(mx[:, k, :])
                        then(dve.tensor_tensor(top, maxima[0], maxima[1], ALU.max))
                        if groups == 3:
                            then(dve.tensor_tensor(top, top, maxima[2], ALU.max))
                        for g in range(groups):
                            last = dve.tensor_tensor(w3[g], maxima[g], top, ALU.subtract)
                        last.then_inc(expin, 1)
                        dve.wait_ge(exped, before(i, chunks, EXPS) + k + 1)
                        for g in range(groups):
                            last = dve.tensor_tensor(s3[g], w3[g], sums_of[g], ALU.mult)
                        then(last)
                        then(dve.tensor_reduce(sums[:, k, :], sl[:, 0:groups * H].rearrange("p (g h) -> p h g", h=H),
                                               AX.X, ALU.add))
                        then(dve.reciprocal(sums[:, k, :], sums[:, k, :]))
                        for g in range(groups):
                            last = dve.tensor_tensor(w3[g], w3[g], heads(sums[:, k, :]), ALU.mult)
                        then(last)
                        o3 = big[:, 0:groups * H, :]
                        wide = wt[:, k, 0:groups * H].unsqueeze(2).to_broadcast([P, groups * H, HD])
                        if groups == NG:
                            split = dict(s=2)
                            then(dve.tensor_tensor(o3.rearrange("p (c s) d -> p c s d", **split), o,
                                                   wide.rearrange("p (c s) d -> p c s d", **split), ALU.mult))
                        else:
                            then(dve.tensor_tensor(o3, o, wide, ALU.mult))
                        if groups == 3:
                            then(dve.tensor_tensor(part[:, :, :], o3[:, 0:H, :], o3[:, H:2 * H, :], ALU.add))
                            then(dve.tensor_tensor(out, part[:, :, :], o3[:, 2 * H:3 * H, :], ALU.add))
                        else:
                            then(dve.tensor_tensor(out, o3[:, 0:H, :], o3[:, H:2 * H, :], ALU.add))

                    dve.wait_ge(oin[b], (i - b) * 24 + 48)
                    waits(dve, tp_ready, i - 1)
                    na = nat[b][:, 0, :].rearrange("p (h d) -> p h d", h=H)
                    nb_ = nat[b][:, 1, :].rearrange("p (h d) -> p h d", h=H)
                    rec = oa[b][:, :, :, :]
                    join(0, NG, rec[:, :, :, 0:2 * HD].rearrange("p g c (s d) -> p (g c) s d", s=2),
                         [rec[:, g, :, 2 * HD:2 * HD + 2] for g in range(NG)],
                         [rec[:, g, :, 2 * HD + 2:REC] for g in range(NG)], na)
                    if chunks == 2:
                        join(1, 2, ob[b][:, :, :, 0:HD].rearrange("p c h d -> p (c h) d"),
                             [ob[b][:, c, :, HD] for c in range(2)], [ob[b][:, c, :, HD + 1] for c in range(2)], nb_)
                    else:
                        then(dve.reciprocal(sums[:, 1, :], ob[b][:, 0, :, HD]))
                        then(dve.tensor_tensor(nb_, ob[b][:, 0, :, 0:HD],
                                               sums[:, 1, :].unsqueeze(2).to_broadcast([P, H, HD]), ALU.mult))
                    dve.sem_inc(nat_ready, 1)
                    assert count[0] == STEPS[chunks], count
                    dve.wait_ge(tp_ready, i + 1)
                    waits(dve, stored[b], (i - b) * 8)
                    dve.tensor_tensor(uT[b][:, :, :], tp[b][:, :, :], gz[b][:, :, :], ALU.mult).then_inc(u_ready, 1)

                each_tile(dve, body)

            @block.tensor
            def _(pe):
                def body(i, b, chunks):
                    pe.wait_ge(nat_ready, i + 1)
                    waits(pe, u_ready, i - 1)
                    for c in range(8):
                        last = pe.transpose(tp[b][:, c, :], nat[b][:, c // 4, (c % 4) * P:(c % 4 + 1) * P], ident[:, :])
                    last.then_inc(tp_ready, 1)

                each_tile(pe, body)


def stage_project(nc, t):
    with ExitStack() as ctx:
        m = Mem(nc, ctx, "proj")
        wraw = [m.sb(f"wraw{b}", [P, D]) for b in range(2)]
        w = [m.sb(f"w_{h}", [P, 8, D], F32R) for h in ("hi", "lo")]
        ur = m.sb("ur", [P, 8, 512])
        u = [m.sb(f"u_{h}", [P, 8, 512], F32R) for h in ("hi", "lo")]
        gm = [m.sb(f"gm{b}", [P, 2, 512]) for b in range(2)]
        ga = [m.sb(f"ga{b}", [P, 2, 512]) for b in range(2)]
        mo = [m.sb(f"mo{b}", [P, 512]) for b in range(2)]
        pr = m.ps("pr", [P, 4, 512])
        w_in = [m.sem(f"w_in{b}") for b in range(2)]
        gm_in = [m.sem(f"gm_in{b}") for b in range(2)]
        stored = [m.sem(f"stored{b}") for b in range(2)]
        w_hi, w_lo, u_in, u_hi, u_lo, pr_ready, gated, m_ready, sp_ticks = (
            m.sem(n) for n in ("w_hi", "w_lo", "u_in", "u_hi", "u_lo", "pr_ready", "gated", "m_ready", "sp_ticks"))
        NB = SEQ // 512

        def each_block(eng, body):
            body(0, slice(SEQ, TOK), NS)
            with eng.Fori(0, NB) as i:
                body(i + 1, ds(i * 512, 512), 512)

        with nc.Block() as block:
            @block.sync
            def _(sp):
                for c in range(8):
                    waits(sp, w_lo, c - 1)
                    src = t["w_proj_a"] if c < 4 else t["w_proj_b"]
                    sp.dma_start(wraw[c % 2][:, :], src[(c % 4) * P:(c % 4 + 1) * P, :]).then_inc(w_in[c % 2], 16)

                def body(n, at, width):
                    held(sp, u_lo, n, sp_ticks)
                    sp.dma_start(ur[:, :, 0:width], t["uT"][:, :, at].rearrange("k p n -> p k n")).then_inc(u_in, 16)
                    for c in range(8):
                        held(sp, gated, n * 8 + c - 1, sp_ticks)
                        sp.dma_start(gm[c % 2][:, :, 0:width],
                                     t["gates"][8 + c:24:8, :, at].rearrange("k p n -> p k n")).then_inc(gm_in[c % 2], 16)

                each_block(sp, body)

            @block.gpsimd
            def _(pool):
                def body(n, at, width):
                    for c in range(8):
                        pool.wait_ge(gated, n * 8 + c + 1)
                        waits(pool, stored[c % 2], (n * 4 + c // 2) * 16)
                        pool.tensor_tensor(mo[c % 2][:, 0:width], ga[c % 2][:, 0, 0:width], ga[c % 2][:, 1, 0:width],
                                           ALU.add).then_inc(m_ready, 1)
                        pool.wait_ge(m_ready, n * 8 + c + 1)
                        pool.dma_start(t["mT"][c, :, at], mo[c % 2][:, 0:width]).then_inc(stored[c % 2], 16)

                each_block(pool, body)
                for b in range(2):
                    pool.wait_ge(stored[b], 16 * 4 * (NB + 1))

            @block.scalar
            def _(act):
                for c in range(8):
                    act.wait_ge(w_in[c % 2], 16 * (c // 2 + 1))
                    act.activation(w[0][:, c, :], wraw[c % 2][:, :], ACT.Copy).then_inc(w_hi, 1)

                def body(n, at, width):
                    act.wait_ge(u_in, n * 16 + 16)
                    waits(act, pr_ready, n * 8)
                    act.activation(u[0][:, :, 0:width], ur[:, :, 0:width], ACT.Copy).then_inc(u_hi, 1)

                each_block(act, body)

            @block.vector
            def _(dve):
                for c in range(8):
                    dve.wait_ge(w_hi, c + 1)
                    dve.tensor_tensor(w[1][:, c, :], wraw[c % 2][:, :], w[0][:, c, :].bitcast(F32), ALU.subtract)\
                        .then_inc(w_lo, 1)

                def body(n, at, width):
                    dve.wait_ge(u_hi, n + 1)
                    dve.tensor_tensor(u[1][:, :, 0:width], ur[:, :, 0:width], u[0][:, :, 0:width].bitcast(F32),
                                      ALU.subtract).then_inc(u_lo, 1)
                    for c in range(8):
                        b = c % 2
                        dve.wait_ge(pr_ready, n * 8 + c + 1)
                        dve.wait_ge(gm_in[b], (n * 4 + c // 2 + 1) * 16)
                        waits(dve, m_ready, n * 8 + c - 1)
                        for k in range(2):
                            last = dve.tensor_tensor(ga[b][:, k, 0:width], pr[:, 2 * b + k, 0:width],
                                                     gm[b][:, k, 0:width], ALU.mult)
                        last.then_inc(gated, 1)

                each_block(dve, body)

            @block.tensor
            def _(pe):
                pe.wait_ge(w_lo, 8)

                def body(n, at, width):
                    pe.wait_ge(u_lo, n + 1)
                    for c in range(8):
                        waits(pe, gated, n * 8 + c - 1)
                        for k in range(2):
                            for j in range(4):
                                last = split_matmul(pe, pr[:, 2 * (c % 2) + k, 0:width],
                                                    [w[h][:, 4 * k + j, c * P:(c + 1) * P] for h in range(2)],
                                                    [u[h][:, 4 * k + j, 0:width] for h in range(2)], j == 0, j == 3)
                        last.then_inc(pr_ready, 1)

                each_block(pe, body)


def stage_output(nc, t, copied):
    with ExitStack() as ctx:
        m = Mem(nc, ctx, "out")
        wraw = [m.sb(f"wraw{b}", [P, D]) for b in range(2)]
        w = [m.sb(f"w_{h}", [P, KC, D], F32R) for h in ("hi", "lo")]
        mr = [m.sb(f"mr{b}", [P, KC, P]) for b in range(2)]
        mm = [[m.sb(f"m{b}_{h}", [P, KC, P], F32R) for h in ("hi", "lo")] for b in range(2)]
        x = [m.sb(f"x{b}", [P, D]) for b in range(2)]
        y = [m.sb(f"y{b}", [P, D]) for b in range(2)]
        yn = [m.sb(f"yn{b}", [P, D]) for b in range(2)]
        junk = m.sb("junk", [P, D])
        g = m.sb("g_rows", [P, D])
        stat = [m.sb(f"stat{b}", [P, 3]) for b in range(2)]
        eps = m.sb("eps", [P, 1])
        py = [m.ps(f"py{b}", [P, D]) for b in range(2)]
        w_in = [m.sem(f"w_in{b}") for b in range(2)]
        t_in = [m.sem(f"t_in{b}") for b in range(2)]
        stored = [m.sem(f"stored{b}") for b in range(2)]
        g_in, eps_set, w_hi, w_lo, m_hi, m_lo, ready, squared, rooted, inverted, normed, y_ready, late, sp_ticks = (
            m.sem(n) for n in ("g_in", "eps_set", "w_hi", "w_lo", "m_hi", "m_lo", "ready", "squared", "rooted",
                               "inverted", "normed", "y_ready", "late", "sp_ticks"))

        def each_tile(eng, body):
            for n in range(2):
                body(n, n, P, ds(n * P, P))
            with eng.Fori(1, NT // 2) as i:
                for b in range(2):
                    body(i * 2 + b, b, P, ds((i * 2 + b) * P, P))
            body(NT, 0, NS, slice(SEQ, TOK))

        with nc.Block() as block:
            @block.sync
            def _(sp):
                for gi, (win, _) in enumerate(GROUPS):
                    for which in (1, 2):
                        sp.dma_start(t[f"win{gi}_sample"][:, win - DT:win, which - 1, :],
                                     t["hs"][:, which * QKV + gi * AW:which * QKV + (gi + 1) * AW]
                                     .rearrange("(b k) n -> b k n", b=DB)).then_inc(late, 16)
                sp.dma_start(g[:, :], t["g_post"].partition_broadcast(P)).then_inc(g_in, 16)
                for c in range(KC):
                    waits(sp, w_lo, c - 1)
                    sp.dma_start(wraw[c % 2][:, :], t["w_out"][c * P:(c + 1) * P, :]).then_inc(w_in[c % 2], 16)

                def body(n, b, rows, at):
                    held(sp, y_ready, n - 1, sp_ticks)
                    sp.dma_start(mr[b][:, :, 0:rows], t["mT"][:, :, at].rearrange("k p n -> p k n")).then_inc(t_in[b], 16)
                    src = t["x_sample"] if rows == NS else t["x_prompt"][at, :]
                    sp.dma_start(x[b][0:rows, :], src).then_inc(t_in[b], 16)

                each_tile(sp, body)
                sp.wait_ge(late, 16 * 6)
                sp.wait_ge(copied, 16 * NG * DB)

            @block.gpsimd
            def _(pool):
                def body(n, b, rows, at):
                    pool.wait_ge(y_ready, n + 1)
                    dst = t["y_sample"] if rows == NS else t["y_prompt"][at, :]
                    pool.dma_start(dst, y[b][0:rows, :]).then_inc(stored[b], 16)

                each_tile(pool, body)
                pool.wait_ge(stored[0], 16 * 9)
                pool.wait_ge(stored[1], 16 * 8)

            @block.scalar
            def _(act):
                for c in range(KC):
                    act.wait_ge(w_in[c % 2], 16 * (c // 2 + 1))
                    act.activation(w[0][:, c, :], wraw[c % 2][:, :], ACT.Copy).then_inc(w_hi, 1)
                act.wait_ge(eps_set, 1)

                def high(n, b, rows):
                    act.wait_ge(t_in[b], (n - b) * 16 + 32)
                    waits(act, ready, n - 1)
                    act.activation(mm[b][0][:, :, 0:rows], mr[b][:, :, 0:rows], ACT.Copy).then_inc(m_hi, 1)

                def body(n, b, rows, at):
                    high(n, b, rows)
                    r = slice(0, rows)
                    act.wait_ge(ready, n + 1)
                    waits(act, inverted, n - 1)
                    waits(act, squared, n)
                    act.activation(junk[r, :], py[b][r, :], ACT.Square, accum_out=stat[b][r, 0:1]).then_inc(squared, 1)
                    act.wait_ge(squared, n + 1)
                    act.activation(stat[b][r, 1:2], stat[b][r, 0:1], ACT.Sqrt, bias=eps[r, :], scale=1.0 / D)\
                        .then_inc(rooted, 1)

                each_tile(act, body)

            @block.vector
            def _(dve):
                dve.memset(eps[:, :], EPS).then_inc(eps_set, 1)
                for c in range(KC):
                    dve.wait_ge(w_hi, c + 1)
                    dve.tensor_tensor(w[1][:, c, :], wraw[c % 2][:, :], w[0][:, c, :].bitcast(F32), ALU.subtract)\
                        .then_inc(w_lo, 1)
                dve.wait_ge(g_in, 16)

                def body(n, b, rows, at):
                    r = slice(0, rows)
                    dve.wait_ge(m_hi, n + 1)
                    dve.tensor_tensor(mm[b][1][:, :, 0:rows], mr[b][:, :, 0:rows],
                                      mm[b][0][:, :, 0:rows].bitcast(F32), ALU.subtract).then_inc(m_lo, 1)
                    dve.wait_ge(rooted, n + 1)
                    dve.reciprocal(stat[b][r, 2:3], stat[b][r, 1:2]).then_inc(inverted, 1)
                    dve.wait_ge(inverted, n + 1)
                    dve.scalar_tensor_tensor(yn[b][r, :], py[b][r, :], stat[b][r, 2:3], g[r, :], ALU.mult, ALU.mult)\
                        .then_inc(normed, 1)
                    dve.wait_ge(normed, n + 1)
                    waits(dve, stored[b], (n - b) * 8)
                    dve.tensor_tensor(y[b][r, :], yn[b][r, :], x[b][r, :], ALU.add).then_inc(y_ready, 1)

                each_tile(dve, body)

            @block.tensor
            def _(pe):
                pe.wait_ge(w_lo, KC)

                def body(n, b, rows, at):
                    pe.wait_ge(m_lo, n + 1)
                    waits(pe, normed, n - 1)
                    for half in range(2):
                        cols = slice(half * 512, (half + 1) * 512)
                        for c in range(KC):
                            last = split_matmul(pe, py[b][0:rows, cols], [mm[b][h][:, c, 0:rows] for h in range(2)],
                                                [w[h][:, c, cols] for h in range(2)], c == 0, c == KC - 1)
                    last.then_inc(ready, 1)

                each_tile(pe, body)


def hybrid_step(nc, t):
    t["cqT"] = nc.dram_tensor("scr_cqT", [QL // P, P, TOK], F32).ap()
    t["ckvT"] = nc.dram_tensor("scr_ckvT", [P, TOK], F32).ap()
    t["kpeT"] = nc.dram_tensor("scr_kpeT", [ROPE, TOK], F32).ap()
    t["hs"] = nc.dram_tensor("scr_hs", [NS, 3 * QKV], F32).ap()
    t["oa"] = nc.dram_tensor("scr_oa", [SEQ, NG, 4, REC], F32).ap()
    t["gates"] = nc.dram_tensor("scr_gates", [24, P, TOK], F32).ap()
    t["qs96"] = nc.dram_tensor("scr_qs96", [H, NOPE + ROPE, NS], F32).ap()
    t["ob"] = nc.dram_tensor("scr_ob", [SEQ, 2, H, RECB], F32).ap()
    t["oaT_s"] = nc.dram_tensor("scr_oaT_s", [4, P, NS], F32).ap()
    t["obT_s"] = nc.dram_tensor("scr_obT_s", [4, P, NS], F32).ap()
    t["uT"] = nc.dram_tensor("scr_uT", [8, P, TOK], F32).ap()
    t["mT"] = nc.dram_tensor("scr_mT", [KC, P, TOK], F32).ap()
    with ExitStack() as whole:
        run_stages(nc, t, whole.enter_context(nc.semaphore("windows_copied")))


def run_stages(nc, t, copied):
    Mem.spent.clear()
    start_window_copies(nc, t, copied)
    with ExitStack() as ctx:
        m = Mem(nc, ctx, "all")
        ident = m.sb("ident", [P, P])
        xs = [m.sb(f"xs_{h}", [P, KC, NS], F32R) for h in ("hi", "lo")]
        xT = [m.sb(f"xT_{h}", [P, KC, SEQ], F32R) for h in ("hi", "lo")]
        stage_norm(nc, t, xT, xs, ident)
        stage_latents(nc, t, xT, xs, ident)
        stage_dilated(nc, t, xT, xs, ident)
        stage_gates(nc, t, xT, xs)
    with ExitStack() as ctx:
        m = Mem(nc, ctx, "late")
        ident = m.sb("ident", [P, P])
        with nc.Block() as block, nc.semaphore("late_ident_in") as ident_in:
            @block.sync
            def _(sp):
                sp.dma_start(ident[:, :], t["ident"]).then_inc(ident_in, 16)
                sp.wait_ge(ident_in, 16)
        stage_latent_attn(nc, t, ident)
        clear_semaphores(nc)
        stage_sample_dilated(nc, t, ident)
        stage_sample_latent(nc, t, ident)
        stage_join(nc, t, ident)
        stage_project(nc, t)
        stage_output(nc, t, copied)


def _constants():
    import numpy as np

    f = np.float32
    n = NG * H
    slopes = np.exp2(f(-8.0) * np.arange(1, n + 1, dtype=f) / f(n)).astype(f).reshape(NG, H)
    a = np.arange(P)[:, None]
    c = np.arange(2 * P)[None, :]
    delta = a + P - c
    valid = (delta >= 0) & (delta <= P)
    bias = np.empty((NG, H, P, 2 * P), f)
    for g, (_, dil) in enumerate(GROUPS):
        for h in range(H):
            bias[g, h] = np.where(valid, -slopes[g, h] * (dil * delta).astype(f), f(NEG))
    causal = np.where(np.arange(P)[None, :] <= a, f(0), f(NEG)).astype(f)
    inv = f(10000.0) ** (-np.arange(0, ROPE, 2, dtype=f) / f(ROPE))
    pos = np.concatenate([np.arange(SEQ), np.tile(PAST + np.arange(DT), DB)]).astype(f)
    ang = (pos[:, None] * inv[None, :]).astype(f)
    cos, sin = np.cos(ang).astype(f), np.sin(ang).astype(f)
    rows = np.stack([np.concatenate([cos, cos], 1), np.concatenate([-sin, sin], 1)], 1)
    cols = np.concatenate([rows[:, 0].T, rows[:, 1].T], 0)
    dist = np.stack([dil * (P - np.arange(P)) for _, dil in GROUPS]).astype(f)
    sample_alibi = np.stack([-slopes[:, h, None] * dist for h in range(H)] * DT)
    sample_causal = np.where(np.arange(DT)[:, None] <= np.tile(np.arange(DT), H)[None, :], f(0), f(NEG))
    return {
        "ident": np.eye(P, dtype=f),
        "alibi": np.ascontiguousarray(bias.transpose(0, 2, 1, 3)),
        "causal": causal,
        "rope_rows": np.ascontiguousarray(rows),
        "rope_cols": np.ascontiguousarray(cols),
        "sample_alibi": sample_alibi.astype(f),
        "sample_causal": sample_causal.astype(f),
    }


_CONSTS = ["ident", "alibi", "causal", "rope_rows", "rope_cols", "sample_alibi", "sample_causal"]
_INS = ["x_prompt", "x_sample", "cache_ckv", "cache_kpe", "state_win0", "state_win1", "state_win2", "page_table",
        "w_in", "w_uq", "w_uk", "w_uv", "w_proj_a", "w_proj_b", "w_out", "g_pre", "g_post", "g_q", "g_kv"]
_FLAT = {
    "x_prompt": "a s d -> (a s) d", "x_sample": "b t d -> (b t) d", "cache_ckv": "a n s c -> (a n) s c",
    "cache_kpe": "a n s c -> (a n) s c", "state_win0": "a b w c h d -> (a b) w c (h d)",
    "state_win1": "a b w c h d -> (a b) w c (h d)", "state_win2": "a b w c h d -> (a b) w c (h d)",
    "w_in": "a k n -> (a k) n", "w_uq": "a k n -> (a k) n", "w_uk": "a c h d -> (a c) h d",
    "w_uv": "a c h d -> (a c) h d", "w_proj_a": "a k n -> (a k) n", "w_proj_b": "a k n -> (a k) n",
    "w_out": "a k n -> (a k) n", "g_pre": "a n -> (a n)", "g_post": "a n -> (a n)", "g_q": "a n -> (a n)",
    "g_kv": "a n -> (a n)",
}
_WIN = "a b w c h d -> (a b) w c (h d)"
_OUTS = [
    ("y_prompt", (1, SEQ, D), "a s d -> (a s) d"), ("y_sample", (DB, DT, D), "b t d -> (b t) d"),
    ("ckv_prompt", (1, 1, SEQ, KL), "a b s c -> (a b s) c"), ("kpe_prompt", (1, 1, SEQ, ROPE), "a b s c -> (a b s) c"),
    ("win0_prompt", (1, 1, 128, 2, H, HD), _WIN), ("win1_prompt", (1, 1, 512, 2, H, HD), _WIN),
    ("win2_prompt", (1, 1, 2048, 2, H, HD), _WIN),
    ("ckv_sample", (1, DB, DT, KL), "a b t c -> (a b t) c"), ("kpe_sample", (1, DB, DT, ROPE), "a b t c -> (a b t) c"),
    ("win0_sample", (1, DB, 128, 2, H, HD), _WIN), ("win1_sample", (1, DB, 512, 2, H, HD), _WIN),
    ("win2_sample", (1, DB, 2048, 2, H, HD), _WIN),
]


def kernel(**inputs):
    import numpy as _np
    import concourse.bacc as _bacc
    from concourse import mybir as _mybir
    from concourse.bass_utils import run_bass_kernel_spmd as _run

    nc = _bacc.Bacc("TRN2", target_bir_lowering=False, num_devices=1)
    arrays, t = {}, {}
    consts = _constants()
    for name in _INS + _CONSTS:
        a = _np.ascontiguousarray(inputs[name] if name in inputs else consts[name])
        arrays[f"in_{name}"] = a
        ap = nc.dram_tensor(f"in_{name}", a.shape, _mybir.dt.from_np(a.dtype), kind="ExternalInput").ap()
        t[name] = ap.rearrange(_FLAT[name]) if name in _FLAT else ap
    for name, shape, flat in _OUTS:
        ap = nc.dram_tensor(f"out_{name}", shape, _mybir.dt.float32, kind="ExternalOutput").ap()
        t[name] = ap.rearrange(flat)
    hybrid_step(nc, t)
    r = _run(nc, [arrays], core_ids=[0])
    return tuple(r.results[0][f"out_{name}"] for name, _, _ in _OUTS)
```

```python
from contextlib import ExitStack

import concourse.bass as bass
from concourse import mybir

F32 = mybir.dt.float32
F32R = mybir.dt.float32r
I32 = mybir.dt.int32
ALU = mybir.AluOpType
ACT = mybir.ActivationFunctionType
AX = mybir.AxisListType
ds = bass.ds

P = 128
D = 1024
KC = D // P
SEQ = 2048
NT = SEQ // P
DB, DT = 8, 4
NS = DB * DT
TOK = SEQ + NS
PAST = 4096
NPG = PAST // P
GROUPS = ((128, 1), (512, 4), (2048, 16))
NG = 3
H = 8
HD = 64
AW = H * HD
QKV = NG * AW
QL, KL, ROPE = 256, 128, 32
NOPE = 64
LAT = QL + KL + ROPE
C_ZA = 3 * QKV
C_CQ = C_ZA + AW
C_ZB = C_CQ + LAT
C_MA = C_ZB + AW
IN_DIM = C_MA + 2 * D
A_SCALE = HD ** -0.5
B_SCALE = (NOPE + ROPE) ** -0.5
EPS = 1e-6
NEG = -1.0e30
LOWEST = -3.0e38
REC = 2 * HD + 4
RECB = HD + 2
VW = 2 * HD + 4
VB = HD + 2

COPIES = 2 * DB + 2 * (DB // 2)


class Mem:

    spent = []
    whole = None

    def __init__(self, nc, ctx, stage):
        self.nc, self.ctx, self.stage = nc, ctx, stage

    def sb(self, name, shape, dt=F32):
        return self.ctx.enter_context(self.nc.sbuf_tensor(f"{self.stage}_{name}", shape, dt))

    def ps(self, name, shape):
        return self.ctx.enter_context(self.nc.psum_tensor(f"{self.stage}_{name}", shape, F32))

    def sem(self, name):
        sem = self.ctx.enter_context(self.nc.semaphore(f"{self.stage}_{name}"))
        Mem.spent.append(sem)
        return sem

    def pool_sem(self, name):
        return Mem.whole.enter_context(self.nc.semaphore(f"{self.stage}_{name}"))


def clear_semaphores(nc):
    with nc.Block() as block:
        @block.sync
        def _(sp):
            for sem in Mem.spent:
                sp.sem_clear(sem)
    Mem.spent.clear()


def split_matmul(pe, out, w, x, first, last):
    pe.matmul(out, w[0], x[0], start=first, stop=False)
    pe.matmul(out, w[0], x[1], start=False, stop=False)
    return pe.matmul(out, w[1], x[0], start=False, stop=last)


def waits(eng, sem, count):
    if not isinstance(count, int) or count > 0:
        eng.wait_ge(sem, count)


def held(eng, sem, count, ticks):
    waits(eng, sem, count)
    if not isinstance(count, int):
        eng.sem_inc(ticks, 1)


def peeled(eng, count, step, body):
    body(0)
    with eng.Fori(1, count) as i:
        body(i * step)


def stage_norm(nc, t, xT, xs, ident):
    with ExitStack() as ctx:
        m = Mem(nc, ctx, "norm")
        xin = [m.sb(f"xin{b}", [P, D]) for b in range(2)]
        xn = [m.sb(f"xn{b}", [P, D]) for b in range(2)]
        junk = m.sb("junk", [P, D])
        g = m.sb("g_rows", [P, D])
        eps = m.sb("eps", [P, 1])
        stat = [m.sb(f"stat{b}", [P, 4]) for b in range(2)]
        tp = [m.ps(f"tp{b}", [P, KC, P]) for b in range(2)]
        consts = m.sem("consts")
        x_in = [m.sem(f"x_in{b}") for b in range(2)]
        eps_set, squared, rooted, inverted = (m.sem(n) for n in ("eps_set", "squared", "rooted", "inverted"))
        xn_ready, tp_ready, hi_ready, lo_ready = (m.sem(n) for n in ("xn_ready", "tp_ready", "hi_ready", "lo_ready"))

        with nc.Block() as block:
            @block.sync
            def _(sp):
                sp.dma_start(ident[:, :], t["ident"]).then_inc(consts, 16)
                sp.dma_start(g[:, :], t["g_pre"].partition_broadcast(P)).then_inc(consts, 16)

                def load(i):
                    for b in range(2):
                        waits(sp, xn_ready, i + b - 1)
                        sp.dma_start(xin[b][:, :], t["x_prompt"][ds((i + b) * P, P), :]).then_inc(x_in[b], 16)

                peeled(sp, NT // 2, 2, load)
                sp.wait_ge(xn_ready, NT - 1)
                sp.dma_start(xin[0][0:NS, :], t["x_sample"]).then_inc(x_in[0], 16)

            @block.scalar
            def _(act):
                act.wait_ge(eps_set, 1)

                def square(n, b, loads, rows):
                    act.wait_ge(x_in[b], loads)
                    waits(act, inverted, n - 1)
                    act.activation(junk[0:rows, :], xin[b][0:rows, :], ACT.Square,
                                   accum_out=stat[b][0:rows, 0:1]).then_inc(squared, 1)
                    act.wait_ge(squared, n + 1)
                    act.activation(stat[b][0:rows, 1:2], stat[b][0:rows, 0:1], ACT.Sqrt, bias=eps[0:rows, :],
                                   scale=1.0 / D).then_inc(rooted, 1)

                def high(n, b, out, rows):
                    act.wait_ge(tp_ready, n + 1)
                    act.activation(out, tp[b][:, :, 0:rows], ACT.Copy).then_inc(hi_ready, 1)

                def pair(i):
                    for b in range(2):
                        square(i + b, b, i * 8 + 16, P)
                    for b in range(2):
                        high(i + b, b, xT[0][:, :, ds((i + b) * P, P)], P)

                peeled(act, NT // 2, 2, pair)
                square(NT, 0, NT * 8 + 16, NS)
                high(NT, 0, xs[0][:, :, :], NS)

            @block.vector
            def _(dve):
                dve.memset(eps[:, :], EPS).then_inc(eps_set, 1)
                dve.wait_ge(consts, 32)

                def norm(n, b, rows):
                    dve.wait_ge(rooted, n + 1)
                    dve.reciprocal(stat[b][0:rows, 2:3], stat[b][0:rows, 1:2]).then_inc(inverted, 1)
                    dve.wait_ge(inverted, n + 1)
                    waits(dve, tp_ready, n - 1)
                    dve.scalar_tensor_tensor(xn[b][0:rows, :], xin[b][0:rows, :], stat[b][0:rows, 2:3],
                                             g[0:rows, :], ALU.mult, ALU.mult).then_inc(xn_ready, 1)

                def low(n, b, hi, lo, rows):
                    dve.wait_ge(hi_ready, n + 1)
                    dve.tensor_tensor(lo, tp[b][:, :, 0:rows], hi.bitcast(F32), ALU.subtract).then_inc(lo_ready, 1)

                def pair(i):
                    for b in range(2):
                        norm(i + b, b, P)
                    for b in range(2):
                        at = ds((i + b) * P, P)
                        low(i + b, b, xT[0][:, :, at], xT[1][:, :, at], P)

                peeled(dve, NT // 2, 2, pair)
                norm(NT, 0, NS)
                low(NT, 0, xs[0][:, :, :], xs[1][:, :, :], NS)

            @block.tensor
            def _(pe):
                pe.wait_ge(consts, 32)

                def turn(n, b, rows):
                    pe.wait_ge(xn_ready, n + 1)
                    waits(pe, lo_ready, n - 1)
                    for c in range(KC):
                        last = pe.transpose(tp[b][:, c, 0:rows], xn[b][0:rows, c * P:(c + 1) * P],
                                            ident[0:rows, 0:rows])
                    last.then_inc(tp_ready, 1)

                def pair(i):
                    for b in range(2):
                        turn(i + b, b, P)

                peeled(pe, NT // 2, 2, pair)
                turn(NT, 0, NS)


def stage_latents(nc, t, xT, xs, ident):
    with ExitStack() as ctx:
        m = Mem(nc, ctx, "lat")
        raw = [m.sb(f"raw{b}", [P, LAT]) for b in range(2)]
        w = [m.sb(f"w_{h}", [P, KC, LAT], F32R) for h in ("hi", "lo")]
        lat = [m.sb(f"lat{b}", [P, LAT]) for b in range(2)]
        nat = [m.sb(f"nat{b}", [P, LAT]) for b in range(2)]
        rot = [m.sb(f"rot{b}", [P, 2 * ROPE]) for b in range(2)]
        junk_q, junk_kv = m.sb("junk_q", [P, QL]), m.sb("junk_kv", [P, KL])
        stat = [m.sb(f"stat{b}", [P, 6]) for b in range(2)]
        eps = m.sb("eps", [P, 1])
        gkv = m.sb("gkv_rows", [P, KL])
        gq = m.sb("gq_cols", [P, QL // P])
        cs = m.sb("rope_rows", [P, NT + 1, 2, ROPE])
        cqT = m.sb("cqT", [P, QL // P, TOK])
        ckvT = m.sb("ckvT", [P, TOK])
        kpeT = m.sb("kpeT", [ROPE, TOK])
        pj = [m.ps(f"pj{b}", [P, 512]) for b in range(4)]
        tp = [m.ps(f"tp{b}", [P, 4, P]) for b in range(2)]
        consts = m.sem("consts")
        w_in = [m.sem(f"w_in{b}") for b in range(2)]
        w_hi, w_lo, eps_set = m.sem("w_hi"), m.sem("w_lo"), m.sem("eps_set")
        pj_ready, copied, squared, rooted, inverted = (
            m.sem(n) for n in ("pj_ready", "copied", "squared", "rooted", "inverted"))
        rotated, nat_ready, tp_ready, turned = (m.sem(n) for n in ("rotated", "nat_ready", "tp_ready", "turned"))
        nat_stored = [m.sem(f"nat_stored{b}") for b in range(2)]
        stored = m.sem("stored")
        tiles = [(i, P if i < NT else NS) for i in range(NT + 1)]

        with nc.Block() as block:
            @block.sync
            def _(sp):
                for c in range(KC):
                    waits(sp, w_lo, c - 1)
                    sp.dma_start(raw[c % 2][:, :], t["w_in"][c * P:(c + 1) * P, C_CQ:C_CQ + LAT])\
                        .then_inc(w_in[c % 2], 16)
                sp.dma_start(gkv[:, :], t["g_kv"].partition_broadcast(P)).then_inc(consts, 16)
                with nc.allow_non_contiguous_dma(reason="256 gains, one per partition"):
                    sp.dma_start(gq[:, :], t["g_q"].rearrange("(c p) -> p c", p=P)).then_inc(consts, 16)
                sp.dma_start(cs[:, 0:NT, :, :], t["rope_rows"][0:SEQ].rearrange("(i p) s r -> p i s r", p=P))\
                    .then_inc(consts, 16)
                sp.dma_start(cs[0:NS, NT, :, :], t["rope_rows"][SEQ:TOK]).then_inc(consts, 16)
                for i, rows in tiles:
                    b = i % 2
                    sp.wait_ge(nat_ready, i + 1)
                    if i < NT:
                        ckv, kpe = t["ckv_prompt"][i * P:(i + 1) * P, :], t["kpe_prompt"][i * P:(i + 1) * P, :]
                    else:
                        ckv, kpe = t["ckv_sample"], t["kpe_sample"]
                    sp.dma_start(ckv, nat[b][0:rows, QL:QL + KL]).then_inc(nat_stored[b], 16)
                    sp.dma_start(kpe, nat[b][0:rows, QL + KL:LAT]).then_inc(nat_stored[b], 16)
                sp.wait_ge(turned, NT + 1)
                for c in range(QL // P):
                    sp.dma_start(t["cqT"][c], cqT[:, c, :]).then_inc(stored, 16)
                sp.dma_start(t["ckvT"], ckvT[:, :]).then_inc(stored, 16)
                sp.dma_start(t["kpeT"], kpeT[:, :]).then_inc(stored, 16)
                sp.wait_ge(stored, 64)
                sp.wait_ge(nat_stored[0], 32 * 9)
                sp.wait_ge(nat_stored[1], 32 * 8)

            @block.scalar
            def _(act):
                for c in range(KC):
                    act.wait_ge(w_in[c % 2], 16 * (c // 2 + 1))
                    act.activation(w[0][:, c, :], raw[c % 2][:, :], ACT.Copy).then_inc(w_hi, 1)
                act.wait_ge(eps_set, 1)
                act.wait_ge(consts, 64)

                def turned_out(i, rows):
                    b, at = i % 2, slice(i * P, i * P + rows)
                    act.wait_ge(tp_ready, i + 1)
                    for c in range(QL // P):
                        act.activation(cqT[:, c, at], tp[b][:, c, 0:rows], ACT.Copy, scale=gq[:, c:c + 1])
                    act.activation(ckvT[:, at], tp[b][:, 2, 0:rows], ACT.Copy)
                    act.activation(kpeT[:, at], tp[b][0:ROPE, 3, 0:rows], ACT.Copy).then_inc(turned, 1)

                for i, rows in tiles:
                    b = i % 2
                    act.wait_ge(pj_ready, i + 1)
                    waits(act, nat_ready, i - 1)
                    r = slice(0, rows)
                    act.activation(junk_q[r, :], pj[i % 4][r, 0:QL], ACT.Square,
                                   accum_out=stat[b][r, 0:1]).then_inc(squared, 1)
                    act.activation(junk_kv[r, :], pj[i % 4][r, QL:QL + KL], ACT.Square,
                                   accum_out=stat[b][r, 1:2]).then_inc(squared, 1)
                    act.activation(lat[b][r, :], pj[i % 4][r, 0:LAT], ACT.Copy).then_inc(copied, 1)
                    act.wait_ge(squared, 2 * i + 2)
                    act.activation(stat[b][r, 2:3], stat[b][r, 0:1], ACT.Sqrt, bias=eps[r, :],
                                   scale=1.0 / QL).then_inc(rooted, 1)
                    act.activation(stat[b][r, 3:4], stat[b][r, 1:2], ACT.Sqrt, bias=eps[r, :],
                                   scale=1.0 / KL).then_inc(rooted, 1)
                    if i:
                        turned_out(i - 1, P)
                turned_out(NT, NS)

            @block.vector
            def _(dve):
                dve.memset(eps[:, :], EPS).then_inc(eps_set, 1)
                for c in range(KC):
                    dve.wait_ge(w_hi, c + 1)
                    dve.tensor_tensor(w[1][:, c, :], raw[c % 2][:, :], w[0][:, c, :].bitcast(F32),
                                      ALU.subtract).then_inc(w_lo, 1)
                dve.wait_ge(consts, 64)
                half = ROPE // 2
                for i, rows in tiles:
                    b, r = i % 2, slice(0, rows)
                    dve.wait_ge(rooted, 2 * i + 2)
                    dve.wait_ge(copied, i + 1)
                    dve.reciprocal(stat[b][r, 4:6], stat[b][r, 2:4]).then_inc(inverted, 1)
                    pe_at = lat[b][r, QL + KL:LAT]
                    dve.tensor_tensor(rot[b][r, 0:ROPE], pe_at, cs[r, i, 0, :], ALU.mult)
                    dve.tensor_tensor(rot[b][r, ROPE:ROPE + half], lat[b][r, QL + KL + half:LAT],
                                      cs[r, i, 1, 0:half], ALU.mult)
                    dve.tensor_tensor(rot[b][r, ROPE + half:2 * ROPE], lat[b][r, QL + KL:QL + KL + half],
                                      cs[r, i, 1, half:ROPE], ALU.mult).then_inc(rotated, 1)
                    dve.wait_ge(inverted, i + 1)
                    waits(dve, tp_ready, i - 1)
                    waits(dve, nat_stored[b], 32 * (i // 2))
                    dve.tensor_scalar(nat[b][r, 0:QL], lat[b][r, 0:QL], stat[b][r, 4:5], None, ALU.mult)
                    dve.scalar_tensor_tensor(nat[b][r, QL:QL + KL], lat[b][r, QL:QL + KL], stat[b][r, 5:6],
                                             gkv[r, :], ALU.mult, ALU.mult)
                    dve.wait_ge(rotated, i + 1)
                    dve.tensor_tensor(nat[b][r, QL + KL:LAT], rot[b][r, 0:ROPE], rot[b][r, ROPE:2 * ROPE],
                                      ALU.add).then_inc(nat_ready, 1)

            @block.tensor
            def _(pe):
                pe.wait_ge(w_lo, KC)

                def turn(i, rows):
                    b = i % 2
                    pe.wait_ge(nat_ready, i + 1)
                    waits(pe, turned, i - 1)
                    for c in range(3):
                        pe.transpose(tp[b][:, c, 0:rows], nat[b][0:rows, c * P:(c + 1) * P],
                                     ident[0:rows, 0:rows])
                    pe.transpose(tp[b][0:ROPE, 3, 0:rows], nat[b][0:rows, QL + KL:LAT],
                                 ident[0:rows, 0:rows]).then_inc(tp_ready, 1)

                for i, rows in tiles:
                    waits(pe, copied, i - 3)
                    for c in range(KC):
                        x = [xT[h][:, c, i * P:(i + 1) * P] if i < NT else xs[h][:, c, :] for h in range(2)]
                        last = split_matmul(pe, pj[i % 4][0:rows, 0:LAT], x, [w[h][:, c, :] for h in range(2)],
                                            c == 0, c == KC - 1)
                    last.then_inc(pj_ready, 1)
                    if i:
                        turn(i - 1, P)
                turn(NT, NS)


def stage_dilated(nc, t, xT, xs, ident, copied):
    with ExitStack() as ctx:
        m = Mem(nc, ctx, "dil")
        raw = [m.sb(f"raw{b}", [P, KC, P]) for b in range(2)]
        w = [[m.sb(f"w{b}_{h}", [P, KC, P], F32R) for h in ("hi", "lo")] for b in range(2)]
        qT = m.sb("qT", [P, SEQ])
        kT = m.sb("kT", [P, SEQ])
        v = m.sb("v", [P, NT, VW])
        sm = [m.sb(f"sm{b}", [P, 2, 2, 2 * P]) for b in range(2)]
        pT = [m.sb(f"pT{b}", [P, 4, P]) for b in range(2)]
        neg = [m.sb(f"neg{b}", [P, 2, 2]) for b in range(2)]
        rec = [m.sb(f"rec{b}", [P, 2, REC]) for b in range(4)]
        bias = m.sb("bias", [P, 2, 2 * P])
        hs = m.sb("hs", [NS, 3, P])
        S = m.ps("S", [P, 4, 512])
        T = m.ps("T", [P, 2, 4, P])
        O = m.ps("O", [P, 2, 2, 256])

        raw_in = [m.sem(f"raw_in{b}") for b in range(2)]
        bias_in, ones_set = m.sem("bias_in"), m.sem("ones_set")
        w_hi, w_lo = m.sem("w_hi"), m.sem("w_lo")
        q_ready, k_ready, vT_ready, v_ready, hs_ready = (
            m.sem(n) for n in ("q_ready", "k_ready", "vT_ready", "v_ready", "hs_ready"))
        q_out, k_out, vT_out, v_out, hs_out = (m.sem(n) for n in ("q_out", "k_out", "vT_out", "v_out", "hs_out"))
        kn_ready, kn_out = m.sem("kn_ready"), m.sem("kn_out")
        kn_stored = [m.sem("kn_stored_sm"), m.sem("kn_stored_raw")]
        v_stored, hs_stored = m.sem("v_stored"), m.sem("hs_stored")
        s_ready, masked, negated, exped = (m.sem(n) for n in ("s_ready", "masked", "negated", "exped"))
        t_ready, t_out_a, t_out_b = m.sem("t_ready"), m.sem("t_out_a"), m.sem("t_out_b")
        pv_ready, rec_out = m.sem("pv_ready"), m.sem("rec_out")
        rec_stored = [m.sem(f"rec_stored{b}") for b in range(4)]
        sp_ticks, dve_ticks = m.sem("sp_ticks"), m.sem("dve_ticks")
        NU = NT // 2
        KN_TILES = [min(w_, SEQ) // P for w_, _ in GROUPS]
        KN = [-(-n // 4) for n in KN_TILES]
        KN_BASE = [sum(4 * KN[h] for h in range(g)) for g in range(NG)]

        ORDER = ((2, 0), (1, 1), (0, 0))

        def each_pair(eng, body):
            body(0, 0, 0, False)
            for g in range(NG):
                with eng.Fori(0 if g else 1, 3 if g == NG - 1 else 4) as hp:
                    body(g, hp, hp + 4 * g, False)
            body(NG - 1, 3, 4 * NG - 1, True)

        def knat(k):
            if k < 2:
                return sm[1][:, k, :, :].rearrange("p h c -> p (h c)").rearrange("p (s c) -> p s c", c=P)
            return raw[1][:, 4 * (k - 2):4 * (k - 1), :]

        def kn_stores(g, hp, place):
            here = [min(2, KN[h]) if place == 0 else max(0, KN[h] - 2) for h in range(NG)]
            return hp * here[g] + 4 * sum(here[:g]) + here[g]

        def blocks(g, u):
            nb = NT // GROUPS[g][1]
            return [(s, 2 * u + s, 2 * u + s - ((2 * u + s) % nb > 0), 1 + ((2 * u + s) % nb > 0)) for s in range(2)]

        def tokens(g, j, count=1):
            d = GROUPS[g][1]
            nb = NT // d
            start = j // nb + d * P * (j % nb)
            return slice(start, start + d * (count * P - 1) + 1, d)

        with nc.Block() as block:
            @block.sync
            def _(sp):
                def load(n, o):
                    which, b = ORDER[o]
                    src = t["w_in"][:, ds(n * P + which * QKV, P)]
                    sp.dma_start(raw[b][:, :, :], src.rearrange("(c p) n -> p c n", p=P)).then_inc(raw_in[b], 16)

                load(0, 0)
                load(0, 1)

                def body(g, hp, n, last):
                    held(sp, w_lo, n * 3 + 1, sp_ticks)
                    load(n, 2)
                    held(sp, masked, n * NU, sp_ticks)
                    sp.dma_start(bias[:, :, :], t["alibi"][g, :, ds(hp * 2, 2), :]).then_inc(bias_in, 16)
                    held(sp, v_out, (n + 1) * 4, sp_ticks)
                    win = t[f"win{g}_prompt"][0]
                    col = ds(hp * P, P)
                    if g == 0:
                        sp.dma_start(win[:, 1, col], v[:, NT - 1, 2:2 + P]).then_inc(v_stored, 16)
                    elif g == 1:
                        sp.dma_start(win[:, 1, col].rearrange("(i d) c -> i d c", d=4), v[:, 3:NT:4, 2:2 + P])\
                            .then_inc(v_stored, 16)
                    else:
                        sp.dma_start(win[:, 1, col].rearrange("(i d) c -> i d c", d=NT), v[:, :, 2:2 + P])\
                            .then_inc(v_stored, 16)
                    if not last:
                        held(sp, w_lo, n * 3 + 3, sp_ticks)
                        load(n + 1, 0)
                    for k in range(KN[g]):
                        tiles = min(4, KN_TILES[g])
                        held(sp, kn_out, KN_BASE[g] + hp * KN[g] + k + 1, sp_ticks)
                        rows = slice(k * 4 * P, (k * 4 + tiles) * P)
                        sp.dma_start(win[rows, 0, col].rearrange("(s p) c -> p s c", p=P), knat(k)[:, 0:tiles, :])\
                            .then_inc(kn_stored[k // 2], 16)
                    if not last:
                        if KN[g] > 2:
                            held(sp, kn_stored[1], kn_stores(g, hp, 1) * 16, sp_ticks)
                        load(n + 1, 1)
                    held(sp, hs_out, n + 1, sp_ticks)
                    for which in range(3):
                        sp.dma_start(t["hs"][:, ds(which * QKV + g * AW + hp * P, P)], hs[:, which, :])\
                            .then_inc(hs_stored, 16)
                    for u in range(NU):
                        held(sp, rec_out, n * NU + u + 1, sp_ticks)
                        for s, j, _, _ in blocks(g, u):
                            sp.dma_start(t["oa"][tokens(g, j), g, ds(hp, 1), :].rearrange("i o e -> i (o e)"),
                                         rec[u % 4][:, s, :]).then_inc(rec_stored[u % 4], 16)

                each_pair(sp, body)
                sp.wait_ge(hs_stored, 12 * 48)
                sp.wait_ge(v_stored, 12 * 16)
                for place in range(2):
                    sp.wait_ge(kn_stored[place], 16 * kn_stores(NG - 1, 3, place))
                for b in range(4):
                    sp.wait_ge(rec_stored[b], 12 * NU // 4 * 32)

            @block.gpsimd
            def _(pool):
                pool.memset(v[:, :, 0:1], 1.0)
                pool.memset(v[:, :, 1:2], 0.0)
                pool.memset(v[:, :, 2 + P:3 + P], 1.0)
                pool.memset(v[:, :, 3 + P:VW], 0.0).then_inc(ones_set, 1)

                def move(g, b, count, rows):
                    old = t[f"state_win{g}"][ds(b, count), rows.start + DT:rows.stop + DT]
                    pool.dma_start(t[f"win{g}_sample"][ds(b, count), rows].rearrange("b i c n -> b i (c n)"),
                                   old.rearrange("b i c n -> b i (c n)")).then_inc(copied, 16)

                kept = [win - DT for win, _ in GROUPS]
                with pool.Fori(0, DB) as b:
                    pool.wait_ge(vT_ready, b * 4 + 1)
                    move(2, b, 1, slice(0, kept[2] // 2))
                    pool.wait_ge(k_ready, b * 4 + 1)
                    move(2, b, 1, slice(kept[2] // 2, kept[2]))
                with pool.Fori(0, DB // 2) as i:
                    pool.wait_ge(vT_ready, (i + DB) * 4 + 1)
                    move(1, i * 2, 2, slice(0, kept[1]))
                    move(0, i * 2, 2, slice(0, kept[0]))

            @block.scalar
            def _(act):
                def high(n, o):
                    _, b = ORDER[o]
                    act.wait_ge(raw_in[b], n * 16 + 16 if b else n * 32 + (32 if o else 16))
                    if o < 2:
                        waits(act, hs_ready, n * 3 - (1 if o else 0))
                    else:
                        act.wait_ge(hs_ready, n * 3 + 1)
                    act.activation(w[b][0][:, :, :], raw[b][:, :, :], ACT.Copy).then_inc(w_hi, 1)

                high(0, 0)
                high(0, 1)

                def body(g, hp, n, last_pair):
                    for k in range(4):
                        act.wait_ge(vT_ready, n * 4 + k + 1)
                        act.activation(qT[:, k * 512:(k + 1) * 512], S[:, k, :], ACT.Copy).then_inc(vT_out, 1)
                    high(n, 2)
                    waits(act, v_stored, n * 16)
                    for k in range(4):
                        act.wait_ge(v_ready, n * 4 + k + 1)
                        act.activation(v[:, 4 * k:4 * k + 4, 2:2 + P], T[:, k % 2, :, :], ACT.Copy).then_inc(v_out, 1)
                    for k in range(4):
                        act.wait_ge(q_ready, n * 4 + k + 1)
                        act.activation(qT[:, k * 512:(k + 1) * 512], S[:, k, :], ACT.Copy, scale=A_SCALE)\
                            .then_inc(q_out, 1)

                    def exps(u):
                        b = u % 2
                        act.wait_ge(negated, n * NU + u + 1)
                        for s, _, _, nk in blocks(g, u):
                            for h in range(2):
                                part = sm[b][:, s, h, 0:nk * P]
                                last = act.activation(part, part, ACT.Exp, bias=neg[b][:, s, h:h + 1])
                        last.then_inc(exped, 1)

                    def turned(u):
                        act.wait_ge(t_ready, (n * NU + u) * 2 + 1)
                        waits(act, pv_ready, n * NU + u)
                        q = 2 * blocks(g, u)[0][3]
                        act.activation(pT[0][:, 0:q, :], T[:, 0, 0:q, :], ACT.Copy).then_inc(t_out_a, 1)

                    for u in range(NU + 1):
                        if u < NU:
                            exps(u)
                        if u == 0:
                            act.wait_ge(hs_ready, n * 3 + 3)
                            waits(act, hs_stored, n * 48)
                            act.activation(hs[:, :, :], O[0:NS, 0, :, :].rearrange("p a b -> p (a b)")[:, 0:3 * P]
                                           .rearrange("p (a b) -> p a b", a=3), ACT.Copy).then_inc(hs_out, 1)
                        else:
                            turned(u - 1)
                        if u in (3, 5) and not last_pair:
                            high(n + 1, (u - 3) // 2)

                each_pair(act, body)

            @block.vector
            def _(dve):
                def low(n, o):
                    _, b = ORDER[o]
                    dve.wait_ge(w_hi, n * 3 + o + 1)
                    dve.tensor_tensor(w[b][1][:, :, :], raw[b][:, :, :], w[b][0][:, :, :].bitcast(F32),
                                      ALU.subtract).then_inc(w_lo, 1)

                low(0, 0)
                low(0, 1)

                def body(g, hp, n, last_pair):
                    low(n, 2)
                    for k in range(4):
                        dve.wait_ge(k_ready, n * 4 + k + 1)
                        dve.tensor_copy(kT[:, k * 512:(k + 1) * 512], S[:, k, :]).then_inc(k_out, 1)
                    tiles = min(4, KN_TILES[g])
                    for k in range(KN[g]):
                        c = KN_BASE[g] + hp * KN[g] + k
                        dve.wait_ge(kn_ready, c + 1)
                        dve.tensor_copy(knat(k)[:, 0:tiles, :], T[:, k % 2, 0:tiles, :]).then_inc(kn_out, 1)
                    dve.wait_ge(bias_in, n * 16 + 16)

                    def mask(u):
                        b, c = u % 2, n * NU + u
                        dve.wait_ge(s_ready, c + 1)
                        waits(dve, t_ready, (c - 1) * 2)
                        if u == 1:
                            waits(dve, kn_stored[0], kn_stores(g, hp, 0) * 16)
                        held(dve, rec_stored[u % 4], (n * (NU // 4) + u // 4) * 32, dve_ticks)
                        for s, _, _, nk in blocks(g, u):
                            for h in range(2):
                                last = dve.tensor_tensor_reduce(
                                    sm[b][:, s, h, 0:nk * P], S[:, 2 * b + h, s * 2 * P:(s * 2 + nk) * P],
                                    bias[:, h, (2 - nk) * P:2 * P], 1.0, LOWEST, ALU.add, ALU.max,
                                    rec[u % 4][:, s, 2 * HD + 2 + h:2 * HD + 3 + h])
                        last.then_inc(masked, 1)
                        dve.wait_ge(masked, c + 1)
                        dve.tensor_scalar(neg[b][:, :, :], rec[u % 4][:, :, 2 * HD + 2:REC], -1.0, None, ALU.mult)\
                            .then_inc(negated, 1)

                    def turned(u):
                        c = n * NU + u
                        dve.wait_ge(t_ready, c * 2 + 2)
                        waits(dve, pv_ready, c)
                        q = 2 * blocks(g, u)[1][3]
                        dve.tensor_copy(pT[1][:, 0:q, :], T[:, 1, 0:q, :]).then_inc(t_out_b, 1)

                    def records(u):
                        b = u % 2
                        dve.wait_ge(pv_ready, n * NU + u + 1)
                        dve.tensor_copy(rec[u % 4][:, :, 0:2 * HD], O[:, b, :, 2:2 + 2 * HD])
                        dve.tensor_copy(rec[u % 4][:, :, 2 * HD:2 * HD + 2], O[:, b, :, 0:2 + P + 1:P + 2])\
                            .then_inc(rec_out, 1)

                    for u in range(NU + 2):
                        if u < NU:
                            mask(u)
                        if 0 < u <= NU:
                            turned(u - 1)
                        if u > 1:
                            records(u - 2)
                        if u in (4, 6) and not last_pair:
                            low(n + 1, (u - 4) // 2)

                each_pair(dve, body)

            @block.tensor
            def _(pe):
                def body(g, hp, n, _):
                    def project(o, k):
                        b = ORDER[o][1]
                        for c in range(KC):
                            last = split_matmul(pe, S[:, k, :], [w[b][h][:, c, :] for h in range(2)],
                                                [xT[h][:, c, k * 512:(k + 1) * 512] for h in range(2)],
                                                c == 0, c == KC - 1)
                        last.then_inc((vT_ready, k_ready, q_ready)[o], 1)

                    pe.wait_ge(w_lo, n * 3 + 1)
                    waits(pe, masked, n * NU)
                    for k in range(4):
                        project(0, k)
                    sample(n, 0)
                    pe.wait_ge(w_lo, n * 3 + 2)
                    for k in range(4):
                        pe.wait_ge(vT_out, n * 4 + k + 1)
                        project(1, k)
                        if k == 0:
                            pe.wait_ge(vT_out, n * 4 + 4)
                        if k < 2:
                            waits(pe, t_out_a, n * NU)
                            waits(pe, t_out_b, n * NU)
                        else:
                            pe.wait_ge(v_out, n * 4 + k - 1)
                        for s in range(4):
                            last = pe.transpose(T[:, k % 2, s, :], qT[:, tokens(g, 4 * k + s)], ident[:, :])
                        last.then_inc(v_ready, 1)
                    sample(n, 1)
                    pe.wait_ge(w_lo, n * 3 + 3)
                    for k in range(4):
                        pe.wait_ge(k_out, n * 4 + k + 1)
                        project(2, k)
                        if k < KN[g]:
                            if k == 0:
                                pe.wait_ge(k_out, n * 4 + 4)
                            if k < 2:
                                pe.wait_ge(v_out, n * 4 + 3 + k)
                            else:
                                pe.wait_ge(kn_out, KN_BASE[g] + hp * KN[g] + k - 1)
                            for s in range(min(4, KN_TILES[g])):
                                at = SEQ - KN_TILES[g] * P + (4 * k + s) * P
                                last = pe.transpose(T[:, k % 2, s, :], kT[:, at:at + P], ident[:, :])
                            last.then_inc(kn_ready, 1)
                    pe.wait_ge(q_out, n * 4 + 4)
                    pe.wait_ge(v_out, n * 4 + 4)
                    pe.wait_ge(ones_set, 1)

                    def scores(u):
                        c = n * NU + u
                        if u > 1:
                            pe.wait_ge(masked, c - 1)
                        for s, j, j0, nk in blocks(g, u):
                            for h in range(2):
                                r = slice(h * HD, (h + 1) * HD)
                                last = pe.matmul(S[:, 2 * (u % 2) + h, s * 2 * P:(s * 2 + nk) * P],
                                                 qT[r, tokens(g, j)], kT[r, tokens(g, j0, nk)],
                                                 start=True, stop=True)
                        last.then_inc(s_ready, 1)

                    def turns(u):
                        c = n * NU + u
                        pe.wait_ge(exped, c + 1)
                        if u:
                            pe.wait_ge(t_out_a, c)
                            pe.wait_ge(t_out_b, c)
                        else:
                            pe.wait_ge(kn_out, KN_BASE[g] + hp * KN[g] + KN[g])
                            waits(pe, t_out_a, c)
                            waits(pe, t_out_b, c)
                        for s, _, _, nk in blocks(g, u):
                            for h in range(2):
                                for k in range(nk):
                                    last = pe.transpose(T[:, s, h * nk + k, :],
                                                        sm[u % 2][:, s, h, k * P:(k + 1) * P], ident[:, :])
                            last.then_inc(t_ready, 1)

                    def values(u):
                        c = n * NU + u
                        pe.wait_ge(t_out_a, c + 1)
                        pe.wait_ge(t_out_b, c + 1)
                        if u > 1:
                            pe.wait_ge(rec_out, c - 1)
                        elif u == 0:
                            pe.wait_ge(hs_out, n + 1)
                            waits(pe, rec_out, c - 1)
                        else:
                            waits(pe, rec_out, c - 1)
                        for s, j, j0, nk in blocks(g, u):
                            for h in range(2):
                                for k in range(nk):
                                    last = pe.matmul(O[:, u % 2, s, h * 66:(h + 1) * 66], pT[s][:, h * nk + k, :],
                                                     v[:, j0 + k, h * 66:(h + 1) * 66],
                                                     start=(k == 0), stop=(k == nk - 1))
                        last.then_inc(pv_ready, 1)

                    for u in range(NU + 2):
                        if u < NU:
                            scores(u)
                        if u == 1:
                            sample(n, 2)
                        if 0 < u <= NU:
                            turns(u - 1)
                        if u > 1:
                            values(u - 2)

                def sample(n, o):
                    which, b = ORDER[o]
                    if o == 0:
                        waits(pe, rec_out, n * NU)
                    out = O[0:NS, 0, :, :].rearrange("p a b -> p (a b)")[:, which * P:(which + 1) * P]
                    for c in range(KC):
                        last = split_matmul(pe, out, [xs[h][:, c, :] for h in range(2)],
                                            [w[b][h][:, c, :] for h in range(2)], c == 0, c == KC - 1)
                    last.then_inc(hs_ready, 1)

                each_pair(pe, body)
def stage_gates(nc, t, xT, xs):
    with ExitStack() as ctx:
        m = Mem(nc, ctx, "gate")
        raw = [m.sb(f"raw{b}", [P, KC, P]) for b in range(2)]
        w = [[m.sb(f"w{b}_{h}", [P, KC, P], F32R) for h in ("hi", "lo")] for b in range(2)]
        out = [m.sb(f"out{b}", [P, TOK]) for b in range(2)]
        BANKS = 5
        ps = m.ps("ps", [P, BANKS, 512])
        raw_in = [m.sem(f"raw_in{b}") for b in range(2)]
        w_hi, w_lo, ready, sig, emptied = (m.sem(n) for n in ("w_hi", "w_lo", "ready", "sig", "emptied"))
        stored = [m.pool_sem(f"stored{b}") for b in range(2)]
        sp_ticks = m.sem("sp_ticks")
        KINDS = ((C_ZA, 0, 2, True), (C_ZB, 4, 2, True), (C_MA, 8, 8, False))
        CHUNKS = [(k * 512, 512) for k in range(4)] + [(SEQ, NS)]

        PAIRS = sum(pairs for _, _, pairs, _ in KINDS)

        def each(eng, body):
            n = 0
            for col, blk, pairs, mult in KINDS:
                if n == 0:
                    body(col, blk, 0, mult)
                last = n + pairs == PAIRS
                with eng.Fori(0 if n else 1, pairs - last) as i:
                    body(i * 2 * P + col, i * 2 + blk, i + n, mult)
                n += pairs
                if last:
                    i = pairs - 1
                    body(i * 2 * P + col, i * 2 + blk, PAIRS - 1, mult)

        with nc.Block() as block:
            @block.sync
            def _(sp):
                def body(col, blk, n, mult):
                    for b in range(2):
                        held(sp, w_lo, n * 2 - 1 + b, sp_ticks)
                        sp.dma_start(raw[b][:, :, :],
                                     t["w_in"][:, ds(col + b * P, P)].rearrange("(c p) n -> p c n", p=P))\
                            .then_inc(raw_in[b], 16)

                each(sp, body)

            @block.scalar
            def _(act):
                def high(n, b):
                    act.wait_ge(raw_in[b], n * 16 + 16)
                    waits(act, ready, (n * 2 + b - 1) * 5)
                    act.activation(w[b][0][:, :, :], raw[b][:, :, :], ACT.Copy).then_inc(w_hi, 1)

                high(0, 0)
                high(0, 1)

                def body(col, blk, n, mult):
                    for b in range(2):
                        waits(act, stored[b], n * 16)
                        for k, (at, width) in enumerate(CHUNKS):
                            act.wait_ge(ready, n * 10 + b * 5 + k + 1)
                            act.activation(out[b][:, at:at + width], ps[:, k, 0:width], ACT.Sigmoid)\
                                .then_inc(sig, 1)
                        if not isinstance(n, int) or n < PAIRS - 1:
                            high(n + 1, b)

                each(act, body)

            @block.gpsimd
            def _(pool):
                def body(col, blk, n, mult):
                    for b in range(2):
                        pool.wait_ge(emptied, n * 10 + b * 5 + 5)
                        pool.dma_start(t["gates"][ds(blk + b, 1)].rearrange("o p n -> (o p) n"), out[b][:, :])\
                            .then_inc(stored[b], 16)

                each(pool, body)
                for b in range(2):
                    pool.wait_ge(stored[b], 12 * 16)

            @block.vector
            def _(dve):
                def low(n, b):
                    dve.wait_ge(w_hi, n * 2 + b + 1)
                    dve.tensor_tensor(w[b][1][:, :, :], raw[b][:, :, :], w[b][0][:, :, :].bitcast(F32),
                                      ALU.subtract).then_inc(w_lo, 1)

                low(0, 0)
                low(0, 1)

                def body(col, blk, n, mult):
                    for b in range(2):
                        for k, (at, width) in enumerate(CHUNKS):
                            dve.wait_ge(sig, n * 10 + b * 5 + k + 1)
                            o = out[b][:, at:at + width]
                            if mult:
                                dve.tensor_tensor(o, o, ps[:, k, 0:width], ALU.mult).then_inc(emptied, 1)
                            else:
                                if k == 0:
                                    dve.wait_ge(emptied, n * 10 + b * 5)
                                dve.sem_inc(emptied, 1)
                        if not isinstance(n, int) or n < PAIRS - 1:
                            low(n + 1, b)

                each(dve, body)

            @block.tensor
            def _(pe):
                def body(col, blk, n, mult):
                    for b in range(2):
                        pe.wait_ge(w_lo, n * 2 + b + 1)
                        for k, (at, width) in enumerate(CHUNKS):
                            waits(pe, emptied, (n * 2 + b - 1) * 5 + k + 1)
                            for c in range(KC):
                                x = [xT[h][:, c, at:at + width] if at < SEQ else xs[h][:, c, :] for h in range(2)]
                                last = split_matmul(pe, ps[:, k, 0:width], [w[b][h][:, c, :] for h in range(2)],
                                                    x, c == 0, c == KC - 1)
                            last.then_inc(ready, 1)

                each(pe, body)


def load_latents(sp, t, cqT, ckvT, k96, rope, causal, loaded):
    for c in range(QL // P):
        sp.dma_start(cqT[:, c, :], t["cqT"][c]).then_inc(loaded, 16)
    sp.dma_start(ckvT[:, :], t["ckvT"]).then_inc(loaded, 16)
    sp.dma_start(k96[NOPE:NOPE + ROPE, :], t["kpeT"][:, 0:SEQ]).then_inc(loaded, 16)
    sp.dma_start(rope[NOPE:P, :], t["rope_cols"]).then_inc(loaded, 16)
    sp.dma_start(causal[:, :], t["causal"]).then_inc(loaded, 16)


def load_head_weights(eng, t, h, wq, wk, wv, sem):
    W = NOPE + ROPE
    half = ROPE // 2
    uq = t["w_uq"].rearrange("(c p) n -> p c n", p=P)
    eng.dma_start(wq[:, :, 0:W], uq[:, :, ds(h * W, W)]).then_inc(sem, 16)
    eng.dma_start(wq[:, :, W:W + half], uq[:, :, ds(h * W + NOPE + half, half)]).then_inc(sem, 16)
    eng.dma_start(wq[:, :, W + half:P], uq[:, :, ds(h * W + NOPE, half)]).then_inc(sem, 16)
    eng.dma_start(wk[:, :], t["w_uk"][:, ds(h, 1), :].rearrange("c o d -> c (o d)")).then_inc(sem, 16)
    eng.dma_start(wv[:, :], t["w_uv"][:, ds(h, 1), :].rearrange("c o d -> c (o d)")).then_inc(sem, 16)


def stage_latent_attn(nc, t, ident):
    with ExitStack() as ctx:
        m = Mem(nc, ctx, "mla")
        cqT = m.sb("cqT", [P, QL // P, TOK])
        ckvT = m.sb("ckvT", [P, TOK])
        rope = m.sb("rope", [P, TOK])
        causal = m.sb("causal", [P, P])
        q96 = m.sb("q96", [P, TOK])
        k96 = m.sb("k96", [P, SEQ])
        turned = [m.sb(f"turned{b}", [P, 2, 512]) for b in range(2)]
        wq = [m.sb(f"wq{b}", [P, QL // P, P]) for b in range(2)]
        wk = [m.sb(f"wk{b}", [P, NOPE]) for b in range(2)]
        wv = [m.sb(f"wv{b}", [P, HD]) for b in range(2)]
        v = m.sb("v", [P, NT, VB])
        p = [m.sb(f"p{b}", [P, 8 * P]) for b in range(2)]
        pT = [[m.sb(f"pT{b}_{half}", [P, 4, P]) for half in range(2)] for b in range(2)]
        stat = [m.sb(f"stat{b}", [P, 2]) for b in range(2)]
        RING = 6
        rec = [m.sb(f"rec{b}", [P, RECB]) for b in range(RING)]
        S = m.ps("S", [P, 4, 512])
        T = m.ps("T", [P, 2, 4, P])
        O = m.ps("O", [P, 2, 512])
        loaded, ones_set = m.sem("loaded"), m.sem("ones_set")
        w_in = [m.sem(f"w_in{b}") for b in range(2)]
        q_ready, q_out, q_t, q_rot, k_ready, k_out, v_ready, v_out = (
            m.sem(n) for n in ("q_ready", "q_out", "q_t", "q_rot", "k_ready", "k_out", "v_ready", "v_out"))
        s_ready, capped, maxed, negated, exped, t_ready, t_out_a, t_out_b, pv_ready, rec_out = (
            m.sem(n) for n in ("s_ready", "capped", "maxed", "negated", "exped", "t_ready", "t_out_a", "t_out_b",
                               "pv_ready", "rec_out"))
        q_stored, sp_ticks = m.sem("q_stored"), m.sem("sp_ticks")
        rec_stored = [m.sem(f"rec_stored{b}") for b in range(RING)]
        UNITS = [(i, 8 * c, min(i + 1 - 8 * c, 8)) for i in range(NT) for c in range(1 + i // 8)]
        NU = len(UNITS)
        assert NU % RING == 0
        HALF_B = [sum(k > 4 for _, _, k in UNITS[:u]) for u in range(NU + 1)]
        DIAG = [sum(j + k == i + 1 for i, j, k in UNITS[:u]) for u in range(NU + 1)]
        QCH = [(k * 512, 512) for k in range(4)] + [(SEQ, NS)]

        def q_bank(k):
            return S[:, k, :] if k < 4 else T[:, 0, 0, 0:NS]

        def each_head(eng, body):
            body(0, 0)
            body(1, 1)
            with eng.Fori(1, H // 2 - 1) as i:
                body(i * 2, 0)
                body(i * 2 + 1, 1)
            body(H - 2, 0)
            body(H - 1, 1)

        with nc.Block() as block:
            @block.sync
            def _(sp):
                load_latents(sp, t, cqT, ckvT, k96, rope, causal, loaded)
                load_head_weights(sp, t, 0, wq[0], wk[0], wv[0], w_in[0])

                def body(h, b):
                    if not isinstance(h, int) or h < H - 1:
                        held(sp, k_ready, h * 4, sp_ticks)
                        load_head_weights(sp, t, h + 1, wq[1 - b], wk[1 - b], wv[1 - b], w_in[1 - b])
                    held(sp, q_rot, h * 5 + 5, sp_ticks)
                    held(sp, q_out, h * 5 + 5, sp_ticks)
                    sp.dma_start(t["qs96"][ds(h, 1)].rearrange("o c n -> (o c) n"),
                                 q96[0:NOPE + ROPE, SEQ:TOK]).then_inc(q_stored, 16)
                    for u, (i, j, _) in enumerate(UNITS):
                        held(sp, rec_out, h * NU + u + 1, sp_ticks)
                        sp.dma_start(t["ob"][i * P:(i + 1) * P, j // 8, ds(h, 1), :].rearrange("i o e -> i (o e)"),
                                     rec[u % RING][:, :]).then_inc(rec_stored[u % RING], 16)

                each_head(sp, body)
                sp.wait_ge(q_stored, 16 * H)
                for b in range(RING):
                    sp.wait_ge(rec_stored[b], 16 * H * NU // RING)

            @block.gpsimd
            def _(pool):
                pool.memset(v[:, :, HD:HD + 1], 1.0)
                pool.memset(v[:, :, HD + 1:VB], 0.0).then_inc(ones_set, 1)

            @block.scalar
            def _(act):
                def body(h, b):
                    waits(act, q_stored, h * 16)
                    for k, (at, width) in enumerate(QCH):
                        act.wait_ge(q_ready, h * 5 + k + 1)
                        act.activation(q96[0:NOPE, at:at + width], q_bank(k)[0:NOPE, 0:width], ACT.Copy)\
                            .then_inc(q_out, 1)
                    for k in range(2):
                        act.wait_ge(v_ready, h * 2 + k + 1)
                        act.activation(v[:, 8 * k:8 * k + 8, 0:HD],
                                       O[:, k, :].rearrange("p (s c) -> p s c", c=HD), ACT.Copy).then_inc(v_out, 1)
                    for k in range(4):
                        act.wait_ge(k_ready, h * 4 + k + 1)
                        act.activation(k96[0:NOPE, k * 512:(k + 1) * 512], S[0:NOPE, k, :], ACT.Copy)\
                            .then_inc(k_out, 1)

                    def exps(u):
                        c, (i, j, nk) = h * NU + u, UNITS[u]
                        act.wait_ge(negated, c + 1)
                        waits(act, t_ready, (c - 1) * 2)
                        s2 = S[:, 2 * (u % 2):2 * (u % 2) + 2, :].rearrange("p a b -> p (a b)")
                        act.activation(p[u % 2][:, 0:nk * P], s2[:, 0:nk * P], ACT.Exp,
                                       bias=stat[u % 2][:, 1:2], scale=B_SCALE).then_inc(exped, 1)

                    def turn_out(u):
                        c, (_, _, nk) = h * NU + u, UNITS[u]
                        act.wait_ge(t_ready, c * 2 + 1)
                        waits(act, pv_ready, c - 1)
                        q = min(nk, 4)
                        act.activation(pT[u % 2][0][:, 0:q, :], T[:, 0, 0:q, :], ACT.Copy).then_inc(t_out_a, 1)

                    for u in range(NU + 2):
                        if u > 1:
                            turn_out(u - 2)
                        if u < NU:
                            exps(u)

                each_head(act, body)

            @block.vector
            def _(dve):
                dve.wait_ge(loaded, 96)

                def body(h, b):
                    for k, (at, width) in enumerate(QCH):
                        n = h * 5 + k
                        dve.wait_ge(q_ready, n + 1)
                        waits(dve, q_rot, n - 1)
                        if k == 4:
                            waits(dve, q_stored, h * 16)
                        src = slice(at, at + width)
                        r, sw = slice(NOPE, NOPE + ROPE), slice(NOPE + ROPE, P)
                        tb = turned[k % 2]
                        dve.tensor_tensor(tb[r, 0, 0:width], q_bank(k)[r, 0:width], rope[r, src], ALU.mult)
                        dve.tensor_tensor(tb[r, 1, 0:width], q_bank(k)[sw, 0:width], rope[sw, src], ALU.mult)\
                            .then_inc(q_t, 1)
                        dve.wait_ge(q_t, n + 1)
                        dve.tensor_tensor(q96[r, src], tb[r, 0, 0:width], tb[r, 1, 0:width], ALU.add)\
                            .then_inc(q_rot, 1)

                    def maxima(u):
                        c, (i, j, nk), b2 = h * NU + u, UNITS[u], u % 2
                        dve.wait_ge(s_ready, c + 1)
                        waits(dve, rec_stored[u % RING], (h * (NU // RING) + u // RING) * 16)
                        waits(dve, exped, c - 1)
                        s2 = S[:, 2 * b2:2 * b2 + 2, :].rearrange("p a b -> p (a b)")
                        if j + nk == i + 1:
                            diag = s2[:, (nk - 1) * P:nk * P]
                            dve.tensor_tensor(diag, diag, causal[:, :], ALU.add).then_inc(capped, 1)
                            dve.wait_ge(capped, h * DIAG[NU] + DIAG[u] + 1)
                        dve.tensor_reduce(stat[b2][:, 0:1], s2[:, 0:nk * P], AX.X, ALU.max).then_inc(maxed, 1)
                        dve.wait_ge(maxed, c + 1)
                        dve.tensor_scalar(stat[b2][:, 1:2], stat[b2][:, 0:1], -B_SCALE, None, ALU.mult)\
                            .then_inc(negated, 1)
                        dve.tensor_scalar(rec[u % RING][:, HD + 1:RECB], stat[b2][:, 0:1], B_SCALE, None, ALU.mult)

                    def turn_out(u):
                        c, (_, _, nk) = h * NU + u, UNITS[u]
                        if nk > 4:
                            dve.wait_ge(t_ready, c * 2 + 2)
                            waits(dve, pv_ready, c - 1)
                            dve.tensor_copy(pT[u % 2][1][:, 0:nk - 4, :], T[:, 1, 0:nk - 4, :]).then_inc(t_out_b, 1)

                    def record(u):
                        dve.wait_ge(pv_ready, h * NU + u + 1)
                        dve.tensor_copy(rec[u % RING][:, 0:HD + 1], O[:, u % 2, 0:HD + 1]).then_inc(rec_out, 1)

                    for u in range(NU + 3):
                        if u < NU:
                            maxima(u)
                        if 1 < u < NU + 2:
                            turn_out(u - 2)
                        if u > 2:
                            record(u - 3)

                each_head(dve, body)

            @block.tensor
            def _(pe):
                pe.wait_ge(loaded, 96)
                pe.wait_ge(ones_set, 1)

                def body(h, b):
                    pe.wait_ge(w_in[b], (h - b + 2) * 40)
                    for k, (at, width) in enumerate(QCH):
                        waits(pe, exped if k < 4 else t_out_a, h * NU)
                        for c in range(QL // P):
                            last = pe.matmul(q_bank(k)[:, 0:width], wq[b][:, c, :], cqT[:, c, at:at + width],
                                             start=c == 0, stop=c == QL // P - 1)
                        last.then_inc(q_ready, 1)
                    waits(pe, rec_out, h * NU)
                    for k in range(2):
                        for s in range(8):
                            at = (8 * k + s) * P
                            last = pe.matmul(O[:, k, s * HD:(s + 1) * HD], ckvT[:, at:at + P], wv[b][:, :],
                                             start=True, stop=True)
                        last.then_inc(v_ready, 1)
                    for k in range(4):
                        pe.wait_ge(q_out, h * 5 + k + 1)
                        pe.wait_ge(q_rot, h * 5 + k + 1)
                        pe.matmul(S[0:NOPE, k, :], wk[b][:, :], ckvT[:, k * 512:(k + 1) * 512],
                                  start=True, stop=True).then_inc(k_ready, 1)
                    pe.wait_ge(q_out, h * 5 + 5)
                    pe.wait_ge(q_rot, h * 5 + 5)
                    pe.wait_ge(k_out, h * 4 + 4)
                    pe.wait_ge(v_out, h * 2 + 2)

                    def scores(u):
                        c, (i, j, nk) = h * NU + u, UNITS[u]
                        if u > 1:
                            pe.wait_ge(exped, c - 1)
                        for a in range(0, nk, 4):
                            width = min(nk - a, 4) * P
                            last = pe.matmul(S[:, 2 * (u % 2) + a // 4, 0:width], q96[0:NOPE + ROPE, i * P:(i + 1) * P],
                                             k96[0:NOPE + ROPE, (j + a) * P:(j + a) * P + width],
                                             start=True, stop=True)
                        last.then_inc(s_ready, 1)

                    def turns(u):
                        c, (_, _, nk) = h * NU + u, UNITS[u]
                        pe.wait_ge(exped, c + 1)
                        waits(pe, t_out_a, c)
                        for k in range(min(nk, 4)):
                            last = pe.transpose(T[:, 0, k, :], p[u % 2][:, k * P:(k + 1) * P], ident[:, :])
                        if nk <= 4:
                            last.then_inc(t_ready, 2)
                            return
                        last.then_inc(t_ready, 1)
                        waits(pe, t_out_b, h * HALF_B[NU] + HALF_B[u])
                        for k in range(4, nk):
                            last = pe.transpose(T[:, 1, k - 4, :], p[u % 2][:, k * P:(k + 1) * P], ident[:, :])
                        last.then_inc(t_ready, 1)

                    def values(u):
                        c, (_, j, nk) = h * NU + u, UNITS[u]
                        pe.wait_ge(t_out_a, c + 1)
                        if nk > 4:
                            pe.wait_ge(t_out_b, h * HALF_B[NU] + HALF_B[u] + 1)
                        if u > 1:
                            pe.wait_ge(rec_out, c - 1)
                        for k in range(nk):
                            last = pe.matmul(O[:, u % 2, 0:VB], pT[u % 2][k // 4][:, k % 4, :], v[:, j + k, :],
                                             start=k == 0, stop=k == nk - 1)
                        last.then_inc(pv_ready, 1)

                    for u in range(NU + 3):
                        if u < NU:
                            scores(u)
                        if 1 < u < NU + 2:
                            turns(u - 2)
                        if u > 2:
                            values(u - 3)

                each_head(pe, body)


def stage_sample_dilated(nc, t, ident):
    with ExitStack() as ctx:
        m = Mem(nc, ctx, "sdil")
        R = DT * H
        kv = [m.sb(f"kv{b}", [P, DT, NG, 2, AW]) for b in range(2)]
        qb = [m.sb(f"qb{b}", [P, DT, NG, AW]) for b in range(2)]
        row = [m.sb(f"row{b}", [R, 3, NG, HD]) for b in range(2)]
        prod = [m.sb(f"prod{b}", [P, NG, AW]) for b in range(2)]
        st = m.sb("st", [P, NG, R])
        sr = m.sb("sr", [R, NG * P + NG])
        selfp = m.sb("selfp", [R, NG, HD])
        bias = m.sb("bias", [R, NG, P])
        stat = m.sb("stat", [R, 4])
        own = m.sb("own", [R, 2, HD])
        own3 = m.sb("own3", [R, NG, HD])
        pT = m.sb("pT", [P, NG, R])
        ownT = m.sb("ownT", [P, R])
        oT = m.sb("oT", [P, 4, NS])
        tS = m.ps("tS", [P, 512])
        tP = m.ps("tP", [P, 512])
        tO = m.ps("tO", [P, 512])
        pO = m.ps("pO", [P, 512])
        bias_in, kv_in = m.sem("bias_in"), [m.sem(f"kv_in{b}") for b in range(2)]
        prod_ready, dotted, st_turned, biased, own_scored = (
            m.sem(n) for n in ("prod_ready", "dotted", "st_turned", "biased", "own_scored"))
        maxed, negated, exped, inverted, scaled, p_turned, pT_out = (
            m.sem(n) for n in ("maxed", "negated", "exped", "inverted", "scaled", "p_turned", "pT_out"))
        own_mult, own_added, own_copied, own_turned, ownT_out, pv_ready, o_copied, o_added = (
            m.sem(n) for n in ("own_mult", "own_added", "own_copied", "own_turned", "ownT_out", "pv_ready",
                               "o_copied", "o_added"))
        selfm, sp_ticks, pe_ticks, stored = (m.sem(n) for n in ("selfm", "sp_ticks", "pe_ticks", "stored"))
        PER = 9 + DT + DT * NG + 2 * (DT - 1)

        def each_pair(eng, body):
            body(0, 0)
            body(1, 1)
            with eng.Fori(1, DB // 2) as i:
                body(i * 2, 0)
                body(i * 2 + 1, 1)

        with nc.Block() as block:
            @block.sync
            def _(sp):
                sp.dma_start(bias[:, :, :], t["sample_alibi"][0:R]).then_inc(bias_in, 16)

                def body(b, f):
                    held(sp, o_added, (b - 1) * 2, sp_ticks)
                    count = 0
                    for which in range(3):
                        for g in range(NG):
                            src = t["hs"][ds(b * DT, DT), which * QKV + g * AW:which * QKV + (g + 1) * AW]
                            sp.dma_start(row[f][:, which, g, :], src.rearrange("t (h d) -> t h d", h=H))\
                                .then_inc(kv_in[f], 16)
                            count += 1
                    for tk in range(DT):
                        src = t["hs"][ds(b * DT + tk, 1), 0:QKV]
                        sp.dma_start(qb[f][:, tk, :, :].rearrange("p g c -> p (g c)"),
                                     src.rearrange("o n -> (o n)").partition_broadcast(P)).then_inc(kv_in[f], 16)
                        count += 1
                        for g, (win, dil) in enumerate(GROUPS):
                            state = t[f"state_win{g}"]
                            old = P - tk if dil == 1 else P
                            src = state[ds(b, 1), tk:tk + dil * (old - 1) + 1:dil, :, :]
                            sp.dma_start(kv[f][0:old, tk, g, :, :], src.rearrange("o i c n -> (o i) c n"))\
                                .then_inc(kv_in[f], 16)
                            count += 1
                            if old < P:
                                for which in (1, 2):
                                    src = t["hs"][ds(b * DT, tk), which * QKV + g * AW:which * QKV + (g + 1) * AW]
                                    sp.dma_start(kv[f][old:P, tk, g, which - 1, :], src).then_inc(kv_in[f], 16)
                                    count += 1
                    assert count == PER

                each_pair(sp, body)
                sp.wait_ge(o_added, 2 * DB)
                for c in range(4):
                    sp.dma_start(t["oaT_s"][c], oT[:, c, :]).then_inc(stored, 16)
                sp.wait_ge(stored, 64)

            @block.gpsimd
            def _(pool):
                def body(b, f):
                    pool.wait_ge(kv_in[f], (b - f + 2) * (8 * PER))
                    for tk in range(DT):
                        n = b * DT + tk
                        waits(pool, dotted, n - 1)
                        pool.tensor_tensor(prod[tk % 2][:, :, :], qb[f][:, tk, :, :], kv[f][:, tk, :, 0, :],
                                           ALU.mult).then_inc(prod_ready, 1)

                each_pair(pool, body)

            @block.vector
            def _(dve):
                dve.wait_ge(bias_in, 16)

                def dots(b, f):
                    for tk in range(DT):
                        n = b * DT + tk
                        dve.wait_ge(prod_ready, n + 1)
                        if tk == 0:
                            waits(dve, st_turned, b)
                        dve.tensor_reduce(st[:, :, tk * H:(tk + 1) * H],
                                          prod[tk % 2][:, :, :].rearrange("p g (h d) -> p g h d", h=H),
                                          AX.X, ALU.add).then_inc(dotted, 1)

                def softmax(b, f):
                    dve.wait_ge(kv_in[f], (b - f + 2) * (8 * PER))
                    dve.tensor_tensor(selfp[:, :, :], row[f][:, 0, :, :], row[f][:, 1, :, :], ALU.mult)\
                        .then_inc(selfm, 1)
                    dve.wait_ge(selfm, b + 1)
                    waits(dve, own_added, b * 3)
                    dve.tensor_reduce(stat[:, 0:NG], selfp[:, :, :], AX.X, ALU.add).then_inc(own_scored, 1)
                    dve.wait_ge(own_scored, b + 1)
                    waits(dve, p_turned, b)
                    dve.tensor_scalar(sr[:, NG * P:NG * P + NG], stat[:, 0:NG], A_SCALE, None, ALU.mult)
                    dve.wait_ge(st_turned, b + 1)
                    dve.scalar_tensor_tensor(sr[:, 0:NG * P], tS[0:R, 0:NG * P], A_SCALE,
                                             bias[:, :, :].rearrange("p g k -> p (g k)"), ALU.mult, ALU.add)\
                        .then_inc(biased, 1)
                    dve.wait_ge(biased, b + 1)
                    dve.tensor_reduce(stat[:, 0:1], sr[:, :], AX.X, ALU.max).then_inc(maxed, 1)
                    dve.wait_ge(maxed, b + 1)
                    dve.tensor_scalar(stat[:, 1:2], stat[:, 0:1], -1.0, None, ALU.mult).then_inc(negated, 1)
                    dve.wait_ge(exped, b + 1)
                    dve.reciprocal(stat[:, 3:4], stat[:, 2:3]).then_inc(inverted, 1)
                    dve.wait_ge(inverted, b + 1)
                    dve.tensor_scalar(sr[:, :], sr[:, :], stat[:, 3:4], None, ALU.mult).then_inc(scaled, 1)
                    dve.wait_ge(scaled, b + 1)
                    waits(dve, own_turned, b)
                    for g in range(NG):
                        dve.tensor_scalar(own3[:, g, :], row[f][:, 2, g, :], sr[:, NG * P + g:NG * P + g + 1], None,
                                          ALU.mult).then_inc(own_mult, 1)
                    dve.wait_ge(own_mult, (b + 1) * 3)
                    dve.tensor_tensor(own[:, 0, :], own3[:, 0, :], own3[:, 1, :], ALU.add).then_inc(own_added, 1)
                    dve.wait_ge(own_added, b * 3 + 1)
                    dve.tensor_tensor(own[:, 1, :], own[:, 0, :], own3[:, 2, :], ALU.add).then_inc(own_added, 1)
                    dve.wait_ge(own_added, b * 3 + 2)
                    dve.tensor_copy(own[:, 0, :], own[:, 1, :]).then_inc(own_added, 1)

                def outputs(b, f):
                    dve.wait_ge(ownT_out, b + 1)
                    dve.wait_ge(pv_ready, b + 1)
                    for h in range(2):
                        r = slice(h * HD, (h + 1) * HD)
                        dve.tensor_tensor(oT[r, :, ds(b * DT, DT)],
                                          pO[r, 0:DT * 8].rearrange("p (k c s) -> p c k s", k=DT, c=4)[:, :, :, h],
                                          ownT[r, :].rearrange("p (k c s) -> p c k s", k=DT, c=4)[:, :, :, h],
                                          ALU.add).then_inc(o_added, 1)

                def body(b, f):
                    dots(b, f)
                    softmax(b, f)
                    outputs(b, f)

                each_pair(dve, body)

            @block.scalar
            def _(act):
                def body(b, f):
                    act.wait_ge(negated, b + 1)
                    act.activation(sr[:, :], sr[:, :], ACT.Exp, bias=stat[:, 1:2], accum_out=stat[:, 2:3])\
                        .then_inc(exped, 1)
                    act.wait_ge(p_turned, b + 1)
                    waits(act, pv_ready, b)
                    act.activation(pT[:, :, :], tP[:, 0:NG * R].rearrange("p (g r) -> p g r", g=NG), ACT.Copy)\
                        .then_inc(pT_out, 1)
                    act.wait_ge(own_turned, b + 1)
                    waits(act, o_added, b * 2)
                    act.activation(ownT[:, :], tO[:, 0:R], ACT.Copy).then_inc(ownT_out, 1)

                each_pair(act, body)

            @block.tensor
            def _(pe):
                def body(b, f):
                    pe.wait_ge(dotted, (b + 1) * DT)
                    waits(pe, biased, b)
                    for g in range(NG):
                        last = pe.transpose(tS[0:R, g * P:(g + 1) * P], st[:, g, :], ident[:, :])
                    last.then_inc(st_turned, 1)
                    pe.wait_ge(scaled, b + 1)
                    waits(pe, pT_out, b)
                    pe.sem_inc(pe_ticks, 1)
                    for g in range(NG):
                        last = pe.transpose(tP[:, g * R:(g + 1) * R], sr[:, g * P:(g + 1) * P], ident[0:R, 0:R])
                    last.then_inc(p_turned, 1)
                    pe.wait_ge(own_added, b * 3 + 3)
                    waits(pe, ownT_out, b)
                    pe.sem_inc(pe_ticks, 1)
                    pe.transpose(tO[:, 0:R], own[:, :, :].rearrange("p a d -> p (a d)"), ident[0:R, 0:R])\
                        .then_inc(own_turned, 1)
                    pe.wait_ge(pT_out, b + 1)
                    waits(pe, o_added, b * 2)
                    for tk in range(DT):
                        for c in range(4):
                            for g in range(NG):
                                last = pe.matmul(pO[:, tk * H + 2 * c:tk * H + 2 * c + 2],
                                                 kv[f][:, tk, g, 1, c * P:(c + 1) * P],
                                                 pT[:, g, tk * H + 2 * c:tk * H + 2 * c + 2],
                                                 start=g == 0, stop=g == NG - 1)
                    last.then_inc(pv_ready, 1)

                each_pair(pe, body)


def stage_sample_latent(nc, t, ident):
    with ExitStack() as ctx:
        m = Mem(nc, ctx, "slat")
        R = H * DT
        GP = 4
        NGP = NPG // GP
        table = m.sb("table", [1, DB * NPG], I32)
        ckv = [m.sb(f"ckv{b}", [P, NPG, KL]) for b in range(2)]
        kpe = [m.sb(f"kpe{b}", [P, NPG, ROPE]) for b in range(2)]
        new = [m.sb(f"new{b}", [DT, KL]) for b in range(2)]
        q64 = m.sb("q64", [NOPE, H, NS])
        qpe = m.sb("qpe", [P, H, NS])
        wuk = m.sb("wuk", [P, AW])
        wuv = m.sb("wuv", [P, AW])
        wukT = m.sb("wukT", [NOPE, H, P])
        qlat = m.sb("qlat", [P, H, NS])
        newT = m.sb("newT", [P, NS])
        newpT = m.sb("newpT", [ROPE, NS])
        mask = m.sb("mask", [DT, R])
        qc = [m.sb(f"qc{b}", [P, R]) for b in range(2)]
        qz = [m.sb(f"qz{b}", [P, GP, R]) for b in range(2)]
        nc_ = [m.sb(f"nc{b}", [P, DT]) for b in range(2)]
        np_ = [m.sb(f"np{b}", [ROPE, DT]) for b in range(2)]
        cT = [m.sb(f"cT{b}", [P, GP, P]) for b in range(2)]
        pTt = [m.sb(f"pTt{b}", [P, P]) for b in range(2)]
        sx = m.sb("sx", [P, NPG + 1, R])
        pr = m.sb("pr", [P, NPG + 1, R])
        top = m.sb("top", [P, R])
        rmax = m.sb("rmax", [R, 4])
        rmaxb = m.sb("rmaxb", [R, P])
        mb = m.sb("mb", [P, R])
        ones = m.sb("ones", [P, 1])
        psumx = m.sb("psumx", [P, R])
        ol = m.sb("ol", [R, KL])
        olT = m.sb("olT", [P, H, NS])
        obT = m.sb("obT", [P, 4, NS])
        tc_ = [m.ps(f"tc{b}", [P, 512]) for b in range(2)]
        S = m.ps("S", [P, 2, 512])
        X = m.ps("X", [P, 512])
        N = m.ps("N", [P, 512])
        OL = m.ps("OL", [P, 512])
        sems = ("loaded", "ones_set", "uk_turned", "uk_out", "ql_ready", "ql_out", "c_turned", "c_out", "s_ready",
                "sx_out", "new_out", "topped", "top_turned", "rmaxed", "rmax_wide", "mb_turned", "mb_out", "centred",
                "exped", "p_summed", "ol_ready", "inverted", "ol_scaled", "ol_turned", "olT_out", "q_laid",
                "ob_ready", "ob_out", "stored", "x_turned", "x_out", "n_ready", "zeroed", "table_in", "sp_ticks", "pool_ticks", "pe_ticks")
        s = {n: m.sem(n) for n in sems}
        ckv_in = [m.sem(f"ckv_in{b}") for b in range(2)]
        kpe_in = [m.pool_sem(f"kpe_in{b}") for b in range(2)]
        HALF = NGP // 2

        def each_pair(eng, body):
            body(0, 0)
            body(1, 1)
            with eng.Fori(1, DB // 2 - 1) as i:
                body(i * 2, 0)
                body(i * 2 + 1, 1)
            body(DB - 2, 0)
            body(DB - 1, 1)

        AT_ONCE = 4

        ACT_PAGES = 8

        def load_pages(eng, b, f, cache, dst, landed, first=0, last=NPG):
            with eng.Fori(first // AT_ONCE, last // AT_ONCE) as i:
                numbers = [eng.value_load(table[0:1, ds(b * NPG + i * AT_ONCE + k, 1)], min_val=0,
                                          max_val=t[cache].shape[0] - 1) for k in range(AT_ONCE)]
                for k, number in enumerate(numbers):
                    eng.dma_start(dst[f][:, ds(i * AT_ONCE + k, 1), :].rearrange("p o c -> p (o c)"),
                                  t[cache][ds(number, 1)].rearrange("o s c -> (o s) c")).then_inc(landed[f], 16)

        with nc.Block() as block:
            @block.sync
            def _(sp):
                ld = s["loaded"]
                sp.dma_start(table[:, :], t["page_table"].rearrange("b n -> (b n)").unsqueeze(0))\
                    .then_inc(s["table_in"], 16)
                sp.dma_start(q64[:, :, :], t["qs96"][:, 0:NOPE, :].rearrange("h c n -> c h n")).then_inc(ld, 16)
                for j in range(GP):
                    sp.dma_start(qpe[j * ROPE:(j + 1) * ROPE, :, :],
                                 t["qs96"][:, NOPE:NOPE + ROPE, :].rearrange("h c n -> c h n")).then_inc(ld, 16)
                sp.dma_start(wuk[:, :], t["w_uk"].rearrange("c h d -> c (h d)")).then_inc(ld, 16)
                sp.dma_start(wuv[:, :], t["w_uv"].rearrange("c h d -> c (h d)")).then_inc(ld, 16)
                sp.dma_start(newT[:, :], t["ckvT"][:, SEQ:TOK]).then_inc(ld, 16)
                sp.dma_start(newpT[:, :], t["kpeT"][:, SEQ:TOK]).then_inc(ld, 16)
                sp.dma_start(mask[:, :], t["sample_causal"]).then_inc(ld, 16)
                sp.wait_ge(s["table_in"], 16)

                def body(b, f):
                    held(sp, s["ol_ready"], b - 1, s["sp_ticks"])
                    sp.dma_start(new[f][:, :], t["ckv_sample"][ds(b * DT, DT), :]).then_inc(ckv_in[f], 16)

                    load_pages(sp, b, f, "cache_ckv", ckv, ckv_in, 0, NPG - ACT_PAGES)

                each_pair(sp, body)
                sp.wait_ge(s["ob_out"], 2)
                for c in range(4):
                    sp.dma_start(t["obT_s"][c], obT[:, c, :]).then_inc(s["stored"], 16)
                sp.wait_ge(s["stored"], 64)

            @block.gpsimd
            def _(pool):
                pool.memset(ones[:, :], 1.0).then_inc(s["ones_set"], 1)
                pool.memset(sx[:, NPG:NPG + 1, :], NEG).then_inc(s["ones_set"], 1)
                for f in range(2):
                    pool.memset(qz[f][:, :, :], 0.0).then_inc(s["zeroed"], 1)
                pool.wait_ge(s["table_in"], 16)

                def body(b, f):
                    held(pool, s["ol_ready"], b - 1, s["pool_ticks"])
                    load_pages(pool, b, f, "cache_kpe", kpe, kpe_in)

                each_pair(pool, body)

            @block.scalar
            def _(act):
                act.wait_ge(s["table_in"], 16)
                load_pages(act, 0, 0, "cache_ckv", ckv, ckv_in, NPG - ACT_PAGES)
                act.wait_ge(s["uk_turned"], 1)
                act.activation(wukT[:, 0:4, :], tc_[0][0:NOPE, :].rearrange("p (h c) -> p h c", h=4), ACT.Copy)
                act.activation(wukT[:, 4:8, :], tc_[1][0:NOPE, :].rearrange("p (h c) -> p h c", h=4), ACT.Copy)\
                    .then_inc(s["uk_out"], 1)
                act.wait_ge(s["ql_ready"], 1)
                act.activation(qlat[:, :, :], S[:, 0, 0:H * NS].rearrange("p (h k) -> p h k", h=H), ACT.Copy)\
                    .then_inc(s["ql_out"], 1)

                def body(b, f):
                    for k in range(NGP):
                        n = b * NGP + k
                        act.wait_ge(s["c_turned"], n + 1)
                        waits(act, s["s_ready"], n - 1)
                        act.activation(cT[k % 2][:, :, :], tc_[k % 2][:, :].rearrange("p (g k) -> p g k", g=GP),
                                       ACT.Copy).then_inc(s["c_out"], 1)
                    act.wait_ge(s["top_turned"], b + 1)
                    act.wait_ge(s["mb_turned"], b + 1)
                    waits(act, s["centred"], b * 2)
                    act.activation(mb[:, :], N[:, P * 2:P * 2 + R], ACT.Copy).then_inc(s["mb_out"], 1)
                    act.wait_ge(s["centred"], b * 2 + 2)
                    waits(act, s["ol_ready"], b)
                    act.activation(pr[:, :, :], sx[:, :, :], ACT.Exp, scale=B_SCALE).then_inc(s["exped"], 1)
                    if not isinstance(b, int) or b < DB - 1:
                        load_pages(act, b + 1, 1 - f, "cache_ckv", ckv, ckv_in, NPG - ACT_PAGES)
                    act.wait_ge(s["ol_turned"], b + 1)
                    act.activation(olT[:, :, ds(b * DT, DT)], N[:, P * 3:P * 3 + R].rearrange("p (h k) -> p h k", h=H),
                                   ACT.Copy).then_inc(s["olT_out"], 1)

                each_pair(act, body)
                act.wait_ge(s["ob_ready"], 1)
                act.activation(obT[:, :, :], X[:, 0:4 * NS].rearrange("p (c k) -> p c k", c=4), ACT.Copy)\
                    .then_inc(s["ob_out"], 2)

            @block.vector
            def _(dve):
                dve.wait_ge(s["loaded"], 16 * 10)
                dve.wait_ge(s["ones_set"], 2)
                dve.wait_ge(s["zeroed"], 2)
                dve.wait_ge(s["ql_out"], 1)

                def lay_queries(b, f):
                    waits(dve, s["n_ready"], b - 1)
                    at = ds(b * DT, DT)
                    dve.tensor_copy(qc[f][:, :].rearrange("p (h k) -> p h k", h=H), qlat[:, :, at])
                    dve.tensor_copy(nc_[f][:, :], newT[:, at])
                    dve.tensor_copy(np_[f][:, :], newpT[:, at])
                    for j in range(GP):
                        r = slice(j * ROPE, (j + 1) * ROPE)
                        last = dve.tensor_copy(qz[f][r, j, :].rearrange("p (h k) -> p h k", h=H), qpe[r, :, at])
                    last.then_inc(s["q_laid"], 1)

                def body(b, f):
                    lay_queries(b, f)
                    for k in range(NGP):
                        n = b * NGP + k
                        dve.wait_ge(s["x_turned"], n + 1)
                        waits(dve, s["s_ready"], n - 1)
                        dve.tensor_copy(pTt[k % 2][:, :], X[:, (k % 2) * P:(k % 2) * P + P]).then_inc(s["x_out"], 1)
                    waits(dve, s["exped"], b)
                    dve.wait_ge(s["s_ready"], (b + 1) * NGP)
                    for k in range(2):
                        dve.tensor_copy(sx[:, k * 16:(k + 1) * 16, :], S[:, k, :].rearrange("p (g r) -> p g r", g=16))\
                            .then_inc(s["sx_out"], 1)
                    dve.wait_ge(s["n_ready"], b + 1)
                    dve.tensor_tensor(sx[0:DT, NPG, :], N[0:DT, 0:R], mask[:, :], ALU.add).then_inc(s["new_out"], 1)
                    dve.wait_ge(s["sx_out"], (b + 1) * 2)
                    dve.wait_ge(s["new_out"], b + 1)
                    dve.tensor_reduce(top[:, :], sx[:, :, :].rearrange("p g r -> p r g"), AX.X, ALU.max)\
                        .then_inc(s["topped"], 1)
                    dve.wait_ge(s["top_turned"], b + 1)
                    dve.tensor_reduce(rmax[:, 0:1], N[0:R, P:2 * P], AX.X, ALU.max).then_inc(s["rmaxed"], 1)
                    dve.wait_ge(s["rmaxed"], b + 1)
                    dve.tensor_copy(rmaxb[:, :], rmax[:, 0:1].to_broadcast([R, P])).then_inc(s["rmax_wide"], 1)
                    dve.wait_ge(s["mb_out"], b + 1)
                    dve.tensor_tensor(sx[:, 0:NPG, :], sx[:, 0:NPG, :],
                                      mb[:, :].unsqueeze(1).to_broadcast([P, NPG, R]), ALU.subtract)\
                        .then_inc(s["centred"], 1)
                    dve.tensor_tensor(sx[0:DT, NPG, :], sx[0:DT, NPG, :], mb[0:DT, :], ALU.subtract)\
                        .then_inc(s["centred"], 1)
                    dve.wait_ge(s["exped"], b + 1)
                    dve.tensor_reduce(psumx[:, :], pr[:, :, :].rearrange("p g r -> p r g"), AX.X, ALU.add)\
                        .then_inc(s["p_summed"], 1)
                    dve.wait_ge(s["ol_ready"], b + 1)
                    dve.reciprocal(rmax[:, 1:2], OL[0:R, KL:KL + 1]).then_inc(s["inverted"], 1)
                    dve.wait_ge(s["inverted"], b + 1)
                    dve.tensor_scalar(ol[:, :], OL[0:R, 0:KL], rmax[:, 1:2], None, ALU.mult)\
                        .then_inc(s["ol_scaled"], 1)

                each_pair(dve, body)

            @block.tensor
            def _(pe):
                pe.wait_ge(s["loaded"], 16 * 10)
                pe.wait_ge(s["ones_set"], 2)
                for h in range(H):
                    last = pe.transpose(tc_[h // 4][0:NOPE, (h % 4) * P:(h % 4 + 1) * P],
                                        wuk[:, h * NOPE:(h + 1) * NOPE], ident[:, :])
                last.then_inc(s["uk_turned"], 1)
                pe.wait_ge(s["uk_out"], 1)
                for h in range(H):
                    last = pe.matmul(S[:, 0, h * NS:(h + 1) * NS], wukT[:, h, :], q64[:, h, :], start=True, stop=True)
                last.then_inc(s["ql_ready"], 1)
                pe.wait_ge(s["ql_out"], 1)

                def body(b, f):
                    pe.wait_ge(ckv_in[f], (b - f + 2) * 8 * (NPG + 1))
                    pe.wait_ge(kpe_in[f], (b - f + 2) * 8 * NPG)
                    pe.wait_ge(s["q_laid"], b + 1)

                    def turns(k):
                        n = b * NGP + k
                        waits(pe, s["c_out"], n - 1)
                        for j in range(GP):
                            last = pe.transpose(tc_[k % 2][:, j * P:(j + 1) * P], ckv[f][:, k * GP + j, :],
                                                ident[:, :])
                        last.then_inc(s["c_turned"], 1)
                        waits(pe, s["x_out"], n)
                        pe.transpose(X[:, (k % 2) * P:(k % 2) * P + P],
                                     kpe[f][:, k * GP:(k + 1) * GP, :].rearrange("p g r -> p (g r)"), ident[:, :])\
                            .then_inc(s["x_turned"], 1)

                    def scores(k):
                        n = b * NGP + k
                        pe.wait_ge(s["c_out"], n + 1)
                        pe.wait_ge(s["x_out"], n + 1)
                        if k == 0:
                            waits(pe, s["sx_out"], b * 2)
                        bank, at = k // HALF, (k % HALF) * GP * R
                        pe.matmul(S[:, bank, at:at + GP * R], pTt[k % 2][:, :],
                                  qz[f][:, :, :].rearrange("p g r -> p (g r)"), start=True, stop=False,
                                  skip_group_check=True)
                        for j in range(GP):
                            last = pe.matmul(S[:, bank, at + j * R:at + (j + 1) * R], cT[k % 2][:, j, :], qc[f][:, :],
                                             start=False, stop=True, skip_group_check=True)
                        last.then_inc(s["s_ready"], 1)

                    for k in range(NGP + 1):
                        if k < NGP:
                            turns(k)
                        if k:
                            scores(k - 1)
                    waits(pe, s["olT_out"], b)
                    pe.matmul(N[0:DT, 0:R], nc_[f][:, :], qc[f][:, :], start=True, stop=False)
                    pe.matmul(N[0:DT, 0:R], np_[f][:, :], qz[f][0:ROPE, 0, :], start=False, stop=True)\
                        .then_inc(s["n_ready"], 1)
                    pe.wait_ge(s["topped"], b + 1)
                    pe.transpose(N[0:R, P:2 * P], top[:, :], ident[:, :]).then_inc(s["top_turned"], 1)
                    pe.wait_ge(s["rmax_wide"], b + 1)
                    pe.sem_inc(s["pe_ticks"], 1)
                    pe.transpose(N[:, 2 * P:2 * P + R], rmaxb[:, :], ident[0:R, 0:R]).then_inc(s["mb_turned"], 1)
                    pe.wait_ge(s["exped"], b + 1)
                    waits(pe, s["ol_scaled"], b)
                    for k in range(NPG):
                        pe.matmul(OL[0:R, 0:KL], pr[:, k, :], ckv[f][:, k, :], start=k == 0, stop=False)
                    pe.matmul(OL[0:R, 0:KL], pr[0:DT, NPG, :], new[f][:, :], start=False, stop=True)
                    pe.wait_ge(s["p_summed"], b + 1)
                    pe.matmul(OL[0:R, KL:KL + 1], psumx[:, :], ones[:, :], start=True, stop=True)\
                        .then_inc(s["ol_ready"], 1)
                    pe.wait_ge(s["ol_scaled"], b + 1)
                    pe.sem_inc(s["pe_ticks"], 1)
                    pe.transpose(N[:, 3 * P:3 * P + R], ol[:, :], ident[0:R, 0:R]).then_inc(s["ol_turned"], 1)

                each_pair(pe, body)
                pe.wait_ge(s["olT_out"], DB)
                for h in range(H):
                    r = slice((h % 2) * HD, (h % 2 + 1) * HD)
                    last = pe.matmul(X[r, (h // 2) * NS:(h // 2 + 1) * NS], wuv[:, h * HD:(h + 1) * HD], olT[:, h, :],
                                     start=True, stop=True)
                last.then_inc(s["ob_ready"], 1)


def stage_join(nc, t, ident, wraw):
    with ExitStack() as ctx:
        m = Mem(nc, ctx, "join")
        oa = [m.sb(f"oa{b}", [P, NG, 4, REC]) for b in range(2)]
        ob = [m.sb(f"ob{b}", [P, 2, H, RECB]) for b in range(2)]
        gz = [m.sb(f"gz{b}", [P, 8, P]) for b in range(2)]
        us = m.sb("us", [P, 3, 8, NS])
        big = m.sb("big", [P, NG * H, HD])
        part = m.sb("part", [P, H, HD])
        mx = m.sb("mx", [P, 2, H])
        wt = m.sb("wt", [P, 2, NG * H])
        sl = m.sb("sl", [P, NG * H])
        sums = m.sb("sums", [P, 2, H])
        nat = [m.sb(f"nat{b}", [P, 2, AW]) for b in range(2)]
        uT = [m.sb(f"uT{b}", [P, 8, P]) for b in range(2)]
        tp = [m.ps(f"tp{b}", [P, 8, P]) for b in range(2)]
        oin = [m.sem(f"in{b}") for b in range(2)]
        gz_in = [m.sem(f"gz_in{b}") for b in range(2)]
        us_in, us_out, step, expin, exped, nat_ready, tp_ready, u_ready, sp_ticks = (
            m.sem(n) for n in ("us_in", "us_out", "step", "expin", "exped", "nat_ready", "tp_ready", "u_ready",
                               "sp_ticks"))
        stored = [m.pool_sem(f"stored{b}") for b in range(2)]
        us_stored, w_in = m.sem("us_stored"), m.pool_sem("w_in")
        HALF = NT // 2
        STEPS = {1: 11, 2: 16}
        EXPS = {1: 1, 2: 2}

        def each_tile(eng, body):
            body(0, 0, 1)
            body(1, 1, 1)
            with eng.Fori(1, HALF // 2) as i:
                body(i * 2, 0, 1)
                body(i * 2 + 1, 1, 1)
            with eng.Fori(HALF // 2, HALF) as i:
                body(i * 2, 0, 2)
                body(i * 2 + 1, 1, 2)

        def before(i, chunks, per):
            return i * per[1] if chunks == 1 else (i - HALF) * per[2] + HALF * per[1]

        with nc.Block() as block:
            @block.sync
            def _(sp):
                for k, name in enumerate(("oaT_s", "obT_s")):
                    sp.dma_start(us[:, 0, 4 * k:4 * k + 4, :], t[name].rearrange("c p n -> p c n")).then_inc(us_in, 16)
                sp.dma_start(us[:, 1, :, :], t["gates"][0:8, :, SEQ:TOK].rearrange("k p n -> p k n")).then_inc(us_in, 16)

                def body(i, b, chunks):
                    held(sp, nat_ready, i - 1, sp_ticks)
                    rows = ds(i * P, P)
                    sp.dma_start(oa[b][:, :, :, :], t["oa"][rows]).then_inc(oin[b], 16)
                    sp.dma_start(ob[b][:, 0:chunks, :, :], t["ob"][rows, 0:chunks]).then_inc(oin[b], 16)
                    held(sp, u_ready, i - 1, sp_ticks)
                    sp.dma_start(gz[b][:, :, :], t["gates"][0:8, :, rows].rearrange("k p n -> p k n"))\
                        .then_inc(gz_in[b], 16)

                each_tile(sp, body)
                sp.wait_ge(us_out, 1)
                sp.dma_start(t["uT"][:, :, SEQ:TOK].rearrange("k p n -> p k n"), us[:, 2, :, :]).then_inc(us_stored, 16)
                sp.wait_ge(us_stored, 16)

            @block.gpsimd
            def _(pool):
                pool.wait_ge(nat_ready, 1)
                for k, name in enumerate(("w_proj_a", "w_proj_b")):
                    pool.dma_start(wraw[:, 4 * k:4 * k + 4, :], t[name].rearrange("(c p) n -> p c n", p=P))\
                        .then_inc(w_in, 16)

                def body(i, b, chunks):
                    pool.wait_ge(u_ready, i + 1)
                    pool.dma_start(t["uT"][:, :, ds(i * P, P)].rearrange("k p n -> p k n"), uT[b][:, :, :])\
                        .then_inc(stored[b], 16)

                each_tile(pool, body)
                for b in range(2):
                    pool.wait_ge(stored[b], 16 * HALF)
                pool.wait_ge(w_in, 32)

            @block.scalar
            def _(act):
                def body(i, b, chunks):
                    for k in range(chunks):
                        n = before(i, chunks, EXPS) + k
                        act.wait_ge(expin, n + 1)
                        width = NG * H if k == 0 else 2 * H
                        act.activation(wt[:, k, 0:width], wt[:, k, 0:width], ACT.Exp).then_inc(exped, 1)

                each_tile(act, body)

            @block.vector
            def _(dve):
                dve.wait_ge(us_in, 48)
                dve.tensor_tensor(us[:, 2, :, :], us[:, 0, :, :], us[:, 1, :, :], ALU.mult).then_inc(us_out, 1)

                def body(i, b, chunks):
                    first = before(i, chunks, STEPS)
                    count = [0]

                    def then(ins):
                        count[0] += 1
                        ins.then_inc(step, 1)
                        dve.wait_ge(step, first + count[0])

                    def join(k, groups, o, sums_of, maxima, out):
                        def heads(ap):
                            return ap.rearrange("p (c s) -> p c s", s=2) if groups == NG else ap

                        w3 = [heads(wt[:, k, g * H:(g + 1) * H]) for g in range(groups)]
                        s3 = [heads(sl[:, g * H:(g + 1) * H]) for g in range(groups)]
                        top = heads(mx[:, k, :])
                        then(dve.tensor_tensor(top, maxima[0], maxima[1], ALU.max))
                        if groups == 3:
                            then(dve.tensor_tensor(top, top, maxima[2], ALU.max))
                        for g in range(groups):
                            last = dve.tensor_tensor(w3[g], maxima[g], top, ALU.subtract)
                        last.then_inc(expin, 1)
                        dve.wait_ge(exped, before(i, chunks, EXPS) + k + 1)
                        for g in range(groups):
                            last = dve.tensor_tensor(s3[g], w3[g], sums_of[g], ALU.mult)
                        then(last)
                        then(dve.tensor_reduce(sums[:, k, :], sl[:, 0:groups * H].rearrange("p (g h) -> p h g", h=H),
                                               AX.X, ALU.add))
                        then(dve.reciprocal(sums[:, k, :], sums[:, k, :]))
                        for g in range(groups):
                            last = dve.tensor_tensor(w3[g], w3[g], heads(sums[:, k, :]), ALU.mult)
                        then(last)
                        o3 = big[:, 0:groups * H, :]
                        wide = wt[:, k, 0:groups * H].unsqueeze(2).to_broadcast([P, groups * H, HD])
                        if groups == NG:
                            then(dve.tensor_tensor(o3.rearrange("p (c s) d -> p c s d", s=2), o,
                                                   wide.rearrange("p (c s) d -> p c s d", s=2), ALU.mult))
                        else:
                            then(dve.tensor_tensor(o3, o, wide, ALU.mult))
                        if groups == 3:
                            then(dve.tensor_tensor(part[:, :, :], o3[:, 0:H, :], o3[:, H:2 * H, :], ALU.add))
                            then(dve.tensor_tensor(out, part[:, :, :], o3[:, 2 * H:3 * H, :], ALU.add))
                        else:
                            then(dve.tensor_tensor(out, o3[:, 0:H, :], o3[:, H:2 * H, :], ALU.add))

                    dve.wait_ge(oin[b], (i - b) * 16 + 32)
                    waits(dve, tp_ready, i - 1)
                    nat_a = nat[b][:, 0, :].rearrange("p (h d) -> p h d", h=H)
                    nat_b = nat[b][:, 1, :].rearrange("p (h d) -> p h d", h=H)
                    rec = oa[b][:, :, :, :]
                    join(0, NG, rec[:, :, :, 0:2 * HD].rearrange("p g c (s d) -> p (g c) s d", s=2),
                         [rec[:, g, :, 2 * HD:2 * HD + 2] for g in range(NG)],
                         [rec[:, g, :, 2 * HD + 2:REC] for g in range(NG)], nat_a)
                    if chunks == 2:
                        join(1, 2, ob[b][:, :, :, 0:HD].rearrange("p c h d -> p (c h) d"),
                             [ob[b][:, c, :, HD] for c in range(2)], [ob[b][:, c, :, HD + 1] for c in range(2)], nat_b)
                    else:
                        then(dve.reciprocal(sums[:, 1, :], ob[b][:, 0, :, HD]))
                        then(dve.tensor_tensor(nat_b, ob[b][:, 0, :, 0:HD],
                                               sums[:, 1, :].unsqueeze(2).to_broadcast([P, H, HD]), ALU.mult))
                    dve.sem_inc(nat_ready, 1)
                    assert count[0] == STEPS[chunks], count
                    if not isinstance(i, int) or i > 0:
                        gate(i - 1, 1 - b)

                def gate(i, b):
                    dve.wait_ge(tp_ready, i + 1)
                    dve.wait_ge(gz_in[b], (i - b) * 8 + 16)
                    waits(dve, stored[b], (i - b) * 8)
                    dve.tensor_tensor(uT[b][:, :, :], tp[b][:, :, :], gz[b][:, :, :], ALU.mult).then_inc(u_ready, 1)

                each_tile(dve, body)
                gate(NT - 1, 1)

            @block.tensor
            def _(pe):
                def body(i, b, chunks):
                    pe.wait_ge(nat_ready, i + 1)
                    waits(pe, u_ready, i - 1)
                    for c in range(8):
                        last = pe.transpose(tp[b][:, c, :], nat[b][:, c // 4, (c % 4) * P:(c % 4 + 1) * P], ident[:, :])
                    last.then_inc(tp_ready, 1)

                each_tile(pe, body)


def stage_project(nc, t, wraw):
    with ExitStack() as ctx:
        m = Mem(nc, ctx, "proj")
        NB = 5
        W = TOK // NB
        assert W * NB == TOK and W <= 512
        w = [m.sb(f"w_{h}", [P, 8, D], F32R) for h in ("hi", "lo")]
        ur = m.sb("ur", [P, 8, W])
        u = [m.sb(f"u_{h}", [P, 8, W], F32R) for h in ("hi", "lo")]
        gm = [m.sb(f"gm{b}", [P, 2, W]) for b in range(4)]
        ga = [m.sb(f"ga{b}", [P, 2, W]) for b in range(2)]
        mo = [m.sb(f"mo{b}", [P, W]) for b in range(2)]
        pr = m.ps("pr", [P, 4, 512])
        out_in = m.pool_sem("out_in")
        gm_in = [m.sem(f"gm_in{b}") for b in range(4)]
        stored = [m.pool_sem(f"stored{b}") for b in range(2)]
        w_hi, w_lo, u_in, u_hi, u_lo, pr_ready, gated, m_ready, sp_ticks = (
            m.sem(n) for n in ("w_hi", "w_lo", "u_in", "u_hi", "u_lo", "pr_ready", "gated", "m_ready", "sp_ticks"))

        def each_block(eng, body):
            body(0, slice(0, W))
            with eng.Fori(1, NB) as n:
                body(n, ds(n * W, W))

        with nc.Block() as block:
            @block.sync
            def _(sp):
                def load_u(n, at):
                    held(sp, u_lo, n * 8, sp_ticks)
                    sp.dma_start(ur[:, :, 0:W], t["uT"][:, :, at].rearrange("k p n -> p k n")).then_inc(u_in, 16)

                def load_gates(n, at, c):
                    held(sp, gated, n * 8 + c - 3, sp_ticks)
                    sp.dma_start(gm[c % 4][:, :, 0:W],
                                 t["gates"][8 + c:24:8, :, at].rearrange("k p n -> p k n")).then_inc(gm_in[c % 4], 16)

                load_u(0, slice(0, W))

                def body(n, at):
                    for c in range(8):
                        load_gates(n, at, c)
                        if c == 2 and not (isinstance(n, int) and n == NB - 1):
                            load_u(n + 1, ds(n * W + W, W))

                body(0, slice(0, W))
                with sp.Fori(1, NB - 1) as n:
                    body(n, ds(n * W, W))
                body(NB - 1, slice((NB - 1) * W, TOK))

            @block.gpsimd
            def _(pool):
                def body(n, at):
                    for c in range(8):
                        pool.wait_ge(gated, n * 8 + c + 1)
                        waits(pool, stored[c % 2], (n * 4 + c // 2) * 16)
                        pool.tensor_tensor(mo[c % 2][:, 0:W], ga[c % 2][:, 0, 0:W], ga[c % 2][:, 1, 0:W],
                                           ALU.add).then_inc(m_ready, 1)
                        pool.wait_ge(m_ready, n * 8 + c + 1)
                        pool.dma_start(t["mT"][c, :, at], mo[c % 2][:, 0:W]).then_inc(stored[c % 2], 16)

                body(0, slice(0, W))
                pool.wait_ge(w_lo, 8)
                share = KC // (NB - 1)
                with pool.Fori(1, NB) as n:
                    part = n - 1
                    pool.dma_start(wraw[:, ds(part * share, share), :],
                                   t["w_out"][ds(part * (share * P), share * P), :].rearrange("(c p) n -> p c n", p=P))\
                        .then_inc(out_in, 16)
                    body(n, ds(n * W, W))
                for b in range(2):
                    pool.wait_ge(stored[b], 16 * 4 * NB)
                pool.wait_ge(out_in, 16 * (NB - 1))

            @block.scalar
            def _(act):
                for c in range(8):
                    act.activation(w[0][:, c, :], wraw[:, c, :], ACT.Copy).then_inc(w_hi, 1)

                def body(n, at):
                    act.wait_ge(u_in, n * 16 + 16)
                    waits(act, pr_ready, n * 8)
                    for k in range(8):
                        act.activation(u[0][:, k, 0:W], ur[:, k, 0:W], ACT.Copy).then_inc(u_hi, 1)

                each_block(act, body)

            @block.vector
            def _(dve):
                for c in range(8):
                    dve.wait_ge(w_hi, c + 1)
                    dve.tensor_tensor(w[1][:, c, :], wraw[:, c, :], w[0][:, c, :].bitcast(F32), ALU.subtract)\
                        .then_inc(w_lo, 1)

                def body(n, at):
                    for k in range(8):
                        dve.wait_ge(u_hi, n * 8 + k + 1)
                        dve.tensor_tensor(u[1][:, k, 0:W], ur[:, k, 0:W], u[0][:, k, 0:W].bitcast(F32),
                                          ALU.subtract).then_inc(u_lo, 1)
                    for c in range(8):
                        b = c % 2
                        dve.wait_ge(pr_ready, n * 8 + c + 1)
                        dve.wait_ge(gm_in[c % 4], (n * 2 + c // 4 + 1) * 16)
                        waits(dve, m_ready, n * 8 + c - 1)
                        for k in range(2):
                            last = dve.tensor_tensor(ga[b][:, k, 0:W], pr[:, 2 * b + k, 0:W],
                                                     gm[c % 4][:, k, 0:W], ALU.mult)
                        last.then_inc(gated, 1)

                each_block(dve, body)

            @block.tensor
            def _(pe):
                def body(n, at):
                    for c in range(8):
                        waits(pe, gated, n * 8 + c - 1)
                        for k in range(2):
                            for j in range(4):
                                if c == 0:
                                    pe.wait_ge(u_lo, n * 8 + 4 * k + j + 1)
                                    if isinstance(n, int):
                                        pe.wait_ge(w_lo, 4 * k + j + 1)
                                last = split_matmul(pe, pr[:, 2 * (c % 2) + k, 0:W],
                                                    [w[h][:, 4 * k + j, c * P:(c + 1) * P] for h in range(2)],
                                                    [u[h][:, 4 * k + j, 0:W] for h in range(2)], j == 0, j == 3)
                        last.then_inc(pr_ready, 1)

                each_block(pe, body)


def stage_output(nc, t, copied, wraw):
    with ExitStack() as ctx:
        m = Mem(nc, ctx, "out")
        w = [m.sb(f"w_{h}", [P, KC, D], F32R) for h in ("hi", "lo")]
        mr = [m.sb(f"mr{b}", [P, KC, P]) for b in range(2)]
        mm = [[m.sb(f"m{b}_{h}", [P, KC, P], F32R) for h in ("hi", "lo")] for b in range(2)]
        x = [m.sb(f"x{b}", [P, D]) for b in range(2)]
        y = [m.sb(f"y{b}", [P, D]) for b in range(2)]
        yn = [m.sb(f"yn{b}", [P, D]) for b in range(2)]
        junk = m.sb("junk", [P, D])
        g = m.sb("g_rows", [P, D])
        stat = [m.sb(f"stat{b}", [P, 3]) for b in range(2)]
        eps = m.sb("eps", [P, 1])
        py = [m.ps(f"py{b}", [P, D]) for b in range(2)]
        m_in = [m.sem(f"m_in{b}") for b in range(2)]
        x_in = [m.sem(f"x_in{b}") for b in range(2)]
        stored = [m.pool_sem(f"stored{b}") for b in range(2)]
        g_in, eps_set, w_hi, w_lo, m_hi, m_lo, ready, squared, rooted, inverted, normed, y_ready, rows_stored, sp_ticks = (
            m.sem(n) for n in ("g_in", "eps_set", "w_hi", "w_lo", "m_hi", "m_lo", "ready", "squared", "rooted",
                               "inverted", "normed", "y_ready", "rows_stored", "sp_ticks"))

        def each_tile(eng, body):
            for n in range(2):
                body(n, n, P, ds(n * P, P))
            with eng.Fori(1, NT // 2 - 1) as i:
                for b in range(2):
                    body(i * 2 + b, b, P, ds((i * 2 + b) * P, P))
            for n in range(NT - 2, NT):
                body(n, n % 2, P, ds(n * P, P))
            body(NT, 0, NS, slice(SEQ, TOK))

        with nc.Block() as block:
            @block.sync
            def _(sp):
                sp.dma_start(g[:, :], t["g_post"].partition_broadcast(P)).then_inc(g_in, 16)
                def body(n, b, rows, at):
                    held(sp, m_lo, n - 1, sp_ticks)
                    sp.dma_start(mr[b][:, :, 0:rows], t["mT"][:, :, at].rearrange("k p n -> p k n")).then_inc(m_in[b], 16)
                    held(sp, y_ready, n - 1, sp_ticks)
                    src = t["x_sample"] if rows == NS else t["x_prompt"][at, :]
                    sp.dma_start(x[b][0:rows, :], src).then_inc(x_in[b], 16)

                each_tile(sp, body)
                for gi, (win, _) in enumerate(GROUPS):
                    for which in (1, 2):
                        sp.dma_start(t[f"win{gi}_sample"][:, win - DT:win, which - 1, :],
                                     t["hs"][:, which * QKV + gi * AW:which * QKV + (gi + 1) * AW]
                                     .rearrange("(b k) n -> b k n", b=DB)).then_inc(rows_stored, 16)
                sp.wait_ge(rows_stored, 16 * 6)
                sp.wait_ge(copied, COPIES * 16)

            @block.gpsimd
            def _(pool):
                def body(n, b, rows, at):
                    pool.wait_ge(y_ready, n + 1)
                    dst = t["y_sample"] if rows == NS else t["y_prompt"][at, :]
                    pool.dma_start(dst, y[b][0:rows, :]).then_inc(stored[b], 16)

                each_tile(pool, body)
                pool.wait_ge(stored[0], 16 * 9)
                pool.wait_ge(stored[1], 16 * 8)

            @block.scalar
            def _(act):
                def high(n, b, rows):
                    act.wait_ge(m_in[b], (n - b) * 8 + 16)
                    waits(act, ready, n - 1)
                    act.activation(mm[b][0][:, :, 0:rows], mr[b][:, :, 0:rows], ACT.Copy).then_inc(m_hi, 1)

                for c in range(KC):
                    act.activation(w[0][:, c, :], wraw[:, c, :], ACT.Copy).then_inc(w_hi, 1)
                    if c == 0:
                        high(0, 0, P)
                act.wait_ge(eps_set, 1)

                def body(n, b, rows, at):
                    if rows == P:
                        high(n + 1, 1 - b, NS if isinstance(n, int) and n == NT - 1 else P)
                    r = slice(0, rows)
                    act.wait_ge(ready, n + 1)
                    waits(act, inverted, n - 1)
                    waits(act, squared, n)
                    act.activation(junk[r, :], py[b][r, :], ACT.Square, accum_out=stat[b][r, 0:1]).then_inc(squared, 1)
                    act.wait_ge(squared, n + 1)
                    act.activation(stat[b][r, 1:2], stat[b][r, 0:1], ACT.Sqrt, bias=eps[r, :], scale=1.0 / D)\
                        .then_inc(rooted, 1)

                each_tile(act, body)

            @block.vector
            def _(dve):
                dve.memset(eps[:, :], EPS).then_inc(eps_set, 1)

                def low(n, b, rows):
                    dve.wait_ge(m_hi, n + 1)
                    dve.tensor_tensor(mm[b][1][:, :, 0:rows], mr[b][:, :, 0:rows],
                                      mm[b][0][:, :, 0:rows].bitcast(F32), ALU.subtract).then_inc(m_lo, 1)

                for c in range(KC):
                    dve.wait_ge(w_hi, c + 1)
                    dve.tensor_tensor(w[1][:, c, :], wraw[:, c, :], w[0][:, c, :].bitcast(F32), ALU.subtract)\
                        .then_inc(w_lo, 1)
                    if c == 0:
                        low(0, 0, P)
                dve.wait_ge(g_in, 16)

                def body(n, b, rows, at):
                    r = slice(0, rows)
                    if rows == P:
                        low(n + 1, 1 - b, NS if isinstance(n, int) and n == NT - 1 else P)
                    dve.wait_ge(rooted, n + 1)
                    dve.reciprocal(stat[b][r, 2:3], stat[b][r, 1:2]).then_inc(inverted, 1)
                    dve.wait_ge(inverted, n + 1)
                    dve.scalar_tensor_tensor(yn[b][r, :], py[b][r, :], stat[b][r, 2:3], g[r, :], ALU.mult, ALU.mult)\
                        .then_inc(normed, 1)
                    dve.wait_ge(normed, n + 1)
                    dve.wait_ge(x_in[b], (n - b) * 8 + 16)
                    waits(dve, stored[b], (n - b) * 8)
                    dve.tensor_tensor(y[b][r, :], yn[b][r, :], x[b][r, :], ALU.add).then_inc(y_ready, 1)

                each_tile(dve, body)

            @block.tensor
            def _(pe):
                def body(n, b, rows, at):
                    pe.wait_ge(m_lo, n + 1)
                    waits(pe, normed, n - 1)
                    for half in range(2):
                        cols = slice(half * 512, (half + 1) * 512)
                        for c in range(KC):
                            if isinstance(n, int) and n == 0:
                                pe.wait_ge(w_lo, c + 1)
                            last = split_matmul(pe, py[b][0:rows, cols], [mm[b][h][:, c, 0:rows] for h in range(2)],
                                                [w[h][:, c, cols] for h in range(2)], c == 0, c == KC - 1)
                    last.then_inc(ready, 1)

                each_tile(pe, body)


def hybrid_step(nc, t):
    t["cqT"] = nc.dram_tensor("scr_cqT", [QL // P, P, TOK], F32).ap()
    t["ckvT"] = nc.dram_tensor("scr_ckvT", [P, TOK], F32).ap()
    t["kpeT"] = nc.dram_tensor("scr_kpeT", [ROPE, TOK], F32).ap()
    t["hs"] = nc.dram_tensor("scr_hs", [NS, 3 * QKV], F32).ap()
    t["oa"] = nc.dram_tensor("scr_oa", [SEQ, NG, 4, REC], F32).ap()
    t["gates"] = nc.dram_tensor("scr_gates", [24, P, TOK], F32).ap()
    t["qs96"] = nc.dram_tensor("scr_qs96", [H, NOPE + ROPE, NS], F32).ap()
    t["ob"] = nc.dram_tensor("scr_ob", [SEQ, 2, H, RECB], F32).ap()
    t["oaT_s"] = nc.dram_tensor("scr_oaT_s", [4, P, NS], F32).ap()
    t["obT_s"] = nc.dram_tensor("scr_obT_s", [4, P, NS], F32).ap()
    t["uT"] = nc.dram_tensor("scr_uT", [8, P, TOK], F32).ap()
    t["mT"] = nc.dram_tensor("scr_mT", [KC, P, TOK], F32).ap()
    with ExitStack() as whole:
        Mem.whole = whole
        run_stages(nc, t, whole.enter_context(nc.semaphore("windows_copied")))


def run_stages(nc, t, copied):
    Mem.spent.clear()
    with ExitStack() as ctx:
        m = Mem(nc, ctx, "all")
        ident = m.sb("ident", [P, P])
        xs = [m.sb(f"xs_{h}", [P, KC, NS], F32R) for h in ("hi", "lo")]
        xT = [m.sb(f"xT_{h}", [P, KC, SEQ], F32R) for h in ("hi", "lo")]
        stage_norm(nc, t, xT, xs, ident)
        stage_latents(nc, t, xT, xs, ident)
        stage_dilated(nc, t, xT, xs, ident, copied)
        stage_gates(nc, t, xT, xs)
    with ExitStack() as ctx:
        m = Mem(nc, ctx, "late")
        ident = m.sb("ident", [P, P])
        with nc.Block() as block, nc.semaphore("late_ident_in") as ident_in:
            @block.sync
            def _(sp):
                sp.dma_start(ident[:, :], t["ident"]).then_inc(ident_in, 16)
                sp.wait_ge(ident_in, 16)
        stage_latent_attn(nc, t, ident)
        clear_semaphores(nc)
        stage_sample_dilated(nc, t, ident)
        stage_sample_latent(nc, t, ident)
        wraw = m.sb("wraw", [P, KC, D])
        stage_join(nc, t, ident, wraw)
        stage_project(nc, t, wraw)
        stage_output(nc, t, copied, wraw)


def _constants():
    import numpy as np

    f = np.float32
    n = NG * H
    slopes = np.exp2(f(-8.0) * np.arange(1, n + 1, dtype=f) / f(n)).astype(f).reshape(NG, H)
    a = np.arange(P)[:, None]
    c = np.arange(2 * P)[None, :]
    delta = a + P - c
    valid = (delta >= 0) & (delta <= P)
    bias = np.empty((NG, H, P, 2 * P), f)
    for g, (_, dil) in enumerate(GROUPS):
        for h in range(H):
            bias[g, h] = np.where(valid, -slopes[g, h] * (dil * delta).astype(f), f(NEG))
    causal = np.where(np.arange(P)[None, :] <= a, f(0), f(NEG)).astype(f)
    inv = f(10000.0) ** (-np.arange(0, ROPE, 2, dtype=f) / f(ROPE))
    pos = np.concatenate([np.arange(SEQ), np.tile(PAST + np.arange(DT), DB)]).astype(f)
    ang = (pos[:, None] * inv[None, :]).astype(f)
    cos, sin = np.cos(ang).astype(f), np.sin(ang).astype(f)
    rows = np.stack([np.concatenate([cos, cos], 1), np.concatenate([-sin, sin], 1)], 1)
    cols = np.concatenate([rows[:, 0].T, rows[:, 1].T], 0)
    dist = np.stack([dil * (P - np.arange(P)) for _, dil in GROUPS]).astype(f)
    sample_alibi = np.stack([-slopes[:, h, None] * dist for h in range(H)] * DT)
    sample_causal = np.where(np.arange(DT)[:, None] <= np.tile(np.arange(DT), H)[None, :], f(0), f(NEG))
    return {
        "ident": np.eye(P, dtype=f),
        "alibi": np.ascontiguousarray(bias.transpose(0, 2, 1, 3)),
        "causal": causal,
        "rope_rows": np.ascontiguousarray(rows),
        "rope_cols": np.ascontiguousarray(cols),
        "sample_alibi": sample_alibi.astype(f),
        "sample_causal": sample_causal.astype(f),
    }


_CONSTS = ["ident", "alibi", "causal", "rope_rows", "rope_cols", "sample_alibi", "sample_causal"]
_INS = ["x_prompt", "x_sample", "cache_ckv", "cache_kpe", "state_win0", "state_win1", "state_win2", "page_table",
        "w_in", "w_uq", "w_uk", "w_uv", "w_proj_a", "w_proj_b", "w_out", "g_pre", "g_post", "g_q", "g_kv"]
_FLAT = {
    "x_prompt": "a s d -> (a s) d", "x_sample": "b t d -> (b t) d", "cache_ckv": "a n s c -> (a n) s c",
    "cache_kpe": "a n s c -> (a n) s c", "state_win0": "a b w c h d -> (a b) w c (h d)",
    "state_win1": "a b w c h d -> (a b) w c (h d)", "state_win2": "a b w c h d -> (a b) w c (h d)",
    "w_in": "a k n -> (a k) n", "w_uq": "a k n -> (a k) n", "w_uk": "a c h d -> (a c) h d",
    "w_uv": "a c h d -> (a c) h d", "w_proj_a": "a k n -> (a k) n", "w_proj_b": "a k n -> (a k) n",
    "w_out": "a k n -> (a k) n", "g_pre": "a n -> (a n)", "g_post": "a n -> (a n)", "g_q": "a n -> (a n)",
    "g_kv": "a n -> (a n)",
}
_WIN = "a b w c h d -> (a b) w c (h d)"
_OUTS = [
    ("y_prompt", (1, SEQ, D), "a s d -> (a s) d"), ("y_sample", (DB, DT, D), "b t d -> (b t) d"),
    ("ckv_prompt", (1, 1, SEQ, KL), "a b s c -> (a b s) c"), ("kpe_prompt", (1, 1, SEQ, ROPE), "a b s c -> (a b s) c"),
    ("win0_prompt", (1, 1, 128, 2, H, HD), _WIN), ("win1_prompt", (1, 1, 512, 2, H, HD), _WIN),
    ("win2_prompt", (1, 1, 2048, 2, H, HD), _WIN),
    ("ckv_sample", (1, DB, DT, KL), "a b t c -> (a b t) c"), ("kpe_sample", (1, DB, DT, ROPE), "a b t c -> (a b t) c"),
    ("win0_sample", (1, DB, 128, 2, H, HD), _WIN), ("win1_sample", (1, DB, 512, 2, H, HD), _WIN),
    ("win2_sample", (1, DB, 2048, 2, H, HD), _WIN),
]


def kernel(**inputs):
    import numpy as _np
    import concourse.bacc as _bacc
    from concourse import mybir as _mybir
    from concourse.bass_utils import run_bass_kernel_spmd as _run

    nc = _bacc.Bacc("TRN2", target_bir_lowering=False, num_devices=1)
    arrays, t = {}, {}
    consts = _constants()
    for name in _INS + _CONSTS:
        a = _np.ascontiguousarray(inputs[name] if name in inputs else consts[name])
        arrays[f"in_{name}"] = a
        ap = nc.dram_tensor(f"in_{name}", a.shape, _mybir.dt.from_np(a.dtype), kind="ExternalInput").ap()
        t[name] = ap.rearrange(_FLAT[name]) if name in _FLAT else ap
    for name, shape, flat in _OUTS:
        ap = nc.dram_tensor(f"out_{name}", shape, _mybir.dt.float32, kind="ExternalOutput").ap()
        t[name] = ap.rearrange(flat)
    hybrid_step(nc, t)
    r = _run(nc, [arrays], core_ids=[0])
    return tuple(r.results[0][f"out_{name}"] for name, _, _ in _OUTS)
```
